# Optimizing a Trainium2 kernel written in Bass

```python
import math
import jax, jax.numpy as jnp
from jax import lax
import numpy as np

D_MODEL = 2048
BATCH = 1
SEQ = 256
DEPTH = 1
DEC_BATCH = 8
DEC_SEQ = 1
PAST_LEN = 2048
PAGE_SIZE = 128

F32 = jnp.float32
HEAD_DIM = 128
RET_HEADS = D_MODEL // (2 * HEAD_DIM)
NSA_HEADS = D_MODEL // (2 * HEAD_DIM)
NSA_KV_HEADS = 2
RET_W = RET_HEADS * HEAD_DIM
NSA_W = NSA_HEADS * HEAD_DIM
KV_W = NSA_KV_HEADS * HEAD_DIM
MIX_W = RET_W + NSA_W
RET_CHUNK = 128
RET_ROPE_THETA = 10000.0
ROPE_THETA = 500000.0
ROT_DIM = HEAD_DIM // 4
CMP_BLOCK = 64
SEL_TOPK = 16
WINDOW = 512
WIN_Q_BLOCK = 128
SEL_Q_BLOCK = 64
N_GROUPS = 4
EXPERTS_PER_GROUP = 8
N_EXPERTS = N_GROUPS * EXPERTS_PER_GROUP
EXPERT_TOPK = 2
D_EXPERT = 512
MOE_BLOCK = 128
LN_EPS = 1e-5
GN_EPS = 1e-5
NEG = -1e30
DEEPNORM_ALPHA = (2 * DEPTH) ** 0.25
DEEPNORM_BETA = (8 * DEPTH) ** -0.25
SPLITS = (RET_W, RET_W, RET_W, RET_W, NSA_W, KV_W, KV_W, KV_W, KV_W, KV_W, KV_W, NSA_HEADS * 3)
IN_W = sum(SPLITS)

kernel_name = 'retnet_nsa_hymba_hmoe_deepnorm_step'

def _layer_norm(x, g, b):
    xf = x.astype(F32)
    mu = xf.mean(-1, keepdims=True)
    var = jnp.square(xf - mu).mean(-1, keepdims=True)
    return ((xf - mu) * lax.rsqrt(var + LN_EPS) * g + b).astype(x.dtype)

def _rope(x, pos, rot_dim, theta):
    half = rot_dim // 2
    inv = theta ** (-jnp.arange(0, rot_dim, 2, dtype=F32) / rot_dim)
    ang = pos[..., None].astype(F32) * inv
    cos = jnp.cos(ang)[:, :, None, :]
    sin = jnp.sin(ang)[:, :, None, :]
    xr = x[..., :rot_dim].astype(F32)
    x1, x2 = xr[..., :half], xr[..., half:]
    rot = jnp.concatenate([x1 * cos - x2 * sin, x2 * cos + x1 * sin], -1).astype(x.dtype)
    return jnp.concatenate([rot, x[..., rot_dim:]], -1)

def _heads(t, n):
    return t.reshape(t.shape[0], t.shape[1], n, HEAD_DIM)

def _project(x, w_in):
    p = jnp.einsum('bld,de->ble', x, w_in)
    cuts = [int(c) for c in np.cumsum(SPLITS)[:-1]]
    return jnp.split(p, cuts, axis=-1)

def _chunk_retention(q, k, v, s0):
    n, l, h, d = q.shape
    c = RET_CHUNK if l % RET_CHUNK == 0 else l
    nc = l // c
    log_g = jnp.log1p(-jnp.exp2(-5.0 - jnp.arange(h, dtype=F32)))
    i = jnp.arange(c, dtype=F32)
    rel = i[:, None] - i[None, :]
    dmask = jnp.where(rel[None] >= 0, jnp.exp(jnp.maximum(rel[None], 0.0) * log_g[:, None, None]), 0.0)
    q_dec = jnp.exp((i + 1.0)[None] * log_g[:, None])[..., None]
    k_dec = jnp.exp((c - 1.0 - i)[None] * log_g[:, None])[..., None]
    c_dec = jnp.exp(c * log_g)[:, None, None]

    def to_chunks(t):
        return t.astype(F32).reshape(n, nc, c, h, d).transpose(1, 0, 3, 2, 4)

    def step(s, qkv):
        qc, kc, vc = qkv
        att = jnp.einsum('bhid,bhjd->bhij', qc, kc) * dmask
        o = jnp.einsum('bhij,bhjd->bhid', att, vc) + jnp.einsum('bhid,bhde->bhie', qc * q_dec, s)
        s = c_dec * s + jnp.einsum('bhjd,bhje->bhde', kc * k_dec, vc)
        return s, o

    s, o = lax.scan(step, s0.astype(F32), (to_chunks(q), to_chunks(k), to_chunks(v)))
    return o.transpose(1, 0, 3, 2, 4).reshape(n, l, h, d), s

def _retention_group(rq, rk, rv, rg, pos, s0, gn_g):
    q = _rope(_heads(rq, RET_HEADS), pos, HEAD_DIM, RET_ROPE_THETA)
    k = _rope(_heads(rk, RET_HEADS), pos, HEAD_DIM, RET_ROPE_THETA) * (HEAD_DIM ** -0.5)
    v = _heads(rv, RET_HEADS)
    o, s = _chunk_retention(q, k, v, s0)
    mu = o.mean(-1, keepdims=True)
    var = jnp.square(o - mu).mean(-1, keepdims=True)
    on = (o - mu) * lax.rsqrt(var + GN_EPS) * gn_g.reshape(RET_HEADS, HEAD_DIM).astype(F32)
    out = jax.nn.silu(rg.astype(F32)) * on.reshape(rg.shape)
    return out.astype(rq.dtype), s

def _gqa_attend(q, k, v, mask):
    n, lq, h, d = q.shape
    kv = k.shape[2]
    qg = q.reshape(n, lq, kv, h // kv, d)
    s = jnp.einsum('nqkgd,nskd->nkgqs', qg, k).astype(F32) * (d ** -0.5)
    m = mask[:, None, None]
    p = jax.nn.softmax(jnp.where(m, s, NEG), axis=-1) * m
    o = jnp.einsum('nkgqs,nskd->nqkgd', p.astype(v.dtype), v)
    return o.reshape(n, lq, h, d), p

def _nsa_heads(nq, ck, sk, wk, cv, sv, wv, pos):
    rp = lambda t, nh: _rope(_heads(t, nh), pos, ROT_DIM, ROPE_THETA)
    return (rp(nq, NSA_HEADS), rp(ck, NSA_KV_HEADS), rp(sk, NSA_KV_HEADS), rp(wk, NSA_KV_HEADS),
            _heads(cv, NSA_KV_HEADS), _heads(sv, NSA_KV_HEADS), _heads(wv, NSA_KV_HEADS))

def _compress(rows, w):
    n, t, kv, d = rows.shape
    return jnp.einsum('nbjkd,jd->nbkd', rows.reshape(n, t // CMP_BLOCK, CMP_BLOCK, kv, d), w)

def _cmp_branch(q, pos, kc, vc):
    nb = kc.shape[1]
    blk_end = (jnp.arange(nb) + 1) * CMP_BLOCK - 1
    mask = blk_end[None, None, :] <= pos[:, :, None]
    o, p = _gqa_attend(q, kc, vc, mask)
    imp = p.sum(axis=2).transpose(0, 2, 1, 3)
    return o, imp

def _select_blocks(imp, pos, n_sel):
    nb = imp.shape[-1]
    imp = jnp.pad(imp, ((0, 0), (0, 0), (0, 0), (0, n_sel - nb)))
    blk = jnp.arange(n_sel)
    cur = (pos // CMP_BLOCK)[:, :, None, None]
    forced = (blk == 0) | (blk == cur) | (blk == cur - 1)
    score = jnp.where(blk > cur, NEG, jnp.where(forced, -NEG, imp))
    top, idx = lax.top_k(score, min(SEL_TOPK, n_sel))
    return idx, top > 0.5 * NEG

def _sel_attend(q, pos, ks, vs, idx, valid):
    n, lq, kv, kk, cb, d = ks.shape
    h = q.shape[2]
    kpos = idx[..., None] * CMP_BLOCK + jnp.arange(CMP_BLOCK)
    m = ((kpos <= pos[:, :, None, None, None]) & valid[..., None]).reshape(n, lq, kv, 1, kk * cb)
    qg = q.reshape(n, lq, kv, h // kv, d)
    kf = ks.reshape(n, lq, kv, kk * cb, d)
    vf = vs.reshape(n, lq, kv, kk * cb, d)
    s = jnp.einsum('nqkgd,nqkjd->nqkgj', qg, kf).astype(F32) * (d ** -0.5)
    p = jax.nn.softmax(jnp.where(m, s, NEG), axis=-1) * m
    o = jnp.einsum('nqkgj,nqkjd->nqkgd', p.astype(vf.dtype), vf)
    return o.reshape(n, lq, h, d)

def _sel_prompt(q, pos, k, v, idx, valid):
    b, s, h, d = q.shape
    kv = k.shape[2]
    nb = s // CMP_BLOCK
    nq = s // SEL_Q_BLOCK
    kb = k.reshape(b, nb, CMP_BLOCK, kv, d).transpose(0, 3, 1, 2, 4)
    vb = v.reshape(b, nb, CMP_BLOCK, kv, d).transpose(0, 3, 1, 2, 4)
    bi = jnp.arange(b)[:, None, None, None]
    hi = jnp.arange(kv)[None, None, :, None]

    def blockwise(t):
        return t.reshape(t.shape[0], nq, SEL_Q_BLOCK, *t.shape[2:]).swapaxes(0, 1)

    def one(args):
        qc, pc, ic, vc = args
        return _sel_attend(qc, pc, kb[bi, hi, ic], vb[bi, hi, ic], ic, vc)

    o = lax.map(one, (blockwise(q), blockwise(pos), blockwise(idx), blockwise(valid)))
    return o.swapaxes(0, 1).reshape(b, s, h, d)

def _win_prompt(q, k, v):
    b, s, h, d = q.shape
    kv = k.shape[2]
    nb = s // WIN_Q_BLOCK
    nprev = WINDOW // WIN_Q_BLOCK
    nw = nprev + 1
    padw = ((0, 0), (WINDOW, 0), (0, 0), (0, 0))
    kp = jnp.pad(k, padw).reshape(b, nb + nprev, WIN_Q_BLOCK, kv, d)
    vp = jnp.pad(v, padw).reshape(b, nb + nprev, WIN_Q_BLOCK, kv, d)
    kw = jnp.concatenate([kp[:, i:i + nb] for i in range(nw)], axis=2)
    vw = jnp.concatenate([vp[:, i:i + nb] for i in range(nw)], axis=2)
    qpos = jnp.arange(s).reshape(nb, WIN_Q_BLOCK)
    kpos = (jnp.arange(nb)[:, None] - nprev) * WIN_Q_BLOCK + jnp.arange(nw * WIN_Q_BLOCK)[None]
    qq, kk = qpos[:, :, None], kpos[:, None, :]
    mask = (kk <= qq) & (qq - kk < WINDOW) & (kk >= 0)
    mask = jnp.broadcast_to(mask[None], (b,) + mask.shape).reshape(b * nb, WIN_Q_BLOCK, nw * WIN_Q_BLOCK)
    o, _ = _gqa_attend(q.reshape(b * nb, WIN_Q_BLOCK, h, d), kw.reshape(b * nb, nw * WIN_Q_BLOCK, kv, d),
                       vw.reshape(b * nb, nw * WIN_Q_BLOCK, kv, d), mask)
    return o.reshape(b, s, h, d)

def _gather_selected(pool, new_rows, page_table, idx):
    n, l, kv, d = new_rows.shape
    n_pages = page_table.shape[1]
    past_blocks = n_pages * PAGE_SIZE // CMP_BLOCK
    nbn = -(-l // CMP_BLOCK)
    newb = jnp.pad(new_rows, ((0, 0), (0, nbn * CMP_BLOCK - l), (0, 0), (0, 0)))
    newb = newb.reshape(n, nbn, CMP_BLOCK, kv, d).transpose(0, 3, 1, 2, 4)
    bi = jnp.arange(n)[:, None, None, None]
    hi = jnp.arange(kv)[None, None, :, None]
    start = idx * CMP_BLOCK
    phys = page_table[bi, jnp.minimum(start // PAGE_SIZE, n_pages - 1)]
    off = (start % PAGE_SIZE)[..., None] + jnp.arange(CMP_BLOCK)
    past = pool[phys[..., None], off, hi[..., None]]
    new = newb[bi, hi, jnp.clip(idx - past_blocks, 0, nbn - 1)]
    return jnp.where((idx < past_blocks)[..., None, None], past, new)

def _nsa_combine(gl, o_cmp, o_sel, o_win):
    n, l = gl.shape[0], gl.shape[1]
    g = jax.nn.sigmoid(gl.astype(F32)).reshape(n, l, NSA_HEADS, 3, 1)
    o = g[..., 0, :] * o_cmp + g[..., 1, :] * o_sel + g[..., 2, :] * o_win
    return o.reshape(n, l, NSA_W).astype(o_cmp.dtype)

def _prompt_mixer(x, win_buf, w_in, w_cmp_k, w_cmp_v, gn_g):
    n, s, _ = x.shape
    pos = jnp.arange(s)[None]
    rq, rk, rv, rg, nq, ck, cv, sk, sv, wk, wv, gl = _project(x, w_in)
    s0 = jnp.zeros((n, RET_HEADS, HEAD_DIM, HEAD_DIM), F32)
    ret_out, s_fin = _retention_group(rq, rk, rv, rg, pos, s0, gn_g)
    q, ck, sk, wk, cv, sv, wv = _nsa_heads(nq, ck, sk, wk, cv, sv, wv, pos)
    o_cmp, imp = _cmp_branch(q, pos, _compress(ck, w_cmp_k), _compress(cv, w_cmp_v))
    idx, valid = _select_blocks(imp, pos, s // CMP_BLOCK)
    o_sel = _sel_prompt(q, pos, sk, sv, idx, valid)
    o_win = _win_prompt(q, wk, wv)
    feats = jnp.concatenate([ret_out, _nsa_combine(gl, o_cmp, o_sel, o_win)], -1)
    if s >= win_buf:
        bk, bv = wk[:, s - win_buf:], wv[:, s - win_buf:]
    else:
        padb = ((0, 0), (win_buf - s, 0), (0, 0), (0, 0))
        bk, bv = jnp.pad(wk, padb), jnp.pad(wv, padb)
    return feats, (ck, cv, sk, sv, bk, bv, s_fin)

def _sample_mixer(x, c_cmp_k, c_cmp_v, c_sel_k, c_sel_v, c_win_k, c_win_v, s_ret, page_table,
                  w_in, w_cmp_k, w_cmp_v, gn_g):
    n, l, _ = x.shape
    past = page_table.shape[1] * PAGE_SIZE
    pos = past + jnp.arange(l)[None]
    rq, rk, rv, rg, nq, ck, cv, sk, sv, wk, wv, gl = _project(x, w_in)
    ret_out, s_new = _retention_group(rq, rk, rv, rg, pos, s_ret, gn_g)
    q, ck, sk, wk, cv, sv, wv = _nsa_heads(nq, ck, sk, wk, cv, sv, wv, pos)
    rows = (n, past, NSA_KV_HEADS, HEAD_DIM)
    ck_all = jnp.concatenate([c_cmp_k[page_table].reshape(rows), ck], 1)
    cv_all = jnp.concatenate([c_cmp_v[page_table].reshape(rows), cv], 1)
    t = past + l
    ncb = t // CMP_BLOCK
    kc = _compress(ck_all[:, :ncb * CMP_BLOCK], w_cmp_k)
    vc = _compress(cv_all[:, :ncb * CMP_BLOCK], w_cmp_v)
    o_cmp, imp = _cmp_branch(q, pos, kc, vc)
    idx, valid = _select_blocks(imp, pos, -(-t // CMP_BLOCK))
    ks = _gather_selected(c_sel_k, sk, page_table, idx)
    vs = _gather_selected(c_sel_v, sv, page_table, idx)
    o_sel = _sel_attend(q, pos, ks, vs, idx, valid)
    wb = c_win_k.shape[1]
    kw = jnp.concatenate([c_win_k, wk], 1)
    vw = jnp.concatenate([c_win_v, wv], 1)
    kpos = past - wb + jnp.arange(wb + l)
    mask = (kpos[None, None, :] <= pos[:, :, None]) & (pos[:, :, None] - kpos[None, None, :] < WINDOW)
    o_win, _ = _gqa_attend(q, kw, vw, mask)
    feats = jnp.concatenate([ret_out, _nsa_combine(gl, o_cmp, o_sel, o_win)], -1)
    return feats, (ck, cv, sk, sv, kw[:, l:], vw[:, l:], s_new)

def _hmoe(x, w_group, b_group, w_expert, b_expert, w_gate, w_up, w_down):
    shp = x.shape
    d = shp[-1]
    xt = x.reshape(-1, d)
    t = xt.shape[0]
    g_logit = (xt @ w_group + b_group).astype(F32)
    grp = jnp.argmax(g_logit, -1)
    p_grp = jnp.take_along_axis(jax.nn.softmax(g_logit, -1), grp[:, None], 1)
    e_logit = (xt @ w_expert + b_expert).astype(F32).reshape(t, N_GROUPS, EXPERTS_PER_GROUP)
    e_logit = jnp.take_along_axis(e_logit, grp[:, None, None], 1)[:, 0]
    p_top, i_top = lax.top_k(jax.nn.softmax(e_logit, -1), EXPERT_TOPK)
    gate = p_grp * p_top / p_top.sum(-1, keepdims=True)
    eid = (grp[:, None] * EXPERTS_PER_GROUP + i_top).reshape(-1)
    a = eid.shape[0]
    order = jnp.argsort(eid)
    e_sorted = eid[order]
    tok = order // EXPERT_TOPK
    counts = jnp.bincount(eid, length=N_EXPERTS)
    starts = jnp.cumsum(counts) - counts
    padded = (counts + MOE_BLOCK - 1) // MOE_BLOCK * MOE_BLOCK
    pad_end = jnp.cumsum(padded)
    pad_start = pad_end - padded
    dest = pad_start[e_sorted] + jnp.arange(a) - starts[e_sorted]
    n_blk = -(-(a + N_EXPERTS * (MOE_BLOCK - 1)) // MOE_BLOCK)
    buf = jnp.zeros((n_blk * MOE_BLOCK, d), xt.dtype).at[dest].set(xt[tok])
    blk_e = jnp.minimum(jnp.searchsorted(pad_end, jnp.arange(n_blk) * MOE_BLOCK, side='right'), N_EXPERTS - 1)

    def expert_block(args):
        xb, e = args
        hb = jax.nn.silu(xb @ w_gate[e]) * (xb @ w_up[e])
        return hb @ w_down[e]

    yb = lax.map(expert_block, (buf.reshape(n_blk, MOE_BLOCK, d), blk_e))
    y = yb.reshape(-1, d)[dest] * gate.reshape(-1)[order][:, None].astype(xt.dtype)
    return jnp.zeros_like(xt).at[tok].add(y).reshape(shp)

def _post_block(x, feats, w_o, ln1_g, ln1_b, moe, ln2_g, ln2_b):
    h = _layer_norm(DEEPNORM_ALPHA * x + feats @ w_o, ln1_g, ln1_b)
    return _layer_norm(DEEPNORM_ALPHA * h + _hmoe(h, *moe), ln2_g, ln2_b)

def setup_inputs(seed: int = 0) -> dict:
    key = jax.random.key(seed)
    ks = jax.random.split(key, 32)
    n_pages = PAST_LEN // PAGE_SIZE
    used = DEC_BATCH * n_pages
    n_pool = used + max(1, used // 4)
    win_buf = min(WINDOW, PAST_LEN)
    nrm = lambda k, shape, scale: scale * jax.random.normal(k, shape, F32)
    pool = (DEPTH, n_pool, PAGE_SIZE, NSA_KV_HEADS, HEAD_DIM)
    wbuf = (DEPTH, DEC_BATCH, win_buf, NSA_KV_HEADS, HEAD_DIM)
    page_table = jax.random.permutation(ks[9], n_pool)[:used].reshape(DEC_BATCH, n_pages).astype(jnp.int32)
    return {
        'x_prompt': nrm(ks[0], (BATCH, SEQ, D_MODEL), 1.0),
        'x_sample': nrm(ks[1], (DEC_BATCH, DEC_SEQ, D_MODEL), 1.0),
        'cache_cmp_k': nrm(ks[2], pool, 1.0),
        'cache_cmp_v': nrm(ks[3], pool, 1.0),
        'cache_sel_k': nrm(ks[4], pool, 1.0),
        'cache_sel_v': nrm(ks[5], pool, 1.0),
        'cache_win_k': nrm(ks[6], wbuf, 1.0),
        'cache_win_v': nrm(ks[7], wbuf, 1.0),
        'state_ret': nrm(ks[8], (DEPTH, DEC_BATCH, RET_HEADS, HEAD_DIM, HEAD_DIM), 0.1),
        'page_table': page_table,
        'w_in': nrm(ks[10], (DEPTH, D_MODEL, IN_W), D_MODEL ** -0.5),
        'w_cmp_k': (1.0 + nrm(ks[11], (DEPTH, CMP_BLOCK, HEAD_DIM), 0.1)) / CMP_BLOCK,
        'w_cmp_v': (1.0 + nrm(ks[12], (DEPTH, CMP_BLOCK, HEAD_DIM), 0.1)) / CMP_BLOCK,
        'ret_gn_g': 1.0 + nrm(ks[13], (DEPTH, RET_W), 0.02),
        'w_o': nrm(ks[14], (DEPTH, MIX_W, D_MODEL), DEEPNORM_BETA * MIX_W ** -0.5),
        'ln1_g': 1.0 + nrm(ks[15], (DEPTH, D_MODEL), 0.02),
        'ln1_b': nrm(ks[16], (DEPTH, D_MODEL), 0.02),
        'w_group': nrm(ks[17], (DEPTH, D_MODEL, N_GROUPS), D_MODEL ** -0.5),
        'b_group': nrm(ks[18], (DEPTH, N_GROUPS), 0.01),
        'w_expert': nrm(ks[19], (DEPTH, D_MODEL, N_EXPERTS), D_MODEL ** -0.5),
        'b_expert': nrm(ks[20], (DEPTH, N_EXPERTS), 0.01),
        'w_gate': nrm(ks[21], (DEPTH, N_EXPERTS, D_MODEL, D_EXPERT), D_MODEL ** -0.5),
        'w_up': nrm(ks[22], (DEPTH, N_EXPERTS, D_MODEL, D_EXPERT), D_MODEL ** -0.5),
        'w_down': nrm(ks[23], (DEPTH, N_EXPERTS, D_EXPERT, D_MODEL), DEEPNORM_BETA * D_EXPERT ** -0.5),
        'ln2_g': 1.0 + nrm(ks[24], (DEPTH, D_MODEL), 0.02),
        'ln2_b': nrm(ks[25], (DEPTH, D_MODEL), 0.02),
    }

def reference(x_prompt, x_sample, cache_cmp_k, cache_cmp_v, cache_sel_k, cache_sel_v, cache_win_k, cache_win_v,
              state_ret, page_table, w_in, w_cmp_k, w_cmp_v, ret_gn_g, w_o, ln1_g, ln1_b, w_group, b_group,
              w_expert, b_expert, w_gate, w_up, w_down, ln2_g, ln2_b):
    win_buf = cache_win_k.shape[2]
    hp, hs = x_prompt, x_sample
    acc_p = [[] for _ in range(7)]
    acc_s = [[] for _ in range(7)]
    for l in range(DEPTH):
        fp, st_p = _prompt_mixer(hp, win_buf, w_in[l], w_cmp_k[l], w_cmp_v[l], ret_gn_g[l])
        fs, st_s = _sample_mixer(hs, cache_cmp_k[l], cache_cmp_v[l], cache_sel_k[l], cache_sel_v[l],
                                 cache_win_k[l], cache_win_v[l], state_ret[l], page_table,
                                 w_in[l], w_cmp_k[l], w_cmp_v[l], ret_gn_g[l])
        moe = (w_group[l], b_group[l], w_expert[l], b_expert[l], w_gate[l], w_up[l], w_down[l])
        hp = _post_block(hp, fp, w_o[l], ln1_g[l], ln1_b[l], moe, ln2_g[l], ln2_b[l])
        hs = _post_block(hs, fs, w_o[l], ln1_g[l], ln1_b[l], moe, ln2_g[l], ln2_b[l])
        for acc, t in zip(acc_p, st_p):
            acc.append(t)
        for acc, t in zip(acc_s, st_s):
            acc.append(t)
    p_cmp_k, p_cmp_v, p_sel_k, p_sel_v, p_win_k, p_win_v, p_ret = [jnp.stack(a) for a in acc_p]
    s_cmp_k, s_cmp_v, s_sel_k, s_sel_v, s_win_k, s_win_v, s_ret = [jnp.stack(a) for a in acc_s]
    return (hp, hs, p_cmp_k, p_cmp_v, p_sel_k, p_sel_v, p_win_k, p_win_v, p_ret.astype(state_ret.dtype),
            s_cmp_k, s_cmp_v, s_sel_k, s_sel_v, s_win_k, s_win_v, s_ret.astype(state_ret.dtype))


_drawn_inputs = setup_inputs


def setup_inputs(seed=0):
    import zlib

    import numpy as np

    out = dict(_drawn_inputs(seed))
    spreads = {}
    factors = {'cache_cmp_v': 8.0,
     'cache_sel_k': 6.964,
     'cache_sel_v': 5.468,
     'ret_gn_g': 7.547,
     'b_group': 7.086,
     'ln2_g': 22.734,
     'ln2_b': 21.911,
     'w_cmp_v': 33.176,
     'b_expert': 19.88}
    for name, (base, spread) in spreads.items():
        noise = np.random.default_rng([zlib.crc32(name.encode()), seed]).standard_normal(out[name].shape)
        drawn = base * np.exp(spread * noise) if base else spread * noise
        out[name] = __import__('jax').numpy.asarray(drawn.astype(out[name].dtype))
    for name, factor in factors.items():
        out[name] = (out[name] * factor).astype(out[name].dtype)
    return out
```

```python
from contextlib import ExitStack

import numpy as np

import concourse.bass as bass
from concourse import mybir

F32 = mybir.dt.float32
I32 = mybir.dt.int32
ALU = mybir.AluOpType
ACT = mybir.ActivationFunctionType
AX_X = mybir.AxisListType.X

P = 128
D = 2048
KT = D // P
NP_TOK, NS_TOK = 256, 8
T = NP_TOK + NS_TOK
TOK = ((0, 128), (128, 128), (256, 8))
DH = 128
H = 8
KV = 2
G = H // KV
IN_W = 6680
RQ, RK, RV, RG, NQ, CK, CV, SK, SV, WK, WV, GL = (
    0, 1024, 2048, 3072, 4096, 5120, 5376, 5632, 5888, 6144, 6400, 6656)
NGL = 24
CHUNK = 512
PAST, PAGE, CB = 2048, 128, 64
NPAGE = PAST // PAGE
NBLK = PAST // CB
WIN = 512
TOPK = 16
NG, EPG, NE, DE = 4, 8, 32, 512
BS = 64
MAXB = NE + (2 * T - NE) // BS + 1
SCALE = DH ** -0.5
ALPHA = 2.0 ** 0.25
NEG = -1e30
EPS = 1e-5
RET_SCALE = DH ** -0.5



def _rope_table(pos, rot, theta):
    inv = (np.float32(theta) ** (-np.arange(0, rot, 2, dtype=np.float32) / np.float32(rot))).astype(np.float32)
    ang = (np.asarray(pos, np.float32)[:, None] * inv).astype(np.float32).astype(np.float64)
    return np.cos(ang).astype(np.float32), np.sin(ang).astype(np.float32)


def _layout(parts):
    at, places = 0, {}
    for name, a in parts:
        places[name] = (at, a.shape[1])
        at += a.shape[1]
    table = np.zeros((P, at), np.float32)
    for name, a in parts:
        table[:a.shape[0], places[name][0]:places[name][0] + a.shape[1]] = a
    return table, places


def constants():
    p = np.arange(P)
    log_g = np.log1p(-np.exp2(-5.0 - np.arange(H, dtype=np.float64)))
    rel = p[None, :] - p[:, None]
    dmask = np.concatenate([np.where(rel >= 0, np.exp(np.maximum(rel, 0) * g), 0.0) for g in log_g], 1)
    causal = np.concatenate([np.where(np.arange(NP_TOK)[None] <= (p + P * t)[:, None], 0.0, NEG) for t in (0, 1)], 1)
    cmp_ok = np.concatenate([((np.arange(4)[None] + 1) * CB - 1 <= (p + P * t)[:, None]) for t in (0, 1)], 1)
    cr, sr = _rope_table(np.arange(NP_TOK), DH, 10000.0)
    cn, sn = _rope_table(np.arange(NP_TOK), DH // 4, 500000.0)
    two = lambda a: np.concatenate([a[:P], a[P:]], 1)
    blk4 = np.stack([[(pp + P * t) // CB == b for b in range(4)] for t in (0, 1) for pp in p]).reshape(2, P, 4)
    prompt = [
        ("ident", np.eye(P)), ("dmask", dmask), ("causal", causal),
        ("cmp_add", np.where(cmp_ok, 0.0, NEG)), ("cmp_ok", cmp_ok * 1.0),
        ("q_dec", np.exp((p + 1.0)[:, None] * log_g[None])), ("k_dec", np.exp((P - 1.0 - p)[:, None] * log_g[None])),
        ("c_dec", np.tile(np.exp(P * log_g)[None], (P, 1))),
        ("cos_r", two(cr)), ("sin_r", two(sr)), ("cos_n", two(cn)), ("sin_n", two(sn)),
        ("blk2", np.stack([p < CB, p >= CB], 1) * 1.0), ("blk4", np.concatenate([blk4[0], blk4[1]], 1) * 1.0),
        ("eps", np.full((P, 1), EPS)),
    ]
    router = [
        ("ident", np.eye(P)), ("eps", np.full((P, 1), EPS)),
        ("before", (p[:, None] < p[None]) * 1.0), ("ones", np.ones((P, P))),
        ("lt32", (p[:NE, None] < np.arange(NE)[None]) * 1.0),
        ("desc4", np.tile(4.0 - np.arange(4), (P, 1))), ("desc8", np.tile(8.0 - np.arange(8), (P, 1))),
        ("valid", np.stack([p >= 0, p >= 0, p < NS_TOK], 1) * 1.0),
        ("blocks", np.tile(np.arange(MAXB) * 1.0, (P, 1))),
    ]
    row = np.arange(64)
    seq, head = row // 8, row % 8
    c1, s1 = _rope_table(np.array([PAST]), DH, 10000.0)
    c2, s2 = _rope_table(np.array([PAST]), DH // 4, 500000.0)
    is_k = np.isin(head, (0, 1, 4, 5))[:, None]
    is_w = (np.arange(32) % 4 < 2)[:, None]
    eye8 = (seq[:, None] == np.arange(8)[None]) * 1.0
    b33 = np.arange(NBLK + 1)
    sample = [
        ("cos_r", np.tile(c1, (64, 1))), ("sin_r", np.tile(s1, (64, 1))),
        ("cos_n", np.tile(c2, (64, 1))), ("sin_n", np.tile(s2, (64, 1))),
        ("cos_k", np.where(is_k, c2, 1.0)), ("sin_k", np.where(is_k, s2, 0.0)),
        ("cos_w", np.where(is_w, c2, 1.0)), ("sin_w", np.where(is_w, s2, 0.0)),
        ("own", eye8), ("own_add", (eye8 - 1.0) * -NEG),
        ("to_kv", ((seq * 2 + head // G)[:, None] == np.arange(16)[None]) * 1.0),
        ("from_kv", ((seq * 2 + head // G)[None] == np.arange(16)[:, None]) * 1.0),
        ("half", np.stack([head < G, head >= G], 1) * 1.0),
        ("own_row", np.tile(eye8.T.reshape(1, 512), (P, 1))),
        ("gamma", np.tile(np.exp(log_g)[None], (P, 1))),
        ("earlier", np.tile((b33[None] < b33[:, None]).reshape(1, -1) * 1.0, (16, 1))),
    ]
    return _layout(prompt), _layout(sample), _layout(router)


class Counter:

    def __init__(self, eng, sem):
        self.eng, self.sem, self.base, self.k, self.i, self.per = eng, sem, 0, 0, None, 0

    def enter(self, i, per):
        self.base, self.k, self.i, self.per = self.base + self.k, 0, i, per

    def leave(self, turns):
        assert self.k == self.per, (self.k, self.per)
        self.base, self.k, self.i = self.base + self.per * turns, 0, None

    def value(self):
        return self.base + self.k if self.i is None else self.i * self.per + (self.base + self.k)

    def link(self, ins):
        ins.then_inc(self.sem, 1)
        self.k += 1
        self.eng.wait_ge(self.sem, self.value())


class Memory:
    pass


def view(base, first, *dims):
    v = base[:, first:first + int(np.prod(dims))]
    if len(dims) == 1:
        return v
    names = "abcd"[:len(dims)]
    return v.rearrange(f"p ({' '.join(names)}) -> p {' '.join(names)}", **dict(zip(names, dims)))


class Taker:

    def __init__(self, base, first, end):
        self.base, self.at, self.end = base, first, end

    def __call__(self, *dims):
        v = view(self.base, self.at, *dims)
        self.at += int(np.prod(dims))
        assert self.at <= self.end, (self.at, self.end)
        return v


def rope(v, done, x, cos, sin, scratch):
    half = cos.shape[-1]
    lo, hi = x[..., 0:half], x[..., half:2 * half]
    ct, st = cos.broadcast_to(list(lo.shape)), sin.broadcast_to(list(lo.shape))
    v.tensor_tensor(scratch[0], lo, ct, ALU.mult)
    v.tensor_tensor(scratch[1], hi, st, ALU.mult)
    v.tensor_tensor(scratch[2], hi, ct, ALU.mult)
    done.link(v.tensor_tensor(scratch[3], lo, st, ALU.mult))
    v.tensor_tensor(lo, scratch[0], scratch[1], ALU.subtract)
    done.link(v.tensor_tensor(hi, scratch[2], scratch[3], ALU.add))


RING, PROJ, XT0 = 0, 20480, 33840
WORK = XT0 + KT * T
KVC = WORK + 7168
CONST = KVC + 1024
MISC = CONST + 2064
END = 52600


def phase_a(nc, a, o, m, sem):
    arena, ps, proj, xt, cst = m.arena, m.ps, m.proj, m.xt, m.cst
    ring = view(arena, RING, 8, 4, CHUNK)
    work = Taker(arena, WORK, KVC)
    gath = work(16, KV * DH)
    wsl = work(16, DH)
    sst = work(2, CHUNK)
    w_gl = m.small(KT, NGL)
    page_of = m.small(2).bitcast(I32)
    half_of = m.small(8).bitcast(I32)
    gather_row = m.small(8).bitcast(I32)

    loaded, consts_in = sem("loaded"), sem("consts_in")
    w_full = [sem(f"w_full{j}") for j in range(8)]
    w_free = sem("w_free")
    gl_ready = sem("gl_ready")
    acc_free = sem("acc_free")
    s_out = [sem("s_out0"), sem("s_out1")]
    rows_in, rows_ready = sem("rows_in"), sem("rows_ready")
    gathered, gath_free = sem("gathered"), sem("gath_free")
    wsl_in, wsl_free = sem("wsl_in"), sem("wsl_free")
    w_in = a["w_in"].rearrange("(k p) n -> p k n", p=P)

    with nc.Block() as block:
        @block.sync
        def _(sp):
            sp.dma_start(xt, a["x_t"].rearrange("p (k t) -> p k t", k=KT)).then_inc(loaded, 16)
            with sp.Fori(0, 6) as i:
                for j in range(8):
                    sp.wait_ge(w_free, i * 8 + (j + 1))
                    cols = i * 1024 + (j // 4) * 512
                    sp.dma_start(ring[:, j], w_in[:, (j % 4) * 4:(j % 4) * 4 + 4, bass.ds(cols, CHUNK)]
                                 ).then_inc(w_full[j], 16)
            for j in range(4):
                sp.wait_ge(w_free, 48 + j + 1)
                sp.dma_start(ring[:, j], w_in[:, j * 4:j * 4 + 4, 12 * CHUNK:13 * CHUNK]).then_inc(w_full[j], 16)

        @block.tensor
        def _(pe):
            pe.sem_inc(w_free, 8)
            pe.wait_ge(loaded, 16)

            def chunk(u, banks_free, full):
                pe.wait_ge(acc_free, banks_free)
                for j in range(4 * u, 4 * u + 4):
                    pe.wait_ge(w_full[j], full)
                    for kk in range(4):
                        k = 4 * (j - 4 * u) + kk
                        for t, (t0, n) in enumerate(TOK):
                            last = pe.matmul(ps[0:n, 3 * u + t, :], xt[:, k, t0:t0 + n], ring[:, j, kk, :],
                                             start=(k == 0), stop=(k == KT - 1))
                    last.then_inc(w_free, 1)

            with pe.Fori(0, 6) as i:
                for u in (0, 1):
                    chunk(u, i * 6 + 3 * (u + 1), i * 16 + 16)
            chunk(0, 39, 112)
            pe.wait_ge(acc_free, 42)
            pe.wait_ge(consts_in, 96)
            for t, (t0, n) in enumerate(TOK):
                for k in range(KT):
                    last = pe.matmul(ps[0:n, 3 + t, 0:NGL], xt[:, k, t0:t0 + n], w_gl[:, k, :],
                                     start=(k == 0), stop=(k == KT - 1))
            last.then_inc(gl_ready, 1)

        @block.scalar
        def _(act):
            act.sem_inc(acc_free, 6)
            act.dma_start(cst[:, 0:a["const_p"].shape[1]], a["const_p"]).then_inc(consts_in, 16)
            act.dma_start(w_gl, a["w_gl"].rearrange("p (k n) -> p k n", k=KT)).then_inc(consts_in, 16)
            for t in (0, 1):
                act.dma_start(m.wrep[t * CB:(t + 1) * CB, 0, :], a["w_cmp_k"]).then_inc(consts_in, 16)
                act.dma_start(m.wrep[t * CB:(t + 1) * CB, 1, :], a["w_cmp_v"]).then_inc(consts_in, 16)

            def read_out(u, ready, col, n, sample_to):
                if n == CHUNK:
                    act.wait_ge(w_free, ready * 4 + 8)
                else:
                    act.wait_ge(gl_ready, 1)
                for t in (0, 1):
                    nc.scalar.copy(proj[:, t, col], ps[:, 3 * u + t, 0:n]).then_inc(acc_free, 1)
                nc.scalar.copy(sst[0:NS_TOK, u, 0:n], ps[0:NS_TOK, 3 * u + 2, 0:n]).then_inc(acc_free, 1)
                act.wait_ge(acc_free, 6 + 3 * ready)
                act.dma_start(sample_to, sst[0:NS_TOK, u, 0:n]).then_inc(s_out[u], 16)

            with act.Fori(0, 6) as i:
                for u in (0, 1):
                    read_out(u, i * 2 + (u + 1), bass.ds(i * 1024 + u * 512, CHUNK), CHUNK,
                             m.ps_a[i, :, u * 512:(u + 1) * 512])
                for u in (0, 1):
                    act.wait_ge(s_out[u], i * 16 + 16)
            read_out(0, 13, slice(12 * CHUNK, 13 * CHUNK), CHUNK, m.ps_w)
            read_out(1, 14, slice(GL, IN_W), NGL, m.ps_g)
            for u in (0, 1):
                act.wait_ge(s_out[u], 112)

        @block.gpsimd
        def _(pool):
            for g in (0, 1):
                src = a["page_table"][4 * g:4 * g + 4, :].rearrange("s n -> (s n)").unsqueeze(1).unsqueeze(2)
                pool.dma_start(page_of[:, g:g + 1], src.broadcast_to([64, 2, 1])).then_inc(rows_in, 16)
            pool.dma_start(half_of[:, 0:8], a["half_of"]).then_inc(rows_in, 16)
            pool.wait_ge(rows_ready, 1)
            n = 0
            for kind in (0, 1):
                for quarter in range(4):
                    pool.wait_ge(wsl_free, 4 * kind + quarter + 1)
                    pool.dma_start(wsl, a[("w_cmp_k", "w_cmp_v")[kind]][quarter * 16:quarter * 16 + 16, :]
                                   .unsqueeze(0).broadcast_to([P, 16, DH])).then_inc(wsl_in, 16)
                    for g in (0, 1):
                        n += 1
                        pool.wait_ge(gath_free, n)
                        pool.indirect_dma_start(
                            out=gath.rearrange("p a b -> p (a b)"), out_offset=None,
                            in_=a[("cmp_k", "cmp_v")[kind]],
                            in_offset=bass.IndirectOffsetOnAxis(ap=gather_row[:, 4 * g + quarter:4 * g + quarter + 1], axis=0),
                        ).then_inc(gathered, 16)

        @block.vector
        def _(v):
            done = m.dve = Counter(v, m.dve_done)
            v.wait_ge(rows_in, 48)
            pages = page_of.unsqueeze(2).broadcast_to([P, 2, 4])
            done.link(v.tensor_scalar(gather_row.rearrange("p (g q) -> p g q", g=2), pages, 8, None, ALU.mult))
            v.tensor_tensor(gather_row, gather_row, half_of, ALU.add).then_inc(rows_ready, 1)
            v.sem_inc(wsl_free, 1)
            v.sem_inc(gath_free, 1)
            done.link(v.memset(m.pooled, 0.0))
            n = 0
            for kind in (0, 1):
                for quarter in range(4):
                    v.wait_ge(wsl_in, 16 * (4 * kind + quarter + 1))
                    for g in (0, 1):
                        n += 1
                        v.wait_ge(gathered, 16 * n)
                        x4 = gath.rearrange("p j (k d) -> p j k d", k=KV)
                        done.link(v.tensor_tensor(x4, x4, wsl.unsqueeze(2).broadcast_to([P, 16, KV, DH]), ALU.mult))
                        for w in (8, 4, 2, 1):
                            done.link(v.tensor_tensor(gath[:, 0:w], gath[:, 0:w], gath[:, w:2 * w], ALU.add))
                        done.link(v.tensor_tensor(m.pooled[:, kind, g], m.pooled[:, kind, g], gath[:, 0], ALU.add))
                        v.sem_inc(gath_free, 1)
                    v.sem_inc(wsl_free, 1)


def phase_b(nc, a, o, m, sem):
    arena, ps, proj, xt, cst = m.arena, m.ps, m.proj, m.xt, m.cst
    _, CP = constants()[0]
    c_ = lambda n, r=P: cst[0:r, CP[n][0]:CP[n][0] + CP[n][1]]
    kt = m.small(2, KV, NP_TOK)
    kc4 = m.small(KV, 4)
    vc4 = m.small(KV * DH)
    gates = m.small(2, NGL)
    mean, var = m.small(2, H), m.small(2, H)
    mx, nm, sm, rc = (m.small(2, 3) for _ in range(4))
    k_out = m.small(H, DH)
    w = Taker(arena, WORK, KVC)
    scratch = [w(2, H, 64) for _ in range(4)]
    squares = view(arena, WORK, 2, H, DH)
    gn = view(arena, WORK + 2048, H * DH)
    stage = w(4, P)
    qkt = w(4, P)
    kdec = w(2, P)
    att = w(2, P)
    s1 = w(P)
    cw = view(arena, WORK + 5760, 2, 2, KV * DH)
    n_w = Taker(arena, WORK, WORK + 5760)
    q_stage, q_t = n_w(2, 2, P), n_w(2, P)
    prob = n_w(2, 516)
    prob_t, prob_c = n_w(2, 512), n_w(256)
    zero = n_w(KV * DH)

    names = (
        "b_roped b_gates b_silu r_staged r_kdec r_t r_qkt r_att r_s r_ev r_o r_done r_done_h gn_in "
        "gn_var gn_std gn_out f_t f_free kt_t kt_in cw_ready c4_ready c4_in n_staged n_t n_qt n_s "
        "n_max n_exp n_prob n_pt n_ev n_o n_out b_stored zero_ready ")
    S = {n: sem(n) for n in names.split()}
    V = nc.vector

    with nc.Block() as block:
        @block.sync
        def _(sp):
            for n, (out, col) in enumerate((("p_ck", CK), ("p_cv", CV), ("p_sk", SK), ("p_sv", SV))):
                if n == 0:
                    sp.wait_ge(S["b_roped"], 3)
                sp.dma_start(o[out].rearrange("a b (t p) k d -> p (a b t) (k d)", p=P), proj[:, :, col:col + KV * DH]
                             ).then_inc(S["b_stored"], 16)
            for out, col in (("p_wk", WK), ("p_wv", WV)):
                rows = o[out].rearrange("a b (t p) k d -> p (a b t) (k d)", p=P)
                sp.dma_start(rows[:, 2:4, :], proj[:, :, col:col + KV * DH]).then_inc(S["b_stored"], 16)
                sp.wait_ge(S["zero_ready"], 1)
                for t in (0, 1):
                    sp.dma_start(rows[:, t, :], zero).then_inc(S["b_stored"], 16)
            sp.wait_ge(S["r_done"], 1)
            sp.dma_start(o["p_ret"].rearrange("a b h d e -> d (a b h) e"), k_out).then_inc(S["b_stored"], 16)
            sp.wait_ge(S["b_stored"], 16 * 11)

        @block.scalar
        def _(act):
            A = nc.scalar
            A.activation(gates, proj[:, :, GL:IN_W], ACT.Sigmoid).then_inc(S["b_gates"], 1)
            act.wait_ge(S["b_roped"], 2)
            with act.Fori(0, H) as h:
                act.wait_ge(S["r_t"], h + 1)
                A.copy(stage[:, 0:2, :], proj[:, :, bass.ds(h * DH + RQ, DH)])
                A.copy(stage[:, 2:4, :], proj[:, :, bass.ds(h * DH + RK, DH)]).then_inc(S["r_staged"], 1)
            A.activation(proj[:, :, RG:RG + 1024], proj[:, :, RG:RG + 1024], ACT.Silu).then_inc(S["b_silu"], 1)
            act.dma_start(gn, a["gn_g"].broadcast_to([P, H * DH])).then_inc(S["gn_in"], 16)
            act.wait_ge(S["gn_var"], 1)
            A.activation(var, var, ACT.Sqrt, bias=c_("eps"), scale=1.0 / DH).then_inc(S["gn_std"], 1)
            for br in (0, 1):
                act.wait_ge(S["kt_t"], 1)
                A.copy(kt[:, br], ps[:, 5 + br, :].rearrange("p (k t) -> p k t", k=KV)).then_inc(S["kt_in"], 1)
            act.wait_ge(S["c4_ready"], 1)
            A.copy(kc4, ps[:, 7, 0:8].rearrange("p (k b) -> p k b", k=KV)).then_inc(S["c4_in"], 1)
            A.copy(vc4[0:4, :], ps[0:4, 7, 256:512]).then_inc(S["c4_in"], 1)
            for n in range(4):
                act.wait_ge(S["f_t"], n + 1)
                A.copy(xt[:, 2 * n:2 * n + 2, 0:256], ps[:, n, :].rearrange("p (f t) -> p f t", f=2)
                       ).then_inc(S["f_free"], 1)
            with act.Fori(0, G) as g:
                for kv in range(KV):
                    head = g * DH + (NQ + kv * G * DH)
                    A.copy(q_stage[:, kv], proj[:, :, bass.ds(head, DH)]).then_inc(S["n_staged"], 1)
                    act.wait_ge(S["n_max"], g * 2 + kv + 1)
                    for t in (0, 1):
                        for br in range(3):
                            cols = slice(512, 516) if br == 2 else slice(256 * br, 256 * br + 256)
                            last = A.activation(prob[:, t, cols], prob[:, t, cols], ACT.Exp,
                                                bias=nm[:, t, br:br + 1], accum_out=sm[:, t, br:br + 1])
                    last.then_inc(S["n_exp"], 1)
                    act.wait_ge(S["n_pt"], g * 2 + kv + 1)
                    A.copy(prob_t[:, 0], ps[:, 4, :]).then_inc(S["n_ev"], 1)
                    act.wait_ge(S["n_o"], g * 2 + kv + 1)
                    A.copy(xt[:, bass.ds(g + (H + kv * G), 1), 0:256], ps[:, 7, 0:256].unsqueeze(1)
                           ).then_inc(S["n_out"], 1)

        @block.vector
        def _(v):
            done = m.dve
            done.eng = v
            by_head = lambda col, n: proj[:, :, col:col + n * DH].rearrange("p t (h d) -> p t h d", d=DH)
            table = lambda n, half: c_(n).rearrange("p (t h) -> p t h", t=2).unsqueeze(2)
            cr, sr, cn, sn = (table(n, 0) for n in ("cos_r", "sin_r", "cos_n", "sin_n"))
            rope(v, done, by_head(RQ, H), cr, sr, scratch)
            v.sem_inc(S["b_roped"], 1)
            rope(v, done, by_head(RK, H), cr, sr, scratch)
            done.link(v.tensor_scalar(proj[:, :, RK:RV], proj[:, :, RK:RV], RET_SCALE, None, ALU.mult))
            v.sem_inc(S["b_roped"], 1)
            for n, col in ((H, NQ), (KV, CK), (KV, SK), (KV, WK)):
                rope(v, done, by_head(col, n), cn, sn, [s[:, :, 0:n, 0:16] for s in scratch])
            v.sem_inc(S["b_roped"], 1)
            for k, col in enumerate((CK, CV)):
                last = v.tensor_tensor(
                    cw[:, k].rearrange("p t (k d) -> p (t k) d", d=DH),
                    proj[:, :, col:col + KV * DH].rearrange("p t (k d) -> p t k d", d=DH),
                    m.wrep[:, k].unsqueeze(1).unsqueeze(1).broadcast_to([P, 2, KV, DH]), ALU.mult)
            last.then_inc(S["cw_ready"], 1)
            with v.Fori(0, H) as h:
                done.enter(h, 3)
                for t in (0, 1):
                    last = v.tensor_scalar(kdec[:, t], proj[:, t, bass.ds(h * DH + RK, DH)],
                                           cst[:, bass.ds(h + CP["k_dec"][0], 1)], None, ALU.mult)
                last.then_inc(S["r_kdec"], 1)
                v.wait_ge(S["r_t"], h + 2)
                v.tensor_copy(qkt.rearrange("p a b -> p (a b)"), ps[:, 0, :]).then_inc(S["r_qkt"], 1)
                v.wait_ge(S["r_att"], h + 1)
                v.tensor_tensor(att, ps[:, 1, 0:256].rearrange("p (c i) -> p c i", c=2),
                                cst[:, bass.ds(h * P + CP["dmask"][0], P)].unsqueeze(1).broadcast_to([P, 2, P]), ALU.mult)
                v.wait_ge(S["r_s"], h + 1)
                done.link(v.tensor_copy(s1, ps[:, 2, 0:P]))
                done.link(v.scalar_tensor_tensor(k_out[:, bass.ds(h, 1), :], s1.unsqueeze(1), cst[:, bass.ds(h + CP["c_dec"][0], 1)],
                                                 ps[:, 3, 0:P].unsqueeze(1), ALU.mult, ALU.add))
                v.sem_inc(S["r_ev"], 1)
                v.wait_ge(S["r_o"], h + 1)
                o_col = bass.ds(h * DH + RQ, DH)
                v.tensor_copy(proj[:, 0, o_col], ps[:, 4, 0:P])
                done.link(v.tensor_copy(proj[:, 1, o_col], ps[:, 4, P:2 * P]))
                v.scalar_tensor_tensor(proj[:, 1, o_col], ps[:, 4, 2 * P:3 * P], cst[:, bass.ds(h + CP["q_dec"][0], 1)],
                                       proj[:, 1, o_col], ALU.mult, ALU.add).then_inc(S["r_done_h"], 1)
                v.wait_ge(S["r_done_h"], h + 1)
            done.leave(H)
            v.sem_inc(S["r_done"], 1)
            heads = by_head(RQ, H)
            done.link(v.tensor_reduce(mean, heads, AX_X, ALU.add))
            done.link(v.tensor_scalar(mean, mean, 1.0 / DH, None, ALU.mult))
            done.link(v.tensor_tensor(heads, heads, mean.unsqueeze(3).broadcast_to([P, 2, H, DH]), ALU.subtract))
            done.link(v.tensor_tensor(squares, heads, heads, ALU.mult))
            v.tensor_reduce(var, squares, AX_X, ALU.add).then_inc(S["gn_var"], 1)
            v.wait_ge(S["gn_std"], 1)
            done.link(v.reciprocal(var, var))
            done.link(v.tensor_tensor(heads, heads, var.unsqueeze(3).broadcast_to([P, 2, H, DH]), ALU.mult))
            v.wait_ge(S["gn_in"], 16)
            flat = proj[:, :, RQ:RQ + H * DH]
            done.link(v.tensor_tensor(flat, flat, gn.unsqueeze(1).broadcast_to([P, 2, H * DH]), ALU.mult))
            v.wait_ge(S["b_silu"], 1)
            v.tensor_tensor(flat, flat, proj[:, :, RG:RG + 1024], ALU.mult).then_inc(S["gn_out"], 1)
            v.wait_ge(S["gn_out"], 1)
            v.memset(zero, 0.0).then_inc(S["zero_ready"], 1)
            v.wait_ge(S["b_gates"], 1)
            causal = c_("causal").rearrange("p (t k) -> p t k", t=2)
            cmp_add = c_("cmp_add").rearrange("p (t k) -> p t k", t=2)
            cmp_ok = c_("cmp_ok").rearrange("p (t k) -> p t k", t=2)
            main = prob[:, :, 0:512].rearrange("p t (b k) -> p t b k", b=2)
            cmpp = prob[:, :, 512:516]
            with v.Fori(0, G) as g:
                done.enter(g, 2 * 8)
                for kv in range(KV):
                    n = g * 2 + kv + 1
                    v.wait_ge(S["n_t"], n)
                    v.tensor_copy(q_t.rearrange("p a b -> p (a b)"), ps[:, 0, 0:256]).then_inc(S["n_qt"], 1)
                    v.wait_ge(S["n_s"], n)
                    for t in (0, 1):
                        v.scalar_tensor_tensor(main[:, t], ps[:, 1 + t, :].rearrange("p (b k) -> p b k", b=2), SCALE,
                                               causal[:, t].unsqueeze(1).broadcast_to([P, 2, 256]), ALU.mult, ALU.add)
                    done.link(v.scalar_tensor_tensor(cmpp, ps[:, 3, 0:8].rearrange("p (t k) -> p t k", t=2), SCALE,
                                                     cmp_add, ALU.mult, ALU.add))
                    v.tensor_reduce(mx[:, :, 0:2], main, AX_X, ALU.max)
                    done.link(v.tensor_reduce(mx[:, :, 2:3], cmpp.unsqueeze(2), AX_X, ALU.max))
                    v.tensor_scalar(nm, mx, -1.0, None, ALU.mult).then_inc(S["n_max"], 1)
                    v.wait_ge(S["n_exp"], n)
                    v.tensor_tensor(cmpp, cmpp, cmp_ok, ALU.mult)
                    done.link(v.reciprocal(rc, sm))
                    gate0 = g * 3 + kv * 12
                    done.link(v.tensor_tensor(rc[:, :, 0:2], rc[:, :, 0:2], gates[:, :, bass.ds(gate0 + 1, 2)], ALU.mult))
                    done.link(v.tensor_tensor(rc[:, :, 2:3], rc[:, :, 2:3], gates[:, :, bass.ds(gate0, 1)], ALU.mult))
                    done.link(v.tensor_tensor(cmpp, cmpp, rc[:, :, 2:3].broadcast_to([P, 2, 4]), ALU.mult))
                    for t in (0, 1):
                        done.link(v.tensor_tensor(main[:, t], main[:, t], rc[:, t, 0:2].unsqueeze(2).broadcast_to([P, 2, 256]), ALU.mult))
                    v.sem_inc(S["n_prob"], 1)
                    v.wait_ge(S["n_pt"], n)
                    v.tensor_copy(prob_c[0:4, :], ps[0:4, 6, 0:256])
                    v.tensor_copy(prob_t[:, 1], ps[:, 5, :]).then_inc(S["n_ev"], 1)
                    v.wait_ge(S["n_o"], n)
            done.leave(G)

        @block.tensor
        def _(pe):
            ident = c_("ident")
            pe.sem_inc(S["r_t"], 1)
            with pe.Fori(0, H) as h:
                pe.wait_ge(S["r_staged"], h + 1)
                for n in range(4):
                    last = pe.transpose(ps[:, 0, n * P:(n + 1) * P], stage[:, n, :], ident)
                last.then_inc(S["r_t"], 1)
                pe.wait_ge(S["r_qkt"], h + 1)
                for c in (0, 1):
                    last = pe.matmul(ps[:, 1, c * P:(c + 1) * P], qkt[:, 2 + c, :], qkt[:, c, :], start=True, stop=True)
                last.then_inc(S["r_att"], 1)
                pe.wait_ge(S["r_kdec"], h + 1)
                vals = [proj[:, c, bass.ds(h * DH + RV, DH)] for c in (0, 1)]
                for c in (0, 1):
                    last = pe.matmul(ps[:, 2 + c, 0:P], kdec[:, c, :], vals[c], start=True, stop=True)
                last.then_inc(S["r_s"], 1)
                pe.wait_ge(S["r_ev"], h + 1)
                for c in (0, 1):
                    pe.matmul(ps[:, 4, c * P:(c + 1) * P], att[:, c, :], vals[c], start=True, stop=True)
                pe.matmul(ps[:, 4, 2 * P:3 * P], qkt[:, 1, :], s1, start=True, stop=True).then_inc(S["r_o"], 1)
                pe.wait_ge(S["r_done_h"], h + 1)
            pe.wait_ge(S["b_roped"], 3)
            for br, col in enumerate((SK, WK)):
                for kv in range(KV):
                    for t in (0, 1):
                        last = pe.transpose(ps[:, 5 + br, kv * 256 + t * P:kv * 256 + (t + 1) * P],
                                            proj[:, t, col + kv * DH:col + (kv + 1) * DH], ident)
            last.then_inc(S["kt_t"], 1)
            pe.wait_ge(S["cw_ready"], 1)
            for t in (0, 1):
                for kv in range(KV):
                    pe.matmul(ps[:, 7, kv * 4 + 2 * t:kv * 4 + 2 * t + 2], cw[:, 0, t, kv * DH:(kv + 1) * DH],
                              c_("blk2"), start=True, stop=True)
            for t in (0, 1):
                last = pe.matmul(ps[0:4, 7, 256:512], c_("blk4")[:, 4 * t:4 * t + 4], cw[:, 1, t, :],
                                 start=(t == 0), stop=(t == 1))
            last.then_inc(S["c4_ready"], 1)
            pe.wait_ge(S["gn_out"], 1)
            for n in range(4):
                for f in (0, 1):
                    for t in (0, 1):
                        last = pe.transpose(ps[:, n, f * 256 + t * P:f * 256 + (t + 1) * P],
                                            proj[:, t, (2 * n + f) * DH:(2 * n + f + 1) * DH], ident)
                last.then_inc(S["f_t"], 1)
            pe.wait_ge(S["f_free"], 4)
            pe.wait_ge(S["kt_in"], 2)
            pe.wait_ge(S["c4_in"], 2)
            with pe.Fori(0, G) as g:
                for kv in range(KV):
                    n = g * 2 + kv + 1
                    pe.wait_ge(S["n_staged"], n)
                    for t in (0, 1):
                        last = pe.transpose(ps[:, 0, t * P:(t + 1) * P], q_stage[:, kv, t, :], ident)
                    last.then_inc(S["n_t"], 1)
                    pe.wait_ge(S["n_qt"], n)
                    for t in (0, 1):
                        pe.matmul(ps[:, 1 + t, :], q_t[:, t, :], kt[:, :, kv, :], start=True, stop=True)
                        last = pe.matmul(ps[:, 3, 4 * t:4 * t + 4], q_t[:, t, :], kc4[:, kv, :], start=True, stop=True)
                    last.then_inc(S["n_s"], 1)
                    pe.wait_ge(S["n_prob"], n)
                    for t in (0, 1):
                        for c in range(4):
                            pe.transpose(ps[:, 4 + t, c * P:(c + 1) * P], prob[:, t, c * P:(c + 1) * P], ident)
                        last = pe.transpose(ps[0:4, 6, t * P:(t + 1) * P], prob[:, t, 512:516], ident)
                    last.then_inc(S["n_pt"], 1)
                    pe.wait_ge(S["n_ev"], n * 2)
                    for c in range(4):
                        v0 = (SV, WV)[c // 2] + kv * DH
                        pe.matmul(ps[:, 7, 0:256], proj[:, c % 2, v0:v0 + DH], prob_t[:, :, c * P:(c + 1) * P],
                                  start=(c == 0), stop=False)
                    pe.matmul(ps[:, 7, 0:256], vc4[0:4, kv * DH:(kv + 1) * DH], prob_c[0:4, :],
                              start=False, stop=True).then_inc(S["n_o"], 1)
                    pe.wait_ge(S["n_out"], n)


def phase_s(nc, a, o, m, sem):
    arena, ps, xt, ident = m.arena, m.ps, m.xt, m.cst[:, 0:P]
    (_, CP), (cs, CS), _ = constants()
    w = Taker(arena, PROJ, XT0)
    ct = w(cs.shape[1])
    s_ = lambda n, r=64: ct[0:r, CS[n][0]:CS[n][0] + CS[n][1]]
    rq, rk, rg, nq, gnr, kv5, kvw = (w(DH) for _ in range(7))
    v_new = w(KV * DH)
    gate = w(3)
    rs = [w(64) for _ in range(4)]
    tr = w(5, 64)
    q_kv = w(KV, 64)
    q_own = w(NS_TOK, KV, 64)
    q_st = w(4, KV, 64)
    kct = w(KV, KV * P)
    prob_c = w(256)
    sel = w(NBLK + 1)
    imp8, score = w(256), w(NBLK + 1)
    selrow = w(NBLK + 1)
    mx, nm, sm, rc = (w(3) for _ in range(4))
    osum, otmp, ot_r = w(DH), w(DH), w(64)
    mean, var = w(1), w(1)
    prob = view(arena, WORK, PAST + 16 + WIN)
    probs, probw = prob[0:64, 0:PAST + 8], prob[0:64, PAST + 8:PAST + 16 + WIN]
    new_cols = prob[0:64, PAST:PAST + 16]
    pt = view(arena, WORK + 2600, 23, 64)
    pown = view(arena, WORK + 4100, 2, 20, 64)
    assert 4100 + 2560 <= 7168
    cmpt = view(arena, WORK, NBLK + 1, NBLK + 1)
    eqt = view(arena, WORK + 1100, NBLK + 1, NBLK + 1)
    st_w = Taker(arena, RING, PROJ)
    s_old, s_new = [st_w(H, DH) for _ in (0, 1)], [st_w(H, DH) for _ in (0, 1)]
    v_rep = [st_w(H, DH) for _ in (0, 1)]
    pages = [view(arena, RING + 4096 * n, NPAGE, KV * DH) for n in range(4)]
    windows = view(arena, RING + 16384, 4, 2 * WIN)
    names = (
        "s_in s_rot s_tr s_tr_in s_roped_out s_st_in0 s_st_in1 s_st_new s_st_o s_st_out0 s_st_out1 "
        "s_otr s_or s_or_in s_var s_std s_silu s_gated s_ft s_ftin s_q s_kct s_kct_in s_c s_cexp "
        "s_cmax s_cprob s_imp s_rank s_selb s_wfull s_kdone s_qst s_max s_exp s_prob s_pt s_pt_in "
        "s_pown s_half s_ot s_fin s_page_in s_gate s_cpout s_vst ")
    S = {n: sem(n) for n in names.split()}
    k_full = [sem(f"s_kfull{n}") for n in range(4)]
    v_full = [sem(f"s_vfull{n}") for n in range(4)]

    with nc.Block() as block:
        @block.sync
        def _(sp):
            sp.dma_start(m.page_tab[0:1, :], a["page_table"].rearrange("s n -> (s n)").unsqueeze(0)).then_inc(S["s_page_in"], 16)
            sp.wait_ge(S["s_page_in"], 16)
            for b in range(NS_TOK):
                if b >= 2:
                    sp.wait_ge(S["s_st_new"], b - 1)
                sp.dma_start(s_old[b % 2], a["state"][b].rearrange("h d e -> d h e")).then_inc(S[f"s_st_in{b % 2}"], 16)
                sp.dma_start(v_rep[b % 2].rearrange("p h d -> p (h d)"), m.ps_a[2, b:b + 1, :].broadcast_to([P, H * DH])
                             ).then_inc(S[f"s_st_in{b % 2}"], 16)
            sp.wait_ge(S["s_st_o"], 8)
            sp.wait_ge(S["s_st_out0"], 64)
            sp.wait_ge(S["s_st_out1"], 64)
            for full, src, wsrc, used in ((k_full, "sel_kt", "win_kt", "s_kdone"), (v_full, "sel_v", "win_v", "s_vst")):
                if full is v_full:
                    sp.wait_ge(S["s_kdone"], 8)
                for i in range(2):
                    for u in range(4):
                        if i:
                            sp.wait_ge(S[used], u + 1)
                        with sp.Fori(0, NPAGE) as page:
                            phys = sp.value_load(m.page_tab[0:1, bass.ds(page + (4 * i + u) * NPAGE, 1)],
                                                 min_val=0, max_val=a["sel_v"].shape[0] - 1)
                            if full is k_full:
                                sp.dma_start(pages[u][:, bass.ds(page, 1), :], a[src][phys].rearrange("d k t -> d (k t)").unsqueeze(1)
                                             ).then_inc(full[u], 16)
                            else:
                                sp.dma_start(pages[u][:, bass.ds(page, 1), :], a[src][phys].unsqueeze(1)).then_inc(full[u], 16)
                    if i:
                        sp.wait_ge(S[used], 4)
                    if full is k_full:
                        wsrc_v = a[wsrc][4 * i:4 * i + 4].rearrange("s d k t -> d s (k t)")
                        sp.dma_start(windows, wsrc_v).then_inc(S["s_wfull"], 16)
                    else:
                        for u in range(4):
                            sp.dma_start(windows[:, u, :].rearrange("p (j c) -> p j c", j=4),
                                         a[wsrc][4 * i + u].rearrange("(j p) c -> p j c", p=P)).then_inc(S["s_wfull"], 16)

        @block.gpsimd
        def _(pool):
            for out, src in (("s_wk", "win_k"), ("s_wv", "win_v")):
                rows = o[out].rearrange("a s t k d -> (a s) t (k d)")
                pool.dma_start(rows[:, 0:WIN - 1, :], a[src][:, 1:WIN, :]).then_inc(S["s_cpout"], 16)
            pool.wait_ge(S["s_rot"], 1)
            pool.dma_start(m.kv5_d.rearrange("s x d -> (s x) d"), kv5[0:64, :]).then_inc(S["s_roped_out"], 16)
            pool.dma_start(m.kvw_d.rearrange("s x d -> (s x) d"), kvw[0:32, :]).then_inc(S["s_roped_out"], 16)
            pool.wait_ge(S["s_roped_out"], 32)
            for n, out in enumerate(("s_ck", "s_cv", "s_sk", "s_sv")):
                pool.dma_start(o[out].rearrange("a s t k d -> (a s t) k d"), m.kv5_d[:, 2 * n:2 * n + 2, :]).then_inc(S["s_cpout"], 16)
            for n, out in enumerate(("s_wk", "s_wv")):
                pool.dma_start(o[out][0, :, WIN - 1, :, :], m.kvw_d[:, 2 * n:2 * n + 2, :]).then_inc(S["s_cpout"], 16)
            pool.wait_ge(S["s_cpout"], 128)

        @block.scalar
        def _(act):
            A = nc.scalar
            rows = lambda n: m.ps_a[n].rearrange("s (h d) -> (s h) d", d=DH)
            act.dma_start(ct, a["const_s"]).then_inc(S["s_in"], 16)
            for dst, n in ((rq, 0), (rk, 1), (rg, 3), (nq, 4), (kv5, 5)):
                act.dma_start(dst[0:64, :], rows(n)).then_inc(S["s_in"], 16)
            act.dma_start(kvw[0:32, :], m.ps_w.rearrange("s (x d) -> (s x) d", d=DH)).then_inc(S["s_in"], 16)
            act.dma_start(v_new[0:8, :], m.ps_a[5, :, 768:1024]).then_inc(S["s_in"], 16)
            act.dma_start(v_new[8:16, :], m.ps_w[:, 256:512]).then_inc(S["s_in"], 16)
            act.dma_start(gate[0:64, :], m.ps_g.rearrange("s (h t) -> (s h) t", t=3)).then_inc(S["s_in"], 16)
            act.dma_start(gnr[0:64, :], a["gn_rows"]).then_inc(S["s_in"], 16)
            act.wait_ge(S["s_in"], 176)
            A.activation(gate[0:64, :], gate[0:64, :], ACT.Sigmoid).then_inc(S["s_gate"], 1)
            A.activation(rg[0:64, :], rg[0:64, :], ACT.Silu).then_inc(S["s_silu"], 1)
            act.wait_ge(S["s_tr"], 1)
            A.copy(tr.rearrange("p a b -> p (a b)")[:, 0:288], ps[:, 0, 0:288]).then_inc(S["s_tr_in"], 1)
            for b in range(NS_TOK):
                act.wait_ge(S["s_st_new"], b + 1)
                act.dma_start(o["s_ret"][0, b].rearrange("h d e -> d h e"), s_new[b % 2]).then_inc(S[f"s_st_out{b % 2}"], 16)
            act.wait_ge(S["s_st_o"], 8)
            A.copy(ot_r, ps[:, 1, 0:64]).then_inc(S["s_otr"], 1)
            act.wait_ge(S["s_or"], 1)
            A.copy(osum[0:64, :], ps[0:64, 2, 0:DH]).then_inc(S["s_or_in"], 1)
            act.wait_ge(S["s_var"], 1)
            A.activation(var[0:64, :], var[0:64, :], ACT.Sqrt, bias=m.cst[0:64, CP["eps"][0]:CP["eps"][0] + 1], scale=1.0 / DH
                         ).then_inc(S["s_std"], 1)
            act.wait_ge(S["s_ft"], 1)
            A.copy(xt[:, 0:H, NP_TOK:T], ps[:, 3, 0:64].rearrange("p (s h) -> p h s", h=H)).then_inc(S["s_ftin"], 1)
            act.wait_ge(S["s_kct"], 1)
            A.copy(kct.rearrange("p a b -> p (a b)"), ps[:, 4, :]).then_inc(S["s_kct_in"], 1)
            act.wait_ge(S["s_cmax"], 1)
            A.activation(prob_c[0:64, :], prob_c[0:64, :], ACT.Exp, bias=nm[0:64, 0:1], accum_out=sm[0:64, 0:1]
                         ).then_inc(S["s_cexp"], 1)
            act.wait_ge(S["s_q"], 1)
            for b in range(NS_TOK):
                if b >= 4:
                    act.wait_ge(S["s_kdone"], b - 3)
                A.copy(q_st[:, b % 4], q_own[:, b]).then_inc(S["s_qst"], 1)
            act.wait_ge(S["s_max"], 1)
            A.activation(probs, probs, ACT.Exp, bias=nm[0:64, 1:2], accum_out=sm[0:64, 1:2])
            A.activation(probw, probw, ACT.Exp, bias=nm[0:64, 2:3], accum_out=sm[0:64, 2:3]).then_inc(S["s_exp"], 1)
            act.wait_ge(S["s_pt"], 1)
            A.copy(pt[:, 0:8, :].rearrange("p a b -> p (a b)"), ps[:, 0, :]).then_inc(S["s_pt_in"], 1)
            A.copy(pt[:, 8:16, :].rearrange("p a b -> p (a b)"), ps[:, 1, :]).then_inc(S["s_pt_in"], 1)
            A.copy(pt[:, 16:22, :].rearrange("p a b -> p (a b)"), ps[:, 2, 0:384]).then_inc(S["s_pt_in"], 1)
            A.copy(pt[0:16, 22, :], ps[0:16, 2, 384:448]).then_inc(S["s_pt_in"], 1)
            act.wait_ge(S["s_ot"], 1)
            A.copy(xt[:, H:2 * H, NP_TOK:T], ps[:, 3, 0:64].rearrange("p (s h) -> p h s", h=H)).then_inc(S["s_fin"], 1)
            act.wait_ge(S["s_fin"], 1)

        @block.vector
        def _(v):
            done = m.dve
            r64 = lambda t: t[0:64, :]
            v.wait_ge(S["s_in"], 176)
            rope(v, done, rq[0:64, :], s_("cos_r"), s_("sin_r"), [r[0:64, :] for r in rs])
            rope(v, done, rk[0:64, :], s_("cos_r"), s_("sin_r"), [r[0:64, :] for r in rs])
            done.link(v.tensor_scalar(rk[0:64, :], rk[0:64, :], RET_SCALE, None, ALU.mult))
            rope(v, done, nq[0:64, :], s_("cos_n"), s_("sin_n"), [r[0:64, 0:16] for r in rs])
            rope(v, done, kv5[0:64, :], s_("cos_k"), s_("sin_k"), [r[0:64, 0:16] for r in rs])
            rope(v, done, kvw[0:32, :], s_("cos_w", 32), s_("sin_w", 32), [r[0:32, 0:16] for r in rs])
            v.memset(q_kv, 0.0)
            done.link(v.memset(q_own, 0.0))
            v.sem_inc(S["s_rot"], 1)
            v.wait_ge(S["s_tr_in"], 1)
            gam = s_("gamma", P).unsqueeze(2).broadcast_to([P, H, DH])
            for b in range(NS_TOK):
                v.wait_ge(S[f"s_st_in{b % 2}"], 32 * (b // 2 + 1))
                if b >= 2:
                    v.wait_ge(S["s_st_o"], b - 1)
                    v.wait_ge(S[f"s_st_out{b % 2}"], 16 * (b // 2))
                v.tensor_tensor(s_old[b % 2], s_old[b % 2], gam, ALU.mult)
                done.link(v.tensor_tensor(v_rep[b % 2], v_rep[b % 2], tr[:, 2, 8 * b:8 * b + 8].unsqueeze(2).broadcast_to([P, H, DH]), ALU.mult))
                v.tensor_tensor(s_new[b % 2], s_old[b % 2], v_rep[b % 2], ALU.add).then_inc(S["s_st_new"], 1)
            qs = tr[:, 0, :].rearrange("p (s k g) -> p s k g", s=NS_TOK, k=KV)
            for kv in range(KV):
                v.tensor_copy(q_kv[:, kv].rearrange("p (s k g) -> p s k g", s=NS_TOK, k=KV)[:, :, kv, :], qs[:, :, kv, :])
            for b in range(NS_TOK):
                for kv in range(KV):
                    last = v.tensor_copy(q_own[:, b, kv, 8 * b + 4 * kv:8 * b + 4 * kv + 4], qs[:, b, kv, :])
            last.then_inc(S["s_q"], 1)
            v.wait_ge(S["s_or_in"], 1)
            done.link(v.tensor_reduce(r64(mean), r64(osum), AX_X, ALU.add))
            done.link(v.tensor_scalar(r64(mean), r64(mean), 1.0 / DH, None, ALU.mult))
            done.link(v.tensor_scalar(r64(osum), r64(osum), r64(mean), None, ALU.subtract))
            done.link(v.tensor_tensor(r64(otmp), r64(osum), r64(osum), ALU.mult))
            v.tensor_reduce(r64(var), r64(otmp), AX_X, ALU.add).then_inc(S["s_var"], 1)
            v.wait_ge(S["s_std"], 1)
            done.link(v.reciprocal(r64(var), r64(var)))
            done.link(v.scalar_tensor_tensor(r64(osum), r64(osum), r64(var), r64(gnr), ALU.mult, ALU.mult))
            v.wait_ge(S["s_silu"], 1)
            v.tensor_tensor(r64(osum), r64(osum), r64(rg), ALU.mult).then_inc(S["s_gated"], 1)
            v.wait_ge(S["s_c"], 1)
            own_add, own = s_("own_add").unsqueeze(2), s_("own").unsqueeze(2)
            pc = prob_c[0:64, :].rearrange("p (s b) -> p s b", s=NS_TOK)
            done.link(v.scalar_tensor_tensor(pc, ps[0:64, 5, 0:256].rearrange("p (s b) -> p s b", s=NS_TOK), SCALE,
                                             own_add.broadcast_to([64, 8, NBLK]), ALU.mult, ALU.add))
            done.link(v.tensor_reduce(mx[0:64, 0:1], prob_c[0:64, :], AX_X, ALU.max))
            v.tensor_scalar(nm[0:64, 0:1], mx[0:64, 0:1], -1.0, None, ALU.mult).then_inc(S["s_cmax"], 1)
            v.wait_ge(S["s_cexp"], 1)
            done.link(v.reciprocal(rc[0:64, 0:1], sm[0:64, 0:1]))
            done.link(v.tensor_tensor(pc, pc, own.broadcast_to([64, 8, NBLK]), ALU.mult))
            v.tensor_scalar(prob_c[0:64, :], prob_c[0:64, :], rc[0:64, 0:1], None, ALU.mult).then_inc(S["s_cprob"], 1)
            v.wait_ge(S["s_imp"], 1)
            done.link(v.tensor_copy(imp8[0:16, :], ps[0:16, 6, 0:256]))
            done.link(v.tensor_reduce(score[0:16, 0:NBLK], imp8[0:16, :].rearrange("p (s b) -> p b s", s=NS_TOK), AX_X, ALU.add))
            v.memset(score[0:16, 0:1], -NEG)
            done.link(v.memset(score[0:16, NBLK - 1:NBLK + 1], -NEG))
            other = score[0:16, :].unsqueeze(1).broadcast_to([16, NBLK + 1, NBLK + 1])
            mine = score[0:16, :].unsqueeze(2).broadcast_to([16, NBLK + 1, NBLK + 1])
            v.tensor_tensor(cmpt[0:16], other, mine, ALU.is_gt)
            done.link(v.tensor_tensor(eqt[0:16], other, mine, ALU.is_equal))
            done.link(v.tensor_tensor(eqt[0:16], eqt[0:16], s_("earlier", 16).rearrange("p (a b) -> p a b", a=NBLK + 1), ALU.mult))
            done.link(v.tensor_tensor(cmpt[0:16], cmpt[0:16], eqt[0:16], ALU.add))
            done.link(v.tensor_reduce(selrow[0:16, :], cmpt[0:16], AX_X, ALU.add))
            v.tensor_scalar(selrow[0:16, :], selrow[0:16, :], float(TOPK), None, ALU.is_lt).then_inc(S["s_rank"], 1)
            v.wait_ge(S["s_selb"], 1)
            done.link(v.tensor_scalar(sel[0:64, :], ps[0:64, 6, 256:256 + NBLK + 1], 1.0, -NEG, ALU.subtract, ALU.mult))
            v.wait_ge(S["s_kdone"], 8)
            for c in range(4):
                v.scalar_tensor_tensor(probs[:, c * 512:(c + 1) * 512].rearrange("p (b t) -> p b t", t=CB),
                                       ps[0:64, c, :].rearrange("p (b t) -> p b t", t=CB), SCALE,
                                       sel[0:64, 8 * c:8 * c + 8].unsqueeze(2).broadcast_to([64, 8, CB]), ALU.mult, ALU.add)
            v.scalar_tensor_tensor(probs[:, PAST:PAST + 8], ps[0:64, 5, 256:264], SCALE, s_("own_add"), ALU.mult, ALU.add)
            v.scalar_tensor_tensor(probw[:, 0:8], ps[0:64, 5, 264:272], SCALE, s_("own_add"), ALU.mult, ALU.add)
            done.link(v.tensor_scalar(probw[:, 8:8 + WIN], ps[0:64, 4, :], SCALE, None, ALU.mult))
            done.link(v.memset(probw[:, 8:9], NEG))
            v.tensor_reduce(mx[0:64, 1:2], probs, AX_X, ALU.max)
            done.link(v.tensor_reduce(mx[0:64, 2:3], probw, AX_X, ALU.max))
            v.tensor_scalar(nm[0:64, 1:3], mx[0:64, 1:3], -1.0, None, ALU.mult).then_inc(S["s_max"], 1)
            v.wait_ge(S["s_exp"], 1)
            v.wait_ge(S["s_gate"], 1)
            done.link(v.reciprocal(rc[0:64, 1:3], sm[0:64, 1:3]))
            done.link(v.tensor_tensor(rc[0:64, 1:3], rc[0:64, 1:3], gate[0:64, 1:3], ALU.mult))
            v.tensor_scalar(probs, probs, rc[0:64, 1:2], None, ALU.mult)
            v.tensor_scalar(probw, probw, rc[0:64, 2:3], None, ALU.mult)
            done.link(v.tensor_scalar(prob_c[0:64, :], prob_c[0:64, :], gate[0:64, 0:1], None, ALU.mult))
            v.sem_inc(S["s_prob"], 1)
            v.wait_ge(S["s_pt_in"], 4)
            for b in range(NS_TOK):
                if b >= 2:
                    v.wait_ge(S["s_vst"], b - 1)
                v.tensor_tensor(pown[:, b % 2], pt[:, 0:20, :], s_("own_row", P)[:, 64 * b:64 * b + 64].unsqueeze(1).broadcast_to([P, 20, 64]),
                                ALU.mult).then_inc(S["s_pown"], 1)
            v.wait_ge(S["s_vst"], 8)
            half = s_("half")
            done.link(v.tensor_scalar(r64(osum), ps[0:64, 7, 0:DH], half[:, 0:1], None, ALU.mult))
            v.scalar_tensor_tensor(r64(osum), ps[0:64, 7, DH:2 * DH], half[:, 1:2], r64(osum), ALU.mult, ALU.add
                                   ).then_inc(S["s_half"], 1)

        @block.tensor
        def _(pe):
            id64 = ident[0:64, 0:64]
            pe.wait_ge(S["s_rot"], 1)
            for n, t in enumerate((nq, rq, rk, kv5)):
                pe.transpose(ps[:, 0, 64 * n:64 * n + 64], t[0:64, :], id64)
            pe.transpose(ps[:, 0, 256:288], kvw[0:32, :], ident[0:32, 0:32]).then_inc(S["s_tr"], 1)
            pe.wait_ge(S["s_tr_in"], 1)
            for b in range(NS_TOK):
                pe.wait_ge(S["s_st_new"], b + 1)
                for h in range(H):
                    n = 8 * b + h
                    last = pe.matmul(ps[:, 1, n:n + 1], s_new[b % 2][:, h, :], tr[:, 1, n:n + 1], start=True, stop=True)
                last.then_inc(S["s_st_o"], 1)
            pe.wait_ge(S["s_otr"], 1)
            pe.transpose(ps[0:64, 2, 0:DH], ot_r, ident).then_inc(S["s_or"], 1)
            for g in (0, 1):
                for kv in range(KV):
                    last = pe.transpose(ps[:, 4, kv * 256 + g * P:kv * 256 + (g + 1) * P], m.pooled[:, 0, g, kv * DH:(kv + 1) * DH], ident)
            last.then_inc(S["s_kct"], 1)
            pe.wait_ge(S["s_gated"], 1)
            pe.transpose(ps[:, 3, 0:64], osum[0:64, :], id64).then_inc(S["s_ft"], 1)
            pe.wait_ge(S["s_kct_in"], 1)
            pe.wait_ge(S["s_q"], 1)
            for dst, keys in ((slice(0, 256), [kct[:, kv, :] for kv in range(KV)]),
                              (slice(256, 264), [tr[:, 3, :].rearrange("p (s x) -> p x s", x=8)[:, 4 + kv, :] for kv in range(KV)]),
                              (slice(264, 272), [tr[:, 4, 0:32].rearrange("p (s x) -> p x s", x=4)[:, kv, :] for kv in range(KV)])):
                for kv in range(KV):
                    last = pe.matmul(ps[0:64, 5, dst], q_kv[:, kv, :], keys[kv], start=(kv == 0), stop=(kv == 1))
            last.then_inc(S["s_c"], 1)
            pe.wait_ge(S["s_cprob"], 1)
            pe.matmul(ps[0:16, 6, 0:256], s_("to_kv")[0:64, :], prob_c[0:64, :], start=True, stop=True).then_inc(S["s_imp"], 1)
            pe.wait_ge(S["s_rank"], 1)
            pe.matmul(ps[0:64, 6, 256:256 + NBLK + 1], s_("from_kv", 16), selrow[0:16, :], start=True, stop=True).then_inc(S["s_selb"], 1)
            pe.wait_ge(S["s_ftin"], 1)
            for b in range(NS_TOK):
                u, i = b % 4, b // 4
                pe.wait_ge(S["s_qst"], b + 1)
                pe.wait_ge(k_full[u], 16 * NPAGE * (i + 1))
                pe.wait_ge(S["s_wfull"], 16 * (i + 1))
                for kv in range(KV):
                    for c in range(4):
                        keys = pages[u][:, 4 * c:4 * c + 4, kv * P:(kv + 1) * P]
                        pe.matmul(ps[0:64, c, :], q_st[:, u, kv, :], keys, start=(b == 0 and kv == 0), stop=(b == 7 and kv == 1))
                    last = pe.matmul(ps[0:64, 4, :], q_st[:, u, kv, :], windows[:, u, kv * WIN:(kv + 1) * WIN],
                                     start=(b == 0 and kv == 0), stop=(b == 7 and kv == 1))
                last.then_inc(S["s_kdone"], 1)
            pe.wait_ge(S["s_prob"], 1)
            for n in range(23):
                if n < 16:
                    src = probs[:, n * P:(n + 1) * P]
                elif n < 20:
                    src = probw[:, 8 + (n - 16) * P:8 + (n - 15) * P]
                elif n < 22:
                    src = prob_c[0:64, (n - 20) * P:(n - 19) * P]
                else:
                    src = new_cols
                rows = 16 if n == 22 else P
                last = pe.transpose(ps[0:rows, n // 8, (n % 8) * 64:(n % 8) * 64 + 64], src, id64)
            last.then_inc(S["s_pt"], 1)
            pe.wait_ge(S["s_pt_in"], 4)
            for g in (0, 1):
                pe.matmul(ps[0:64, 7, 0:256], pt[:, 20 + g, :], m.pooled[:, 1, g, :], start=(g == 0), stop=False)
            pe.matmul(ps[0:64, 7, 0:256], pt[0:16, 22, :], v_new[0:16, :], start=False, stop=False)
            for b in range(NS_TOK):
                u, i = b % 4, b // 4
                pe.wait_ge(S["s_pown"], b + 1)
                pe.wait_ge(v_full[u], 16 * NPAGE * (i + 1))
                pe.wait_ge(S["s_wfull"], 32 + 64 * (i + 1))
                for n in range(20):
                    vals = pages[u][:, n, :] if n < 16 else windows[:, u, (n - 16) * 256:(n - 15) * 256]
                    last = pe.matmul(ps[0:64, 7, 0:256], pown[:, b % 2, n, :], vals, start=False, stop=(b == 7 and n == 19))
                last.then_inc(S["s_vst"], 1)
            pe.wait_ge(S["s_half"], 1)
            pe.transpose(ps[:, 3, 0:64], osum[0:64, :], id64).then_inc(S["s_ot"], 1)


def phase_c(nc, a, o, m, sem):
    arena, ps, xt = m.arena, m.ps, m.xt
    _, _, (cr, CR) = constants()
    ring = view(arena, RING, 8, 4, CHUNK)
    hw = Taker(arena, PROJ, XT0)
    h = hw(3, D)
    ln = hw(2, D)
    w_r = hw(KT, NG + NE)
    wk = Taker(arena, WORK, KVC)
    x = wk(3, D)
    ht = xt
    m.cr = view(arena, CONST, cr.shape[1])
    r_ = lambda n, r=P: m.cr[0:r, CR[n][0]:CR[n][0] + CR[n][1]]
    sm = Taker(arena, 16384, RING + 20480)
    stats, agg, rstd = sm(3, 4, 6), sm(3, 2), sm(3)
    bias, lg = sm(NG + NE), sm(3, NG + NE)
    gm, gs, tm, goh, pg = sm(3), sm(3), sm(3), sm(3, NG), sm(3, NG)
    el, sel, c8 = sm(3, NG, EPG), sm(3, EPG), sm(3, EPG)
    em, es, m1, m2 = sm(3), sm(3), sm(3), sm(3)
    oh = [sm(3, EPG), sm(3, EPG)]
    e12 = [sm(3, NG, EPG), sm(3, NG, EPG)]
    both, sums = sm(3, NE), sm(2, NE)
    nb_t, nb_w, base, endb, posb = sm(1), sm(P), sm(NE), sm(NE), sm(3, NE)
    cnt_t, nb_rep, slots, ge = sm(1), sm(NE), sm(2, 3), sm(MAXB, NE)
    btab_f = sm(MAXB + 1)
    zero_i = sm(MAXB).bitcast(I32)
    tok_id = sm(3).bitcast(I32)
    names = (
        "c_in c_x c_free c_acc c_mv c_std c_h c_hst c_ht c_hti c_lg c_gx c_exp c_e c_cum c_nb c_bs "
        "c_pos c_zero c_zst c_scat c_slot c_tmp c_sub ")
    S = {n: sem(n) for n in names.split()}
    w_full = [sem(f"c_wfull{j}") for j in range(8)]
    w_o = a["w_o"].rearrange("(k p) n -> p k n", p=P)

    with nc.Block() as block:
        @block.sync
        def _(sp):
            for i in range(2):
                for j in range(8):
                    if i:
                        sp.wait_ge(S["c_free"], j + 1)
                    cols = i * 1024 + (j // 4) * 512
                    sp.dma_start(ring[:, j], w_o[:, (j % 4) * 4:(j % 4) * 4 + 4, cols:cols + CHUNK]).then_inc(w_full[j], 16)
            sp.wait_ge(S["c_h"], 3)
            for t, (t0, n) in enumerate(TOK):
                sp.dma_start(m.h_d[t0:t0 + n, :], h[0:n, t, :]).then_inc(S["c_hst"], 16)
            sp.wait_ge(S["c_hst"], 48)

        @block.gpsimd
        def _(pool):
            pool.dma_start(tok_id, a["tok_id"]).then_inc(S["c_tmp"], 16)
            pool.memset(zero_i, 0).then_inc(S["c_zero"], 1)
            pool.wait_ge(S["c_zero"], 1)
            pool.dma_start(m.slot_d.rearrange("(s b) o -> s (b o)", s=BS), zero_i[0:BS, :]).then_inc(S["c_zst"], 16)
            pool.wait_ge(S["c_zst"], 16)
            pool.wait_ge(S["c_tmp"], 16)
            pool.wait_ge(S["c_pos"], 1)
            for k in (0, 1):
                for t, (_, n) in enumerate(TOK):
                    pool.indirect_dma_start(out=m.slot_d, out_offset=bass.IndirectOffsetOnAxis(ap=m.pos[0:n, k, t:t + 1], axis=0),
                                            in_=tok_id[0:n, t:t + 1], in_offset=None).then_inc(S["c_scat"], 16)
            pool.wait_ge(S["c_scat"], 96)
            pool.dma_start(m.slot_tok[0:BS, :], m.slot_d.rearrange("(b s) o -> s (b o)", s=BS),
                           allow_slow_non_contiguous=True).then_inc(S["c_slot"], 16)
            pool.wait_ge(S["c_slot"], 16)

        @block.scalar
        def _(act):
            A = nc.scalar
            xr = a["x"]
            for t, (t0, n) in enumerate(TOK):
                act.dma_start(x[0:n, t, :], xr[t0:t0 + n, :]).then_inc(S["c_x"], 16)
            act.dma_start(m.cr, a["const_r"]).then_inc(S["c_in"], 16)
            act.dma_start(w_r, a["w_r"].rearrange("p (k n) -> p k n", k=KT)).then_inc(S["c_in"], 16)
            act.dma_start(bias, a["b_r"].broadcast_to([P, NG + NE])).then_inc(S["c_in"], 16)
            act.dma_start(ln[:, 0, :], a["ln1_g"].broadcast_to([P, D])).then_inc(S["c_in"], 16)
            act.dma_start(ln[:, 1, :], a["ln1_b"].broadcast_to([P, D])).then_inc(S["c_in"], 16)
            act.wait_ge(S["c_in"], 80)
            for t, (_, n) in enumerate(TOK):
                act.wait_ge(S["c_mv"], t + 1)
                A.activation(rstd[0:n, t:t + 1], agg[0:n, t, 1:2], ACT.Sqrt, bias=r_("eps", n)).then_inc(S["c_std"], 1)
            for k in range(KT):
                act.wait_ge(S["c_ht"], k + 1)
                A.copy(ht[:, k, :], ps[:, k % 2, 0:T]).then_inc(S["c_hti"], 1)
            act.wait_ge(S["c_gx"], 1)
            A.activation(pg, pg, ACT.Exp).then_inc(S["c_exp"], 1)
            act.wait_ge(S["c_sub"], 1)
            A.activation(sel, sel, ACT.Exp).then_inc(S["c_exp"], 1)

        @block.vector
        def _(v):
            done = m.dve
            v.wait_ge(S["c_x"], 48)
            for n4 in range(4):
                v.wait_ge(S["c_free"], 4 * (n4 + 1))
                for t, (_, n) in enumerate(TOK):
                    cols = slice(n4 * CHUNK, (n4 + 1) * CHUNK)
                    last = v.scalar_tensor_tensor(h[0:n, t, cols], x[0:n, t, cols], ALPHA, ps[0:n, 3 * (n4 % 2) + t, :], ALU.mult, ALU.add)
                last.then_inc(S["c_acc"], 1)
                v.wait_ge(S["c_acc"], n4 + 1)
                for t, (_, n) in enumerate(TOK):
                    last = v.bn_stats(stats[0:n, t, n4, :], h[0:n, t, cols])
            done.link(last)
            v.wait_ge(S["c_in"], 80)
            for t, (_, n) in enumerate(TOK):
                v.bn_aggr(agg[0:n, t, :], stats[0:n, t].rearrange("p a b -> p (a b)")).then_inc(S["c_mv"], 1)
            for t, (_, n) in enumerate(TOK):
                v.wait_ge(S["c_std"], t + 1)
                done.link(v.reciprocal(rstd[0:n, t:t + 1], rstd[0:n, t:t + 1]))
                done.link(v.tensor_scalar(h[0:n, t], h[0:n, t], agg[0:n, t, 0:1], rstd[0:n, t:t + 1], ALU.subtract, ALU.mult))
                done.link(v.tensor_tensor(h[0:n, t], h[0:n, t], ln[0:n, 0], ALU.mult))
                v.tensor_tensor(h[0:n, t], h[0:n, t], ln[0:n, 1], ALU.add).then_inc(S["c_h"], 1)
            done.link(v.memset(lg, 0.0))
            v.wait_ge(S["c_lg"], 1)
            for t, (_, n) in enumerate(TOK):
                last = v.tensor_tensor(lg[0:n, t], ps[0:n, 2 + t, 0:NG + NE], bias[0:n, :], ALU.add)
            done.link(last)
            gl = lg[:, :, 0:NG]
            b3 = lambda t, n: t.unsqueeze(2).broadcast_to([P, 3, n])

            def first_max(out, vals, top, desc, n):
                done.link(v.tensor_reduce(top, vals, AX_X, ALU.max))
                done.link(v.tensor_tensor(out, vals, b3(top, n), ALU.is_equal))
                done.link(v.tensor_tensor(out, out, desc.unsqueeze(1).broadcast_to([P, 3, n]), ALU.mult))
                done.link(v.tensor_reduce(tm, out, AX_X, ALU.max))
                done.link(v.tensor_tensor(out, out, b3(tm, n), ALU.is_equal))

            first_max(goh, gl, gm, r_("desc4"), NG)
            v.tensor_tensor(pg, gl, b3(gm, NG), ALU.subtract).then_inc(S["c_gx"], 1)
            e4 = lg[:, :, NG:].rearrange("p t (g e) -> p t g e", g=NG)
            for t in range(3):
                last = v.tensor_tensor(el[:, t], e4[:, t], goh[:, t].unsqueeze(2).broadcast_to([P, NG, EPG]), ALU.mult)
            done.link(last)
            for t in range(3):
                last = v.tensor_reduce(sel[:, t], el[:, t].rearrange("p g e -> p e g"), AX_X, ALU.add)
            done.link(last)
            done.link(v.tensor_reduce(em, sel, AX_X, ALU.max))
            v.tensor_tensor(sel, sel, b3(em, EPG), ALU.subtract).then_inc(S["c_sub"], 1)
            v.wait_ge(S["c_exp"], 2)
            v.tensor_reduce(gs, pg, AX_X, ALU.add)
            done.link(v.tensor_reduce(es, sel, AX_X, ALU.add))
            v.reciprocal(gs, gs)
            done.link(v.reciprocal(es, es))
            done.link(v.tensor_tensor(sel, sel, b3(es, EPG), ALU.mult))
            first_max(oh[0], sel, m1, r_("desc8"), EPG)
            done.link(v.scalar_tensor_tensor(sel, oh[0], -2.0, sel, ALU.mult, ALU.add))
            first_max(oh[1], sel, m2, r_("desc8"), EPG)
            done.link(v.tensor_tensor(es, m1, m2, ALU.add))
            done.link(v.reciprocal(es, es))
            done.link(v.tensor_tensor(es, es, gs, ALU.mult))
            v.tensor_tensor(m.gate_w[:, 0], m1, es, ALU.mult)
            v.tensor_tensor(m.gate_w[:, 1], m2, es, ALU.mult)
            done.link(v.tensor_tensor(goh, goh, b3(r_("valid"), NG), ALU.mult))
            for k in (0, 1):
                for t in range(3):
                    last = v.tensor_tensor(e12[k][:, t], goh[:, t].unsqueeze(2).broadcast_to([P, NG, EPG]),
                                           oh[k][:, t].unsqueeze(1).broadcast_to([P, NG, EPG]), ALU.mult)
            done.link(last)
            flat = lambda t: t.rearrange("p t g e -> p t (g e)")
            done.link(v.tensor_tensor(both, flat(e12[0]), flat(e12[1]), ALU.add))
            done.link(v.tensor_tensor(sums[:, 0], both[:, 0], both[:, 1], ALU.add))
            v.tensor_tensor(sums[:, 1], sums[:, 0], both[:, 2], ALU.add).then_inc(S["c_e"], 1)
            v.wait_ge(S["c_cum"], 1)
            for cnt, dst in ((ps[0:NE, 6, 0:1], nb_t[0:NE, :]), (ps[:, 6, 32:64], nb_rep)):
                done.link(v.tensor_scalar(dst, cnt, 0.0, None, ALU.is_gt))
                for n in range(1, (T + BS - 1) // BS):
                    done.link(v.scalar_tensor_tensor(dst, cnt, float(n * BS), dst, ALU.is_gt, ALU.add))
            v.tensor_copy(nb_w[0:NE, :], nb_t[0:NE, :].broadcast_to([NE, P])).then_inc(S["c_nb"], 1)
            v.wait_ge(S["c_bs"], 1)
            done.link(v.tensor_copy(base, ps[:, 6, 64:96]))
            done.link(v.tensor_tensor(endb, base, nb_rep, ALU.add))
            for t in range(3):
                last = v.scalar_tensor_tensor(posb[:, t], base, float(BS), ps[:, 5, 32 * t:32 * t + 32], ALU.mult, ALU.add)
            done.link(last)
            for k in (0, 1):
                done.link(v.tensor_tensor(both, flat(e12[k]), posb, ALU.mult))
                done.link(v.tensor_reduce(slots[:, k], both, AX_X, ALU.add))
            v.tensor_copy(m.pos, slots).then_inc(S["c_pos"], 1)
            done.link(v.tensor_tensor(ge[0:1], endb[0:1].unsqueeze(1).broadcast_to([1, MAXB, NE]),
                                      r_("blocks", 1).unsqueeze(2).broadcast_to([1, MAXB, NE]), ALU.is_le))
            done.link(v.tensor_reduce(btab_f[0:1, 0:MAXB], ge[0:1], AX_X, ALU.add))
            done.link(v.tensor_scalar(btab_f[0:1, 0:MAXB], btab_f[0:1, 0:MAXB], float(NE - 1), None, ALU.min))
            done.link(v.tensor_copy(btab_f[0:1, MAXB:MAXB + 1], endb[0:1, NE - 1:NE]))
            done.link(v.tensor_copy(m.btab[0:1, :], btab_f[0:1, :]))

        @block.tensor
        def _(pe):
            for n4 in range(4):
                if n4 >= 2:
                    pe.wait_ge(S["c_acc"], n4 - 1)
                for q in range(4):
                    j = 4 * (n4 % 2) + q
                    pe.wait_ge(w_full[j], 16 * (n4 // 2 + 1))
                    for kk in range(4):
                        k = 4 * q + kk
                        for t, (t0, n) in enumerate(TOK):
                            last = pe.matmul(ps[0:n, 3 * (n4 % 2) + t, :], xt[:, k, t0:t0 + n], ring[:, j, kk, :],
                                             start=(k == 0), stop=(k == KT - 1))
                    last.then_inc(S["c_free"], 1)
            pe.wait_ge(S["c_in"], 80)
            ident = r_("ident")
            pe.wait_ge(S["c_h"], 3)
            for k in range(KT):
                if k >= 2:
                    pe.wait_ge(S["c_hti"], k - 1)
                for t, (t0, n) in enumerate(TOK):
                    last = pe.transpose(ps[:, k % 2, t0:t0 + n], h[0:n, t, k * P:(k + 1) * P], ident[0:n, 0:n])
                last.then_inc(S["c_ht"], 1)
            pe.wait_ge(S["c_hti"], KT)
            for t, (t0, n) in enumerate(TOK):
                for k in range(KT):
                    last = pe.matmul(ps[0:n, 2 + t, 0:NG + NE], ht[:, k, t0:t0 + n], w_r[:, k, :], start=(k == 0), stop=(k == KT - 1))
            last.then_inc(S["c_lg"], 1)
            pe.wait_ge(S["c_e"], 1)
            for t in range(3):
                pe.matmul(ps[:, 5, 32 * t:32 * t + 32], r_("before"), both[:, t], start=True, stop=(t == 0))
                if t:
                    pe.matmul(ps[:, 5, 32 * t:32 * t + 32], r_("ones"), both[:, 0] if t == 1 else sums[:, 0], start=False, stop=True)
            pe.matmul(ps[0:NE, 6, 0:1], sums[:, 1], r_("ones")[:, 0:1], start=True, stop=True)
            pe.matmul(ps[:, 6, 32:64], r_("ones"), sums[:, 1], start=True, stop=True).then_inc(S["c_cum"], 1)
            pe.wait_ge(S["c_nb"], 1)
            pe.matmul(ps[:, 6, 64:96], nb_w[0:NE, :], r_("lt32", NE), start=True, stop=True).then_inc(S["c_bs"], 1)


def phase_d(nc, a, o, m, sem):
    arena, ps = m.arena, m.ps
    ident = m.cr[:, 0:P]
    w = Taker(arena, 0, CONST)
    slots = w(12, 4 * CHUNK)
    xg = w(D)
    xgt = w(KT, BS)
    act_g, hb = w(DE), w(DE)
    hbt = w(DE // P, BS)
    y = w(D)
    tick, blank = w(1), w(512)
    fin = Taker(arena, 0, CONST)
    h, y1, y2, ln = fin(3, D), fin(3, D), fin(3, D), fin(2, D)
    stats, agg, rstd = fin(3, 4, 6), fin(3, 2), fin(3)
    names = (
        "d_free d_yfree d_seen d_xg d_xgt0 d_xgt1 d_xgi d_silu d_hb d_hbt d_hbi d_y d_yst f_in f_g0 f_g1 f_mv "
        "f_std f_o f_st d_xgfree ")
    S = {n: sem(n) for n in names.split()}
    full = [sem(f"d_full{j}") for j in range(12)]
    wg = a["w_gate"].rearrange("e (k p) f -> e p k f", p=P)
    wu = a["w_up"].rearrange("e (k p) f -> e p k f", p=P)
    wd = a["w_down"].rearrange("e (k p) f -> e p k f", p=P)

    with nc.Block() as block:
        def filled(eng):
            return eng.value_load(m.btab[0:1, MAXB:MAXB + 1], min_val=0, max_val=MAXB - 1)

        @block.sync
        def _(sp):
            n_blocks = filled(sp)
            with sp.Fori(0, MAXB) as b:
                with sp.If(b < n_blocks):
                    e = sp.value_load(m.btab[0:1, bass.ds(b, 1)], min_val=0, max_val=NE - 1)
                    for q in range(4):
                        for j, src in ((q, wg), (4 + q, wu)):
                            sp.wait_ge(S["d_free"], b * 12 + (2 * q + j // 4 + 1))
                            sp.dma_start(slots[:, j].rearrange("p (k f) -> p k f", k=4), src[e, :, 4 * q:4 * q + 4, :]).then_inc(full[j], 16)
                    for q in range(4):
                        sp.wait_ge(S["d_free"], b * 12 + (9 + q))
                        sp.dma_start(slots[:, 8 + q], wd[e, :, q, :]).then_inc(full[8 + q], 16)

        @block.gpsimd
        def _(pool):
            n_blocks = filled(pool)

            def fetch():
                pool.indirect_dma_start(out=xg[0:BS, :], out_offset=None, in_=m.h_d,
                                        in_offset=bass.IndirectOffsetOnAxis(ap=m.cur_tok[0:BS, :], axis=0)).then_inc(S["d_xg"], 16)

            pool.tensor_copy(m.cur_tok[0:BS, :], m.slot_tok[0:BS, 0:1]).then_inc(S["d_xgfree"], 1)
            pool.wait_ge(S["d_xgfree"], 1)
            fetch()
            with pool.Fori(0, MAXB - 1) as b:
                with pool.If(b < n_blocks):
                    pool.wait_ge(S["d_xgt1"], b + 1)
                    pool.tensor_copy(m.cur_tok[0:BS, :], m.slot_tok[0:BS, bass.ds(b + 1, 1)]).then_inc(S["d_xgfree"], 1)
                    pool.wait_ge(S["d_xgfree"], b + 2)
                    pool.sem_inc(S["d_seen"], 1)
                    fetch()

        @block.scalar
        def _(act):
            A = nc.scalar
            n_blocks = filled(act)
            act.wait_ge(S["d_yfree"], 1)
            with act.Fori(0, MAXB) as b:
                with act.If(b < n_blocks):
                    act.wait_ge(S["d_xgt0"], b + 1)
                    A.copy(xgt[:, 0:8, :].rearrange("p k s -> p (k s)"), ps[:, 2, :]).then_inc(S["d_xgi"], 1)
                    act.wait_ge(S["d_free"], b * 12 + 19)
                    A.activation(act_g[0:BS, :], ps[0:BS, 0, :], ACT.Silu).then_inc(S["d_silu"], 1)
                    act.wait_ge(S["d_free"], b * 12 + 24)
                    A.copy(y[0:BS, 0:1024].rearrange("p (a b) -> p a b", a=2), ps[0:BS, 4:6, :]).then_inc(S["d_y"], 1)
                    act.wait_ge(S["d_y"], b * 2 + 4)
                    act.dma_start(m.y_d[bass.ds(b * BS, BS), :], y[0:BS, :]).then_inc(S["d_yst"], 16)
                    act.wait_ge(S["d_yst"], b * 16 + 16)
                    A.copy(tick[0:1, :], tick[0:1, :]).then_inc(S["d_yfree"], 1)
                with act.Else():
                    act.dma_start(m.y_d[bass.ds(b * BS, BS), :].rearrange("p (a b) -> p a b", a=4),
                                  blank[0:BS].unsqueeze(1).broadcast_to([BS, 4, 512])).then_inc(S["d_yst"], 16)
            act.wait_ge(S["d_yst"], 16 * MAXB)

        @block.vector
        def _(v):
            n_blocks = filled(v)
            v.memset(blank, 0.0)
            v.memset(tick, 0.0).then_inc(S["d_yfree"], 1)
            with v.Fori(0, MAXB) as b:
                with v.If(b < n_blocks):
                    v.wait_ge(S["d_xgt1"], b + 1)
                    v.tensor_copy(xgt[:, 8:16, :].rearrange("p k s -> p (k s)"), ps[:, 3, :]).then_inc(S["d_xgi"], 1)
                    v.wait_ge(S["d_silu"], b + 1)
                    v.wait_ge(S["d_free"], b * 12 + 20)
                    v.tensor_tensor(hb[0:BS, :], act_g[0:BS, :], ps[0:BS, 1, :], ALU.mult).then_inc(S["d_hb"], 1)
                    v.wait_ge(S["d_hbt"], b + 1)
                    v.tensor_copy(hbt.rearrange("p k s -> p (k s)"), ps[:, 0, 0:256]).then_inc(S["d_hbi"], 1)
                    v.wait_ge(S["d_free"], b * 12 + 24)
                    v.wait_ge(S["d_yfree"], b + 1)
                    v.tensor_copy(y[0:BS, 1024:2048].rearrange("p (a b) -> p a b", a=2), ps[0:BS, 6:8, :]).then_inc(S["d_y"], 1)
        @block.tensor
        def _(pe):
            n_blocks = filled(pe)
            pe.sem_inc(S["d_free"], 12)
            pe.sem_inc(S["d_y"], 2)
            id64 = ident[0:BS, 0:BS]
            with pe.Fori(0, MAXB) as b:
                with pe.If(b < n_blocks):
                    pe.wait_ge(S["d_xg"], b * 16 + 16)
                    pe.sem_inc(S["d_seen"], 1)
                    for k in range(KT):
                        last = pe.transpose(ps[:, 2 + k // 8, (k % 8) * BS:(k % 8 + 1) * BS], xg[0:BS, k * P:(k + 1) * P], id64)
                        if k == 7:
                            last.then_inc(S["d_xgt0"], 1)
                    last.then_inc(S["d_xgt1"], 1)
                    pe.wait_ge(S["d_xgi"], b * 2 + 2)
                    for q in range(4):
                        for j in (q, 4 + q):
                            pe.wait_ge(full[j], b * 16 + 16)
                            for kk in range(4):
                                k = 4 * q + kk
                                last = pe.matmul(ps[0:BS, j // 4, :], xgt[:, k, :], slots[:, j, kk * CHUNK:(kk + 1) * CHUNK],
                                                 start=(k == 0), stop=(k == KT - 1))
                            last.then_inc(S["d_free"], 1)
                    pe.wait_ge(S["d_hb"], b + 1)
                    pe.sem_inc(S["d_seen"], 1)
                    for f in range(4):
                        last = pe.transpose(ps[:, 0, f * BS:(f + 1) * BS], hb[0:BS, f * P:(f + 1) * P], id64)
                    last.then_inc(S["d_hbt"], 1)
                    pe.wait_ge(S["d_hbi"], b + 1)
                    pe.wait_ge(S["d_y"], b * 2 + 2)
                    for f in range(4):
                        pe.wait_ge(full[8 + f], b * 16 + 16)
                        for n in range(4):
                            last = pe.matmul(ps[0:BS, 4 + n, :], hbt[:, f, :], slots[:, 8 + f, n * CHUNK:(n + 1) * CHUNK],
                                             start=(f == 0), stop=(f == 3))
                        last.then_inc(S["d_free"], 1)

    with nc.Block() as block:
        @block.gpsimd
        def _(pool):
            for k, dst in enumerate((y1, y2)):
                for t, (_, n) in enumerate(TOK):
                    pool.indirect_dma_start(out=dst[0:n, t, :], out_offset=None, in_=m.y_d,
                                            in_offset=bass.IndirectOffsetOnAxis(ap=m.pos[0:n, k, t:t + 1], axis=0)).then_inc(S[f"f_g{k}"], 16)

        @block.vector
        def _(v):
            done = m.dve
            v.wait_ge(S["f_in"], 80)
            v.wait_ge(S["f_g0"], 48)
            v.wait_ge(S["f_g1"], 48)
            for t, (_, n) in enumerate(TOK):
                done.link(v.tensor_scalar(h[0:n, t], h[0:n, t], ALPHA, None, ALU.mult))
                for k, yk in enumerate((y1, y2)):
                    done.link(v.scalar_tensor_tensor(h[0:n, t], yk[0:n, t], m.gate_w[0:n, k, t:t + 1], h[0:n, t], ALU.mult, ALU.add))
                for c in range(4):
                    last = v.bn_stats(stats[0:n, t, c, :], h[0:n, t, c * CHUNK:(c + 1) * CHUNK])
                done.link(last)
                v.bn_aggr(agg[0:n, t, :], stats[0:n, t].rearrange("p a b -> p (a b)")).then_inc(S["f_mv"], 1)
            for t, (_, n) in enumerate(TOK):
                v.wait_ge(S["f_std"], t + 1)
                done.link(v.reciprocal(rstd[0:n, t:t + 1], rstd[0:n, t:t + 1]))
                done.link(v.tensor_scalar(h[0:n, t], h[0:n, t], agg[0:n, t, 0:1], rstd[0:n, t:t + 1], ALU.subtract, ALU.mult))
                done.link(v.tensor_tensor(h[0:n, t], h[0:n, t], ln[0:n, 0], ALU.mult))
                v.tensor_tensor(h[0:n, t], h[0:n, t], ln[0:n, 1], ALU.add).then_inc(S["f_o"], 1)

        @block.scalar
        def _(act):
            for n, src in enumerate((a["ln2_g"], a["ln2_b"])):
                act.dma_start(ln[:, n, :], src.broadcast_to([P, D])).then_inc(S["f_in"], 16)
            for t, (t0, n) in enumerate(TOK):
                act.dma_start(h[0:n, t, :], m.h_d[t0:t0 + n, :]).then_inc(S["f_in"], 16)
            for t, (_, n) in enumerate(TOK):
                act.wait_ge(S["f_mv"], t + 1)
                nc.scalar.activation(rstd[0:n, t:t + 1], agg[0:n, t, 1:2], ACT.Sqrt, bias=m.cr[0:n, P:P + 1]).then_inc(S["f_std"], 1)
            for t, (t0, n) in enumerate(TOK):
                act.wait_ge(S["f_o"], t + 1)
                dst = o["y_s"].rearrange("a b d -> (a b) d") if t == 2 else o["y_p"][0, t0:t0 + n, :]
                act.dma_start(dst, h[0:n, t, :]).then_inc(S["f_st"], 16)
            act.wait_ge(S["f_st"], 48)


def trunk(nc, a, o, upto=9):
    with ExitStack() as ctx:
        m = Memory()
        m.arena = ctx.enter_context(nc.sbuf_tensor("arena", [P, END + 160], F32))
        m.ps = ctx.enter_context(nc.psum_tensor("ps", [P, 8, 512], F32))

        def sem(name):
            return ctx.enter_context(nc.semaphore(name))

        def dram(name, shape, dt=F32):
            return nc.dram_tensor(name, shape, dt).ap()

        m.proj = view(m.arena, PROJ, 2, IN_W)
        m.xt = view(m.arena, XT0, KT, T)
        m.pooled = view(m.arena, KVC, 2, 2, KV * DH)
        m.cst = view(m.arena, CONST, 2064)
        m.small = Taker(m.arena, MISC, END)
        m.wrep = m.small(2, DH)
        m.ps_a = dram("sample_proj", (6, NS_TOK, 1024))
        m.ps_w = dram("sample_proj_w", (NS_TOK, 512))
        m.ps_g = dram("sample_proj_g", (NS_TOK, NGL))
        m.page_tab = m.small(P).bitcast(I32)
        m.kv5_d = dram("sample_kv", (NS_TOK, 8, DH))
        m.kvw_d = dram("sample_kvw", (NS_TOK, 4, DH))
        m.h_d, m.y_d = dram("h_rows", (T, D)), dram("y_rows", (MAXB * BS, D))
        m.slot_d = dram("slot_token", (MAXB * BS, 1), I32)
        keep = Taker(m.arena, END, END + 160)
        m.slot_tok, m.btab, m.cur_tok = keep(MAXB).bitcast(I32), keep(MAXB + 1).bitcast(I32), keep(1).bitcast(I32)
        m.pos = keep(6).bitcast(I32).rearrange("p (k t) -> p k t", k=2)
        m.gate_w = keep(2, 3)
        m.dve_done, m.act_done = sem("dve_done"), sem("act_done")
        for n, phase in enumerate((phase_a, phase_b, phase_s, phase_c, phase_d)):
            if n < upto:
                own = []

                def take(name):
                    own.append(nc.alloc_semaphore(name=name))
                    return own[-1]

                phase(nc, a, o, m, take)
                if n < 4:
                    nc.clear_and_free_semaphores(own)
                    nc.all_engine_barrier()


_OUTS = [(1, 256, 2048), (8, 1, 2048)] + [(1, 1, 256, 2, 128)] * 4 + [(1, 1, 512, 2, 128)] * 2 + [(1, 1, 8, 128, 128)] + \
    [(1, 8, 1, 2, 128)] * 4 + [(1, 8, 512, 2, 128)] * 2 + [(1, 8, 8, 128, 128)]
_NAMES = ["y_p", "y_s", "p_ck", "p_cv", "p_sk", "p_sv", "p_wk", "p_wv", "p_ret",
          "s_ck", "s_cv", "s_sk", "s_sv", "s_wk", "s_wv", "s_ret"]


def host_layout(i):
    f = np.ascontiguousarray
    i = {k: np.asarray(v) for k, v in i.items()}
    (cp, _), (cs, _), (cr, _) = constants()
    x = np.concatenate([i["x_prompt"].reshape(NP_TOK, D), i["x_sample"].reshape(NS_TOK, D)], 0)
    tiles = lambda w: f(w.reshape(KT, P, -1).transpose(1, 0, 2).reshape(P, -1))
    p = np.arange(P)[:, None]
    q = np.arange(4)[None]
    half = np.tile(4 * (p % 2) + q, (1, 2)).astype(np.int32)
    return {
        "x": x, "tok_id": (np.arange(P)[:, None] + P * np.arange(3)[None]).astype(np.int32), "x_t": tiles(f(x.T)), "const_p": cp, "const_s": cs, "const_r": cr, "half_of": half,
        "page_table": i["page_table"],
        "w_in": i["w_in"][0], "w_gl": tiles(i["w_in"][0][:, GL:]),
        "w_cmp_k": i["w_cmp_k"][0], "w_cmp_v": i["w_cmp_v"][0],
        "cmp_k": i["cache_cmp_k"].reshape(-1, 16 * KV * DH), "cmp_v": i["cache_cmp_v"].reshape(-1, 16 * KV * DH),
        "sel_kt": f(i["cache_sel_k"][0].transpose(0, 3, 2, 1)), "sel_v": i["cache_sel_v"][0].reshape(-1, PAGE, KV * DH),
        "win_kt": f(i["cache_win_k"][0].transpose(0, 3, 2, 1)),
        "win_k": i["cache_win_k"][0].reshape(NS_TOK, WIN, KV * DH), "win_v": i["cache_win_v"][0].reshape(NS_TOK, WIN, KV * DH),
        "state": i["state_ret"][0], "gn_g": i["ret_gn_g"], "gn_rows": f(np.broadcast_to(i["ret_gn_g"].reshape(1, H, DH), (8, H, DH)).reshape(64, DH)),
        "w_o": i["w_o"][0], "ln1_g": i["ln1_g"], "ln1_b": i["ln1_b"], "ln2_g": i["ln2_g"], "ln2_b": i["ln2_b"],
        "w_r": tiles(np.concatenate([i["w_group"][0], i["w_expert"][0]], 1)),
        "b_r": np.concatenate([i["b_group"], i["b_expert"]], 1),
        "w_gate": i["w_gate"][0], "w_up": i["w_up"][0], "w_down": i["w_down"][0],
    }


def kernel(**inputs):
    import concourse.bacc as bacc
    from concourse.bass_utils import run_bass_kernel_spmd as run

    nc = bacc.Bacc("TRN2", target_bir_lowering=False, num_devices=1)
    arrays = host_layout(inputs)
    a = {k: nc.dram_tensor(f"in_{k}", v.shape, mybir.dt.from_np(v.dtype), kind="ExternalInput").ap()
         for k, v in arrays.items()}
    o = {n: nc.dram_tensor(f"out_{n}", s, F32, kind="ExternalOutput").ap() for n, s in zip(_NAMES, _OUTS)}
    trunk(nc, a, o)
    r = run(nc, [{f"in_{k}": v for k, v in arrays.items()}], core_ids=[0])
    return tuple(r.results[0][f"out_{n}"] for n in _NAMES)
```

```python
from contextlib import ExitStack

import numpy as np

import concourse.bass as bass
from concourse import mybir

F32 = mybir.dt.float32
I32 = mybir.dt.int32
ALU = mybir.AluOpType
F32R = mybir.dt.float32r
ACT = mybir.ActivationFunctionType
AX_X = mybir.AxisListType.X

P = 128
D = 2048
KT = D // P
NP_TOK, NS_TOK = 256, 8
T = NP_TOK + NS_TOK
TOK = ((0, 128), (128, 128), (256, 8))
DH = 128
H = 8
KV = 2
G = H // KV
IN_W = 6680
RQ, RK, RV, RG, NQ, CK, CV, SK, SV, WK, WV, GL = (
    0, 1024, 2048, 3072, 4096, 5120, 5376, 5632, 5888, 6144, 6400, 6656)
NGL = 24
CHUNK = 512
PAST, PAGE, CB = 2048, 128, 64
NPAGE = PAST // PAGE
NBLK = PAST // CB
WIN = 512
TOPK = 16
NG, EPG, NE, DE = 4, 8, 32, 512
BS = 64
MAXB = NE + (2 * T - NE) // BS + 1
SCALE = DH ** -0.5
ALPHA = 2.0 ** 0.25
NEG = -1e30
EPS = 1e-5
RET_SCALE = DH ** -0.5



def _rope_table(pos, rot, theta):
    inv = (np.float32(theta) ** (-np.arange(0, rot, 2, dtype=np.float32) / np.float32(rot))).astype(np.float32)
    ang = (np.asarray(pos, np.float32)[:, None] * inv).astype(np.float32).astype(np.float64)
    return np.cos(ang).astype(np.float32), np.sin(ang).astype(np.float32)


def _layout(parts):
    at, places = 0, {}
    for name, a in parts:
        places[name] = (at, a.shape[1])
        at += a.shape[1]
    table = np.zeros((P, at), np.float32)
    for name, a in parts:
        table[:a.shape[0], places[name][0]:places[name][0] + a.shape[1]] = a
    return table, places


def constants():
    p = np.arange(P)
    log_g = np.log1p(-np.exp2(-5.0 - np.arange(H, dtype=np.float64)))
    rel = p[None, :] - p[:, None]
    dmask = np.concatenate([np.where(rel >= 0, np.exp(np.maximum(rel, 0) * g), 0.0) for g in log_g], 1)
    causal = np.concatenate([np.where(np.arange(NP_TOK)[None] <= (p + P * t)[:, None], 0.0, NEG) for t in (0, 1)], 1)
    cmp_ok = np.concatenate([((np.arange(4)[None] + 1) * CB - 1 <= (p + P * t)[:, None]) for t in (0, 1)], 1)
    cr, sr = _rope_table(np.arange(NP_TOK), DH, 10000.0)
    cn, sn = _rope_table(np.arange(NP_TOK), DH // 4, 500000.0)
    two = lambda a: np.concatenate([a[:P], a[P:]], 1)
    blk4 = np.stack([[(pp + P * t) // CB == b for b in range(4)] for t in (0, 1) for pp in p]).reshape(2, P, 4)
    prompt = [
        ("ident", np.eye(P)), ("dmask", dmask), ("causal", causal),
        ("cmp_add", np.where(cmp_ok, 0.0, NEG)), ("cmp_ok", cmp_ok * 1.0),
        ("q_dec", np.exp((p + 1.0)[:, None] * log_g[None])), ("k_dec", np.exp((P - 1.0 - p)[:, None] * log_g[None])),
        ("c_dec", np.tile(np.exp(P * log_g)[None], (P, 1))),
        ("cos_r", two(cr)), ("sin_r", two(sr)), ("cos_n", two(cn)), ("sin_n", two(sn)),
        ("blk2", np.stack([p < CB, p >= CB], 1) * 1.0), ("blk4", np.concatenate([blk4[0], blk4[1]], 1) * 1.0),
        ("eps", np.full((P, 1), EPS)),
    ]
    router = [
        ("ident", np.eye(P)), ("eps", np.full((P, 1), EPS)),
        ("before", (p[:, None] < p[None]) * 1.0), ("ones", np.ones((P, P))),
        ("lt32", (p[:NE, None] < np.arange(NE)[None]) * 1.0),
        ("desc4", np.tile(4.0 - np.arange(4), (P, 1))), ("desc8", np.tile(8.0 - np.arange(8), (P, 1))),
        ("valid", np.stack([p >= 0, p >= 0, p < NS_TOK], 1) * 1.0),
        ("blocks", np.tile(np.arange(MAXB) * 1.0, (P, 1))),
    ]
    row = np.arange(64)
    seq, head = row // 8, row % 8
    c1, s1 = _rope_table(np.array([PAST]), DH, 10000.0)
    c2, s2 = _rope_table(np.array([PAST]), DH // 4, 500000.0)
    is_k = np.isin(head, (0, 1, 4, 5))[:, None]
    is_w = (np.arange(32) % 4 < 2)[:, None]
    eye8 = (seq[:, None] == np.arange(8)[None]) * 1.0
    b33 = np.arange(NBLK + 1)
    sample = [
        ("cos_r", np.tile(c1, (64, 1))), ("sin_r", np.tile(s1, (64, 1))),
        ("cos_n", np.tile(c2, (64, 1))), ("sin_n", np.tile(s2, (64, 1))),
        ("cos_k", np.where(is_k, c2, 1.0)), ("sin_k", np.where(is_k, s2, 0.0)),
        ("cos_w", np.where(is_w, c2, 1.0)), ("sin_w", np.where(is_w, s2, 0.0)),
        ("own", eye8), ("own_add", (eye8 - 1.0) * -NEG),
        ("to_kv", ((seq * 2 + head // G)[:, None] == np.arange(16)[None]) * 1.0),
        ("from_kv", ((seq * 2 + head // G)[None] == np.arange(16)[:, None]) * 1.0),
        ("half", np.stack([head < G, head >= G], 1) * 1.0),
        ("own_row", np.tile(eye8.T.reshape(1, 512), (P, 1))),
        ("gamma", np.tile(np.exp(log_g)[None], (P, 1))),
        ("earlier", np.tile((b33[None] < b33[:, None]).reshape(1, -1) * 1.0, (16, 1))),
    ]
    return _layout(prompt), _layout(sample), _layout(router)


class Counter:

    def __init__(self, eng, sem):
        self.eng, self.sem, self.base, self.k, self.i, self.per = eng, sem, 0, 0, None, 0

    def enter(self, i, per):
        self.base, self.k, self.i, self.per = self.base + self.k, 0, i, per

    def leave(self, turns):
        assert self.k == self.per, (self.k, self.per)
        self.base, self.k, self.i = self.base + self.per * turns, 0, None

    def value(self):
        return self.base + self.k if self.i is None else self.i * self.per + (self.base + self.k)

    def link(self, ins):
        ins.then_inc(self.sem, 1)
        self.k += 1
        self.eng.wait_ge(self.sem, self.value())


class Memory:
    pass


def view(base, first, *dims):
    v = base[:, first:first + int(np.prod(dims))]
    if len(dims) == 1:
        return v
    names = "abcd"[:len(dims)]
    return v.rearrange(f"p ({' '.join(names)}) -> p {' '.join(names)}", **dict(zip(names, dims)))


class Taker:

    def __init__(self, base, first, end):
        self.base, self.at, self.end = base, first, end

    def __call__(self, *dims):
        v = view(self.base, self.at, *dims)
        self.at += int(np.prod(dims))
        assert self.at <= self.end, (self.at, self.end)
        return v


def rope(v, done, x, cos, sin, scratch):
    half = cos.shape[-1]
    lo, hi = x[..., 0:half], x[..., half:2 * half]
    ct, st = cos.broadcast_to(list(lo.shape)), sin.broadcast_to(list(lo.shape))
    v.tensor_tensor(scratch[0], lo, ct, ALU.mult)
    v.tensor_tensor(scratch[1], hi, st, ALU.mult)
    v.tensor_tensor(scratch[2], hi, ct, ALU.mult)
    done.link(v.tensor_tensor(scratch[3], lo, st, ALU.mult))
    v.tensor_tensor(lo, scratch[0], scratch[1], ALU.subtract)
    done.link(v.tensor_tensor(hi, scratch[2], scratch[3], ALU.add))


RING, PROJ, XT0 = 0, 20480, 33840
WORK = XT0 + KT * T
KVC = WORK + 7168
CONST = KVC + 1024
MISC = CONST + 2064
END = 52040
KEEP = 700


def phase_a(nc, a, o, m, sem):
    arena, ps, proj, xt, cst = m.arena, m.ps, m.proj, m.xt, m.cst
    ring = view(arena, RING, 8, 4, CHUNK)
    work = Taker(arena, WORK, KVC)
    gath = work(16, KV * DH)
    wsl = work(16, DH)
    sst = work(2, CHUNK)
    w_gl = m.small(KT, NGL)
    page_of = m.small(2).bitcast(I32)
    half_of = m.small(8).bitcast(I32)
    gather_row = m.small(8).bitcast(I32)
    eighth = m.small(NS_TOK).bitcast(I32)

    loaded, consts_in = sem("loaded"), sem("consts_in")
    w_full = [sem(f"w_full{j}") for j in range(8)]
    w_free = sem("w_free")
    gl_ready = sem("gl_ready")
    acc_free = sem("acc_free")
    s_out = [sem("s_out0"), sem("s_out1")]
    rows_in, rows_ready = sem("rows_in"), sem("rows_ready")
    gathered, gath_free = sem("gathered"), sem("gath_free")
    wsl_in, wsl_free = sem("wsl_in"), sem("wsl_free")
    w_in = a["w_in"].rearrange("(k p) n -> p k n", p=P)

    with nc.Block() as block:
        @block.sync
        def _(sp):
            sp.dma_start(xt, a["x_t"].rearrange("p (k t) -> p k t", k=KT)).then_inc(loaded, 16)
            with sp.Fori(0, 6) as i:
                for j in range(8):
                    sp.wait_ge(w_free, i * 8 + (j + 1))
                    cols = i * 1024 + (j // 4) * 512
                    sp.dma_start(ring[:, j], w_in[:, (j % 4) * 4:(j % 4) * 4 + 4, bass.ds(cols, CHUNK)]
                                 ).then_inc(w_full[j], 16)
            for j in range(4):
                sp.wait_ge(w_free, 48 + j + 1)
                sp.dma_start(ring[:, j], w_in[:, j * 4:j * 4 + 4, 12 * CHUNK:13 * CHUNK]).then_inc(w_full[j], 16)

        @block.tensor
        def _(pe):
            pe.sem_inc(w_free, 8)
            pe.wait_ge(loaded, 16)

            def chunk(u, banks_free, full):
                pe.wait_ge(acc_free, banks_free)
                for j in range(4 * u, 4 * u + 4):
                    pe.wait_ge(w_full[j], full)
                    for kk in range(4):
                        k = 4 * (j - 4 * u) + kk
                        for t, (t0, n) in enumerate(TOK):
                            last = pe.matmul(ps[0:n, 3 * u + t, :], xt[:, k, t0:t0 + n], ring[:, j, kk, :],
                                             start=(k == 0), stop=(k == KT - 1))
                    last.then_inc(w_free, 1)

            with pe.Fori(0, 6) as i:
                for u in (0, 1):
                    chunk(u, i * 6 + 3 * (u + 1), i * 16 + 16)
            chunk(0, 39, 112)
            pe.wait_ge(acc_free, 42)
            pe.wait_ge(consts_in, 96)
            for t, (t0, n) in enumerate(TOK):
                for k in range(KT):
                    last = pe.matmul(ps[0:n, 3 + t, 0:NGL], xt[:, k, t0:t0 + n], w_gl[:, k, :],
                                     start=(k == 0), stop=(k == KT - 1))
            last.then_inc(gl_ready, 1)

        @block.scalar
        def _(act):
            act.sem_inc(acc_free, 6)
            act.dma_start(cst[:, 0:a["const_p"].shape[1]], a["const_p"]).then_inc(consts_in, 16)
            act.dma_start(w_gl, a["w_gl"].rearrange("p (k n) -> p k n", k=KT)).then_inc(consts_in, 16)
            for t in (0, 1):
                act.dma_start(m.wrep[t * CB:(t + 1) * CB, 0, :], a["w_cmp_k"]).then_inc(consts_in, 16)
                act.dma_start(m.wrep[t * CB:(t + 1) * CB, 1, :], a["w_cmp_v"]).then_inc(consts_in, 16)

            def read_out(u, ready, col, n, sample_to):
                if n == CHUNK:
                    act.wait_ge(w_free, ready * 4 + 8)
                else:
                    act.wait_ge(gl_ready, 1)
                for t in (0, 1):
                    nc.scalar.copy(proj[:, t, col], ps[:, 3 * u + t, 0:n]).then_inc(acc_free, 1)
                nc.scalar.copy(sst[0:NS_TOK, u, 0:n], ps[0:NS_TOK, 3 * u + 2, 0:n]).then_inc(acc_free, 1)
                act.wait_ge(acc_free, 6 + 3 * ready)
                act.dma_start(sample_to, sst[0:NS_TOK, u, 0:n]).then_inc(s_out[u], 16)

            with act.Fori(0, 6) as i:
                for u in (0, 1):
                    read_out(u, i * 2 + (u + 1), bass.ds(i * 1024 + u * 512, CHUNK), CHUNK,
                             m.ps_a[i, :, u * 512:(u + 1) * 512])
                for u in (0, 1):
                    act.wait_ge(s_out[u], i * 16 + 16)
            read_out(0, 13, slice(12 * CHUNK, 13 * CHUNK), CHUNK, m.ps_w)
            read_out(1, 14, slice(GL, IN_W), NGL, m.ps_g)
            for u in (0, 1):
                act.wait_ge(s_out[u], 112)

        @block.gpsimd
        def _(pool):
            for g in (0, 1):
                src = a["page_table"][4 * g:4 * g + 4, :].rearrange("s n -> (s n)").unsqueeze(1).unsqueeze(2)
                pool.dma_start(page_of[:, g:g + 1], src.broadcast_to([64, 2, 1])).then_inc(rows_in, 16)
            pool.dma_start(half_of[:, 0:8], a["half_of"]).then_inc(rows_in, 16)
            for s in range(NS_TOK):
                pool.dma_start(m.seq_row[:, s:s + 1], a["page_table"][s].unsqueeze(1).unsqueeze(2).broadcast_to([NPAGE, 8, 1])
                               ).then_inc(rows_in, 16)
            pool.dma_start(eighth, a["eighth_of"]).then_inc(rows_in, 16)
            pool.wait_ge(rows_ready, 1)
            n = 0
            for kind in (0, 1):
                for quarter in range(4):
                    pool.wait_ge(wsl_free, 4 * kind + quarter + 1)
                    pool.dma_start(wsl, a[("w_cmp_k", "w_cmp_v")[kind]][quarter * 16:quarter * 16 + 16, :]
                                   .unsqueeze(0).broadcast_to([P, 16, DH])).then_inc(wsl_in, 16)
                    for g in (0, 1):
                        n += 1
                        pool.wait_ge(gath_free, n)
                        pool.indirect_dma_start(
                            out=gath.rearrange("p a b -> p (a b)"), out_offset=None,
                            in_=a[("cmp_k", "cmp_v")[kind]],
                            in_offset=bass.IndirectOffsetOnAxis(ap=gather_row[:, 4 * g + quarter:4 * g + quarter + 1], axis=0),
                        ).then_inc(gathered, 16)

        @block.vector
        def _(v):
            done = m.dve = Counter(v, m.dve_done)
            v.wait_ge(rows_in, 16 * (4 + NS_TOK))
            pages = page_of.unsqueeze(2).broadcast_to([P, 2, 4])
            done.link(v.tensor_scalar(gather_row.rearrange("p (g q) -> p g q", g=2), pages, 8, None, ALU.mult))
            done.link(v.tensor_scalar(m.seq_row, m.seq_row, 8, None, ALU.mult))
            done.link(v.tensor_tensor(m.seq_row, m.seq_row, eighth, ALU.add))
            v.tensor_tensor(gather_row, gather_row, half_of, ALU.add).then_inc(rows_ready, 1)
            v.sem_inc(wsl_free, 1)
            v.sem_inc(gath_free, 1)
            done.link(v.memset(m.pooled, 0.0))
            n = 0
            for kind in (0, 1):
                for quarter in range(4):
                    v.wait_ge(wsl_in, 16 * (4 * kind + quarter + 1))
                    for g in (0, 1):
                        n += 1
                        v.wait_ge(gathered, 16 * n)
                        x4 = gath.rearrange("p j (k d) -> p j k d", k=KV)
                        done.link(v.tensor_tensor(x4, x4, wsl.unsqueeze(2).broadcast_to([P, 16, KV, DH]), ALU.mult))
                        for w in (8, 4, 2, 1):
                            done.link(v.tensor_tensor(gath[:, 0:w], gath[:, 0:w], gath[:, w:2 * w], ALU.add))
                        done.link(v.tensor_tensor(m.pooled[:, kind, g], m.pooled[:, kind, g], gath[:, 0], ALU.add))
                        v.sem_inc(gath_free, 1)
                    v.sem_inc(wsl_free, 1)


def fetch_pages(pool, a, m, name, b):
    return pool.indirect_dma_start(out=m.pages[b % 4].rearrange("p a b -> p (a b)"), out_offset=None, in_=a[name],
                                   in_offset=bass.IndirectOffsetOnAxis(ap=m.seq_row[:, b:b + 1], axis=0))


def phase_b(nc, a, o, m, sem):
    arena, ps, proj, xt, cst = m.arena, m.ps, m.proj, m.xt, m.cst
    _, CP = constants()[0]
    c_ = lambda n, r=P: cst[0:r, CP[n][0]:CP[n][0] + CP[n][1]]
    kt = m.small(2, KV, NP_TOK)
    kc4 = m.small(KV, 4)
    vc4 = m.small(KV * DH)
    gates = m.small(2, NGL)
    mean, var = m.small(2, H), m.small(2, H)
    mx, nm, sm, rc = (m.small(2, 3) for _ in range(4))
    k_out = m.small(H, DH)
    w = Taker(arena, WORK, KVC)
    scratch = [w(2, H, 64) for _ in range(4)]
    squares = view(arena, WORK, 2, H, DH)
    gn = view(arena, WORK + 2048, H * DH)
    stage = w(4, P)
    qkt = w(4, P)
    kdec = w(2, P)
    att = w(2, P)
    s1 = w(P)
    cw = view(arena, WORK + 5760, 2, 2, KV * DH)
    n_w = Taker(arena, WORK, WORK + 5760)
    q_stage, q_t = n_w(2, 2, P), n_w(2, P)
    prob = n_w(2, 516)
    prob_t, prob_c = n_w(2, 512), n_w(256)
    zero = n_w(KV * DH)

    names = (
        "b_roped b_gates b_silu r_staged r_kdec r_t r_qkt r_att r_s r_ev r_o r_done r_done_h gn_in "
        "gn_var gn_std gn_out f_t f_free kt_t kt_in cw_ready c4_ready c4_in n_staged n_t n_qt n_s "
        "n_max n_exp n_prob n_pt n_ev n_o n_out b_stored zero_ready k_ahead win_moved ")
    S = {n: sem(n) for n in names.split()}
    V = nc.vector

    with nc.Block() as block:
        @block.sync
        def _(sp):
            for n, (out, col) in enumerate((("p_ck", CK), ("p_cv", CV), ("p_sk", SK), ("p_sv", SV))):
                if n == 0:
                    sp.wait_ge(S["b_roped"], 3)
                sp.dma_start(o[out].rearrange("a b (t p) k d -> p (a b t) (k d)", p=P), proj[:, :, col:col + KV * DH]
                             ).then_inc(S["b_stored"], 16)
            for out, col in (("p_wk", WK), ("p_wv", WV)):
                rows = o[out].rearrange("a b (t p) k d -> p (a b t) (k d)", p=P)
                sp.dma_start(rows[:, 2:4, :], proj[:, :, col:col + KV * DH]).then_inc(S["b_stored"], 16)
                sp.wait_ge(S["zero_ready"], 1)
                for t in (0, 1):
                    sp.dma_start(rows[:, t, :], zero).then_inc(S["b_stored"], 16)
            sp.wait_ge(S["r_done"], 1)
            sp.dma_start(o["p_ret"].rearrange("a b h d e -> d (a b h) e"), k_out).then_inc(S["b_stored"], 16)
            sp.wait_ge(S["b_stored"], 16 * 11)

        @block.gpsimd
        def _(pool):
            for b in range(4):
                fetch_pages(pool, a, m, "sel_k", b).then_inc(S["k_ahead"], 16)
                pool.dma_start(m.windows[:, b, :], a["win_k"][b].rearrange("(p j) c -> p (j c)", j=4)).then_inc(S["k_ahead"], 16)
            for out, src in (("s_wk", "win_k"), ("s_wv", "win_v")):
                rows = o[out].rearrange("a s t k d -> (a s) t (k d)")
                pool.dma_start(rows[:, 0:WIN - 1, :], a[src][:, 1:WIN, :]).then_inc(S["win_moved"], 16)
            pool.wait_ge(S["k_ahead"], 128)
            pool.wait_ge(S["win_moved"], 32)

        @block.scalar
        def _(act):
            A = nc.scalar
            A.activation(gates, proj[:, :, GL:IN_W], ACT.Sigmoid).then_inc(S["b_gates"], 1)
            act.wait_ge(S["b_roped"], 2)
            with act.Fori(0, H) as h:
                act.wait_ge(S["r_t"], h + 1)
                A.copy(stage[:, 0:2, :], proj[:, :, bass.ds(h * DH + RQ, DH)])
                A.copy(stage[:, 2:4, :], proj[:, :, bass.ds(h * DH + RK, DH)]).then_inc(S["r_staged"], 1)
            A.activation(proj[:, :, RG:RG + 1024], proj[:, :, RG:RG + 1024], ACT.Silu).then_inc(S["b_silu"], 1)
            act.dma_start(gn, a["gn_g"].broadcast_to([P, H * DH])).then_inc(S["gn_in"], 16)
            act.wait_ge(S["gn_var"], 1)
            A.activation(var, var, ACT.Sqrt, bias=c_("eps"), scale=1.0 / DH).then_inc(S["gn_std"], 1)
            for br in (0, 1):
                act.wait_ge(S["kt_t"], 1)
                A.copy(kt[:, br], ps[:, 5 + br, :].rearrange("p (k t) -> p k t", k=KV)).then_inc(S["kt_in"], 1)
            act.wait_ge(S["c4_ready"], 1)
            A.copy(kc4, ps[:, 7, 0:8].rearrange("p (k b) -> p k b", k=KV)).then_inc(S["c4_in"], 1)
            A.copy(vc4[0:4, :], ps[0:4, 7, 256:512]).then_inc(S["c4_in"], 1)
            for n in range(4):
                act.wait_ge(S["f_t"], n + 1)
                A.copy(xt[:, 2 * n:2 * n + 2, 0:256], ps[:, n, :].rearrange("p (f t) -> p f t", f=2)
                       ).then_inc(S["f_free"], 1)
            with act.Fori(0, G) as g:
                for kv in range(KV):
                    head = g * DH + (NQ + kv * G * DH)
                    A.copy(q_stage[:, kv], proj[:, :, bass.ds(head, DH)]).then_inc(S["n_staged"], 1)
                    act.wait_ge(S["n_max"], g * 2 + kv + 1)
                    for t in (0, 1):
                        for br in range(3):
                            cols = slice(512, 516) if br == 2 else slice(256 * br, 256 * br + 256)
                            last = A.activation(prob[:, t, cols], prob[:, t, cols], ACT.Exp,
                                                bias=nm[:, t, br:br + 1], accum_out=sm[:, t, br:br + 1])
                    last.then_inc(S["n_exp"], 1)
                    act.wait_ge(S["n_pt"], g * 2 + kv + 1)
                    A.copy(prob_t[:, 0], ps[:, 4, :]).then_inc(S["n_ev"], 1)
                    act.wait_ge(S["n_o"], g * 2 + kv + 1)
                    A.copy(xt[:, bass.ds(g + (H + kv * G), 1), 0:256], ps[:, 7, 0:256].unsqueeze(1)
                           ).then_inc(S["n_out"], 1)

        @block.vector
        def _(v):
            done = m.dve
            done.eng = v
            by_head = lambda col, n: proj[:, :, col:col + n * DH].rearrange("p t (h d) -> p t h d", d=DH)
            table = lambda n, half: c_(n).rearrange("p (t h) -> p t h", t=2).unsqueeze(2)
            cr, sr, cn, sn = (table(n, 0) for n in ("cos_r", "sin_r", "cos_n", "sin_n"))
            rope(v, done, by_head(RQ, H), cr, sr, scratch)
            v.sem_inc(S["b_roped"], 1)
            rope(v, done, by_head(RK, H), cr, sr, scratch)
            done.link(v.tensor_scalar(proj[:, :, RK:RV], proj[:, :, RK:RV], RET_SCALE, None, ALU.mult))
            v.sem_inc(S["b_roped"], 1)
            for n, col in ((H, NQ), (KV, CK), (KV, SK), (KV, WK)):
                rope(v, done, by_head(col, n), cn, sn, [s[:, :, 0:n, 0:16] for s in scratch])
            v.sem_inc(S["b_roped"], 1)
            for k, col in enumerate((CK, CV)):
                last = v.tensor_tensor(
                    cw[:, k].rearrange("p t (k d) -> p (t k) d", d=DH),
                    proj[:, :, col:col + KV * DH].rearrange("p t (k d) -> p t k d", d=DH),
                    m.wrep[:, k].unsqueeze(1).unsqueeze(1).broadcast_to([P, 2, KV, DH]), ALU.mult)
            last.then_inc(S["cw_ready"], 1)
            with v.Fori(0, H) as h:
                done.enter(h, 3)
                for t in (0, 1):
                    last = v.tensor_scalar(kdec[:, t], proj[:, t, bass.ds(h * DH + RK, DH)],
                                           cst[:, bass.ds(h + CP["k_dec"][0], 1)], None, ALU.mult)
                last.then_inc(S["r_kdec"], 1)
                v.wait_ge(S["r_t"], h + 2)
                v.tensor_copy(qkt.rearrange("p a b -> p (a b)"), ps[:, 0, :]).then_inc(S["r_qkt"], 1)
                v.wait_ge(S["r_att"], h + 1)
                v.tensor_tensor(att, ps[:, 1, 0:256].rearrange("p (c i) -> p c i", c=2),
                                cst[:, bass.ds(h * P + CP["dmask"][0], P)].unsqueeze(1).broadcast_to([P, 2, P]), ALU.mult)
                v.wait_ge(S["r_s"], h + 1)
                done.link(v.tensor_copy(s1, ps[:, 2, 0:P]))
                done.link(v.scalar_tensor_tensor(k_out[:, bass.ds(h, 1), :], s1.unsqueeze(1), cst[:, bass.ds(h + CP["c_dec"][0], 1)],
                                                 ps[:, 3, 0:P].unsqueeze(1), ALU.mult, ALU.add))
                v.sem_inc(S["r_ev"], 1)
                v.wait_ge(S["r_o"], h + 1)
                o_col = bass.ds(h * DH + RQ, DH)
                v.tensor_copy(proj[:, 0, o_col], ps[:, 4, 0:P])
                done.link(v.tensor_copy(proj[:, 1, o_col], ps[:, 4, P:2 * P]))
                v.scalar_tensor_tensor(proj[:, 1, o_col], ps[:, 4, 2 * P:3 * P], cst[:, bass.ds(h + CP["q_dec"][0], 1)],
                                       proj[:, 1, o_col], ALU.mult, ALU.add).then_inc(S["r_done_h"], 1)
                v.wait_ge(S["r_done_h"], h + 1)
            done.leave(H)
            v.sem_inc(S["r_done"], 1)
            heads = by_head(RQ, H)
            done.link(v.tensor_reduce(mean, heads, AX_X, ALU.add))
            done.link(v.tensor_scalar(mean, mean, 1.0 / DH, None, ALU.mult))
            done.link(v.tensor_tensor(heads, heads, mean.unsqueeze(3).broadcast_to([P, 2, H, DH]), ALU.subtract))
            done.link(v.tensor_tensor(squares, heads, heads, ALU.mult))
            v.tensor_reduce(var, squares, AX_X, ALU.add).then_inc(S["gn_var"], 1)
            v.wait_ge(S["gn_std"], 1)
            done.link(v.reciprocal(var, var))
            done.link(v.tensor_tensor(heads, heads, var.unsqueeze(3).broadcast_to([P, 2, H, DH]), ALU.mult))
            v.wait_ge(S["gn_in"], 16)
            flat = proj[:, :, RQ:RQ + H * DH]
            done.link(v.tensor_tensor(flat, flat, gn.unsqueeze(1).broadcast_to([P, 2, H * DH]), ALU.mult))
            v.wait_ge(S["b_silu"], 1)
            v.tensor_tensor(flat, flat, proj[:, :, RG:RG + 1024], ALU.mult).then_inc(S["gn_out"], 1)
            v.wait_ge(S["gn_out"], 1)
            v.memset(zero, 0.0).then_inc(S["zero_ready"], 1)
            v.wait_ge(S["b_gates"], 1)
            causal = c_("causal").rearrange("p (t k) -> p t k", t=2)
            cmp_add = c_("cmp_add").rearrange("p (t k) -> p t k", t=2)
            cmp_ok = c_("cmp_ok").rearrange("p (t k) -> p t k", t=2)
            main = prob[:, :, 0:512].rearrange("p t (b k) -> p t b k", b=2)
            cmpp = prob[:, :, 512:516]
            with v.Fori(0, G) as g:
                done.enter(g, 2 * 8)
                for kv in range(KV):
                    n = g * 2 + kv + 1
                    v.wait_ge(S["n_t"], n)
                    v.tensor_copy(q_t.rearrange("p a b -> p (a b)"), ps[:, 0, 0:256]).then_inc(S["n_qt"], 1)
                    v.wait_ge(S["n_s"], n)
                    for t in (0, 1):
                        v.scalar_tensor_tensor(main[:, t], ps[:, 1 + t, :].rearrange("p (b k) -> p b k", b=2), SCALE,
                                               causal[:, t].unsqueeze(1).broadcast_to([P, 2, 256]), ALU.mult, ALU.add)
                    done.link(v.scalar_tensor_tensor(cmpp, ps[:, 3, 0:8].rearrange("p (t k) -> p t k", t=2), SCALE,
                                                     cmp_add, ALU.mult, ALU.add))
                    v.tensor_reduce(mx[:, :, 0:2], main, AX_X, ALU.max)
                    done.link(v.tensor_reduce(mx[:, :, 2:3], cmpp.unsqueeze(2), AX_X, ALU.max))
                    v.tensor_scalar(nm, mx, -1.0, None, ALU.mult).then_inc(S["n_max"], 1)
                    v.wait_ge(S["n_exp"], n)
                    v.tensor_tensor(cmpp, cmpp, cmp_ok, ALU.mult)
                    done.link(v.reciprocal(rc, sm))
                    gate0 = g * 3 + kv * 12
                    done.link(v.tensor_tensor(rc[:, :, 0:2], rc[:, :, 0:2], gates[:, :, bass.ds(gate0 + 1, 2)], ALU.mult))
                    done.link(v.tensor_tensor(rc[:, :, 2:3], rc[:, :, 2:3], gates[:, :, bass.ds(gate0, 1)], ALU.mult))
                    done.link(v.tensor_tensor(cmpp, cmpp, rc[:, :, 2:3].broadcast_to([P, 2, 4]), ALU.mult))
                    for t in (0, 1):
                        done.link(v.tensor_tensor(main[:, t], main[:, t], rc[:, t, 0:2].unsqueeze(2).broadcast_to([P, 2, 256]), ALU.mult))
                    v.sem_inc(S["n_prob"], 1)
                    v.wait_ge(S["n_pt"], n)
                    v.tensor_copy(prob_c[0:4, :], ps[0:4, 6, 0:256])
                    v.tensor_copy(prob_t[:, 1], ps[:, 5, :]).then_inc(S["n_ev"], 1)
                    v.wait_ge(S["n_o"], n)
            done.leave(G)

        @block.tensor
        def _(pe):
            ident = c_("ident")
            pe.sem_inc(S["r_t"], 1)
            with pe.Fori(0, H) as h:
                pe.wait_ge(S["r_staged"], h + 1)
                for n in range(4):
                    last = pe.transpose(ps[:, 0, n * P:(n + 1) * P], stage[:, n, :], ident)
                last.then_inc(S["r_t"], 1)
                pe.wait_ge(S["r_qkt"], h + 1)
                for c in (0, 1):
                    last = pe.matmul(ps[:, 1, c * P:(c + 1) * P], qkt[:, 2 + c, :], qkt[:, c, :], start=True, stop=True)
                last.then_inc(S["r_att"], 1)
                pe.wait_ge(S["r_kdec"], h + 1)
                vals = [proj[:, c, bass.ds(h * DH + RV, DH)] for c in (0, 1)]
                for c in (0, 1):
                    last = pe.matmul(ps[:, 2 + c, 0:P], kdec[:, c, :], vals[c], start=True, stop=True)
                last.then_inc(S["r_s"], 1)
                pe.wait_ge(S["r_ev"], h + 1)
                for c in (0, 1):
                    pe.matmul(ps[:, 4, c * P:(c + 1) * P], att[:, c, :], vals[c], start=True, stop=True)
                pe.matmul(ps[:, 4, 2 * P:3 * P], qkt[:, 1, :], s1, start=True, stop=True).then_inc(S["r_o"], 1)
                pe.wait_ge(S["r_done_h"], h + 1)
            pe.wait_ge(S["b_roped"], 3)
            for br, col in enumerate((SK, WK)):
                for kv in range(KV):
                    for t in (0, 1):
                        last = pe.transpose(ps[:, 5 + br, kv * 256 + t * P:kv * 256 + (t + 1) * P],
                                            proj[:, t, col + kv * DH:col + (kv + 1) * DH], ident)
            last.then_inc(S["kt_t"], 1)
            pe.wait_ge(S["cw_ready"], 1)
            for t in (0, 1):
                for kv in range(KV):
                    pe.matmul(ps[:, 7, kv * 4 + 2 * t:kv * 4 + 2 * t + 2], cw[:, 0, t, kv * DH:(kv + 1) * DH],
                              c_("blk2"), start=True, stop=True)
            for t in (0, 1):
                last = pe.matmul(ps[0:4, 7, 256:512], c_("blk4")[:, 4 * t:4 * t + 4], cw[:, 1, t, :],
                                 start=(t == 0), stop=(t == 1))
            last.then_inc(S["c4_ready"], 1)
            pe.wait_ge(S["gn_out"], 1)
            for n in range(4):
                for f in (0, 1):
                    for t in (0, 1):
                        last = pe.transpose(ps[:, n, f * 256 + t * P:f * 256 + (t + 1) * P],
                                            proj[:, t, (2 * n + f) * DH:(2 * n + f + 1) * DH], ident)
                last.then_inc(S["f_t"], 1)
            pe.wait_ge(S["f_free"], 4)
            pe.wait_ge(S["kt_in"], 2)
            pe.wait_ge(S["c4_in"], 2)
            with pe.Fori(0, G) as g:
                for kv in range(KV):
                    n = g * 2 + kv + 1
                    pe.wait_ge(S["n_staged"], n)
                    for t in (0, 1):
                        last = pe.transpose(ps[:, 0, t * P:(t + 1) * P], q_stage[:, kv, t, :], ident)
                    last.then_inc(S["n_t"], 1)
                    pe.wait_ge(S["n_qt"], n)
                    for t in (0, 1):
                        pe.matmul(ps[:, 1 + t, :], q_t[:, t, :], kt[:, :, kv, :], start=True, stop=True)
                        last = pe.matmul(ps[:, 3, 4 * t:4 * t + 4], q_t[:, t, :], kc4[:, kv, :], start=True, stop=True)
                    last.then_inc(S["n_s"], 1)
                    pe.wait_ge(S["n_prob"], n)
                    for t in (0, 1):
                        for c in range(4):
                            pe.transpose(ps[:, 4 + t, c * P:(c + 1) * P], prob[:, t, c * P:(c + 1) * P], ident)
                        last = pe.transpose(ps[0:4, 6, t * P:(t + 1) * P], prob[:, t, 512:516], ident)
                    last.then_inc(S["n_pt"], 1)
                    pe.wait_ge(S["n_ev"], n * 2)
                    for c in range(4):
                        v0 = (SV, WV)[c // 2] + kv * DH
                        pe.matmul(ps[:, 7, 0:256], proj[:, c % 2, v0:v0 + DH], prob_t[:, :, c * P:(c + 1) * P],
                                  start=(c == 0), stop=False)
                    pe.matmul(ps[:, 7, 0:256], vc4[0:4, kv * DH:(kv + 1) * DH], prob_c[0:4, :],
                              start=False, stop=True).then_inc(S["n_o"], 1)
                    pe.wait_ge(S["n_out"], n)


def phase_s(nc, a, o, m, sem):
    arena, ps, xt, ident = m.arena, m.ps, m.xt, m.cst[:, 0:P]
    (_, CP), (cs, CS), _ = constants()
    w = Taker(arena, PROJ, XT0)
    ct = w(cs.shape[1])
    s_ = lambda n, r=64: ct[0:r, CS[n][0]:CS[n][0] + CS[n][1]]
    rq, rk, rg, nq, gnr, kv5, kvw = (w(DH) for _ in range(7))
    v_new = w(KV * DH)
    gate = w(3)
    rs = [w(64) for _ in range(4)]
    tr = w(5, 64)
    q_kv = w(KV, 64)
    q_own = w(NS_TOK, KV, 64)
    kct = w(KV, KV * P)
    prob_c = w(256)
    sel = w(NBLK + 1)
    imp8, score = w(256), w(NBLK + 1)
    selrow = w(NBLK + 1)
    mx, nm, sm, rc = (w(3) for _ in range(4))
    osum, otmp, ot_r = w(DH), w(DH), w(64)
    mean, var = w(1), w(1)
    prob = view(arena, WORK, PAST + 16 + WIN)
    probs, probw = prob[0:64, 0:PAST + 8], prob[0:64, PAST + 8:PAST + 16 + WIN]
    new_cols = prob[0:64, PAST:PAST + 16]
    pt = view(arena, WORK + 2600, 23, 64)
    pown = view(arena, WORK + 4100, 2, 20, 64)
    assert 4100 + 2560 <= 7168
    cmpt = view(arena, WORK, NBLK + 1, NBLK + 1)
    eqt = view(arena, WORK + 1100, NBLK + 1, NBLK + 1)
    s_old, s_new = [w(H, DH) for _ in (0, 1)], [w(H, DH) for _ in (0, 1)]
    v_rep = [w(H, DH) for _ in (0, 1)]
    keys_t = view(arena, WORK + 4100, 4, CHUNK)
    pages, windows = m.pages, m.windows
    names = (
        "s_in s_rot s_tr s_tr_in s_roped_out s_st_in0 s_st_in1 s_st_new s_st_o s_st_out0 s_st_out1 "
        "s_otr s_or s_or_in s_var s_std s_silu s_gated s_ft s_ftin s_q s_kct s_kct_in s_c s_cexp "
        "s_cmax s_cprob s_imp s_rank s_selb s_turned s_keys s_scored s_sel s_max s_exp s_prob s_pt s_pt_in "
        "s_pown s_half s_ot s_fin s_gate s_cpout s_vst ")
    S = {n: sem(n) for n in names.split()}
    k_full = [sem(f"s_kfull{n}") for n in range(4)]
    v_full = [sem(f"s_vfull{n}") for n in range(4)]
    kw_full = [sem(f"s_kwfull{n}") for n in range(4)]
    vw_full = [sem(f"s_vwfull{n}") for n in range(4)]

    with nc.Block() as block:
        @block.sync
        def _(sp):
            def state_in(b):
                sp.dma_start(s_old[b % 2], a["state"][b].rearrange("h d e -> d h e")).then_inc(S[f"s_st_in{b % 2}"], 16)
                sp.dma_start(v_rep[b % 2].rearrange("p h d -> p (h d)"), m.ps_a[2, b:b + 1, :].broadcast_to([P, H * DH])
                             ).then_inc(S[f"s_st_in{b % 2}"], 16)

            state_in(0)
            state_in(1)
            for b in range(NS_TOK):
                if b >= 4:
                    sp.wait_ge(S["s_turned"], 10 * (b - 3))
                    sp.dma_start(windows[:, b % 4, :], a["win_k"][b].rearrange("(p j) c -> p (j c)", j=4)).then_inc(kw_full[b % 4], 16)
                sp.wait_ge(S["s_st_new"], b + 1)
                sp.dma_start(o["s_ret"][0, b].rearrange("h d e -> d h e"), s_new[b % 2]).then_inc(S[f"s_st_out{b % 2}"], 16)
                if b + 2 < NS_TOK:
                    state_in(b + 2)
            for b in range(NS_TOK):
                if b < 4:
                    sp.wait_ge(S["s_turned"], 10 * (b + 5))
                else:
                    sp.wait_ge(S["s_vst"], b - 3)
                sp.dma_start(windows[:, b % 4, :], a["win_v"][b].rearrange("(p j) c -> p (j c)", j=4)).then_inc(vw_full[b % 4], 16)
            sp.wait_ge(S["s_st_out0"], 64)
            sp.wait_ge(S["s_st_out1"], 64)

        @block.gpsimd
        def _(pool):
            pool.wait_ge(S["s_rot"], 1)
            pool.dma_start(m.kv5_d.rearrange("s x d -> (s x) d"), kv5[0:64, :]).then_inc(S["s_roped_out"], 16)
            pool.dma_start(m.kvw_d.rearrange("s x d -> (s x) d"), kvw[0:32, :]).then_inc(S["s_roped_out"], 16)
            pool.wait_ge(S["s_roped_out"], 32)
            for n, out in enumerate(("s_ck", "s_cv", "s_sk", "s_sv")):
                pool.dma_start(o[out].rearrange("a s t k d -> (a s t) k d"), m.kv5_d[:, 2 * n:2 * n + 2, :]).then_inc(S["s_cpout"], 16)
            for n, out in enumerate(("s_wk", "s_wv")):
                pool.dma_start(o[out][0, :, WIN - 1, :, :], m.kvw_d[:, 2 * n:2 * n + 2, :]).then_inc(S["s_cpout"], 16)
            for b in range(4, NS_TOK):
                pool.wait_ge(S["s_turned"], 10 * (b - 3))
                fetch_pages(pool, a, m, "sel_k", b).then_inc(k_full[b % 4], 16)
            for b in range(NS_TOK):
                if b < 4:
                    pool.wait_ge(S["s_turned"], 10 * (b + 5))
                else:
                    pool.wait_ge(S["s_vst"], b - 3)
                fetch_pages(pool, a, m, "sel_v", b).then_inc(v_full[b % 4], 16)
            pool.wait_ge(S["s_cpout"], 96)

        @block.scalar
        def _(act):
            A = nc.scalar
            rows = lambda n: m.ps_a[n].rearrange("s (h d) -> (s h) d", d=DH)
            act.dma_start(ct, a["const_s"]).then_inc(S["s_in"], 16)
            for dst, n in ((rq, 0), (rk, 1), (rg, 3), (nq, 4), (kv5, 5)):
                act.dma_start(dst[0:64, :], rows(n)).then_inc(S["s_in"], 16)
            act.dma_start(kvw[0:32, :], m.ps_w.rearrange("s (x d) -> (s x) d", d=DH)).then_inc(S["s_in"], 16)
            act.dma_start(v_new[0:8, :], m.ps_a[5, :, 768:1024]).then_inc(S["s_in"], 16)
            act.dma_start(v_new[8:16, :], m.ps_w[:, 256:512]).then_inc(S["s_in"], 16)
            act.dma_start(gate[0:64, :], m.ps_g.rearrange("s (h t) -> (s h) t", t=3)).then_inc(S["s_in"], 16)
            act.dma_start(gnr[0:64, :], a["gn_rows"]).then_inc(S["s_in"], 16)
            act.wait_ge(S["s_in"], 176)
            A.activation(gate[0:64, :], gate[0:64, :], ACT.Sigmoid).then_inc(S["s_gate"], 1)
            A.activation(rg[0:64, :], rg[0:64, :], ACT.Silu).then_inc(S["s_silu"], 1)
            act.wait_ge(S["s_tr"], 1)
            A.copy(tr.rearrange("p a b -> p (a b)")[:, 0:288], ps[:, 0, 0:288]).then_inc(S["s_tr_in"], 1)
            act.wait_ge(S["s_kct"], 1)
            A.copy(kct.rearrange("p a b -> p (a b)"), ps[:, 4, :]).then_inc(S["s_kct_in"], 1)
            act.wait_ge(S["s_cmax"], 1)
            A.activation(prob_c[0:64, :], prob_c[0:64, :], ACT.Exp, bias=nm[0:64, 0:1], accum_out=sm[0:64, 0:1]
                         ).then_inc(S["s_cexp"], 1)
            for n in range(10 * NS_TOK):
                act.wait_ge(S["s_turned"], n + 1)
                if n >= 4:
                    act.wait_ge(S["s_scored"], n - 3)
                A.copy(keys_t[:, 2 * (n % 2) + n // 2 % 2], ps[:, 6 + n % 2, :]).then_inc(S["s_keys"], 1)
            act.wait_ge(S["s_st_o"], 8)
            A.copy(ot_r, ps[:, 5, 272:336]).then_inc(S["s_otr"], 1)
            act.wait_ge(S["s_or"], 1)
            A.copy(osum[0:64, :], ps[0:64, 6, 0:DH]).then_inc(S["s_or_in"], 1)
            act.wait_ge(S["s_max"], 1)
            A.activation(probs, probs, ACT.Exp, bias=nm[0:64, 1:2], accum_out=sm[0:64, 1:2])
            A.activation(probw, probw, ACT.Exp, bias=nm[0:64, 2:3], accum_out=sm[0:64, 2:3]).then_inc(S["s_exp"], 1)
            act.wait_ge(S["s_var"], 1)
            A.activation(var[0:64, :], var[0:64, :], ACT.Sqrt, bias=m.cst[0:64, CP["eps"][0]:CP["eps"][0] + 1], scale=1.0 / DH
                         ).then_inc(S["s_std"], 1)
            act.wait_ge(S["s_pt"], 1)
            A.copy(pt[:, 0:8, :].rearrange("p a b -> p (a b)"), ps[:, 0, :]).then_inc(S["s_pt_in"], 1)
            A.copy(pt[:, 8:16, :].rearrange("p a b -> p (a b)"), ps[:, 1, :]).then_inc(S["s_pt_in"], 1)
            A.copy(pt[:, 16:22, :].rearrange("p a b -> p (a b)"), ps[:, 2, 0:384]).then_inc(S["s_pt_in"], 1)
            A.copy(pt[0:16, 22, :], ps[0:16, 2, 384:448]).then_inc(S["s_pt_in"], 1)
            act.wait_ge(S["s_ft"], 1)
            A.copy(xt[:, 0:H, NP_TOK:T], ps[:, 6, 256:320].rearrange("p (s h) -> p h s", h=H)).then_inc(S["s_ftin"], 1)
            act.wait_ge(S["s_ot"], 1)
            A.copy(xt[:, H:2 * H, NP_TOK:T], ps[:, 3, 0:64].rearrange("p (s h) -> p h s", h=H)).then_inc(S["s_fin"], 1)
            act.wait_ge(S["s_fin"], 1)
            act.wait_ge(S["s_ftin"], 1)

        @block.vector
        def _(v):
            done = m.dve
            r64 = lambda t: t[0:64, :]
            v.wait_ge(S["s_in"], 176)
            rope(v, done, rq[0:64, :], s_("cos_r"), s_("sin_r"), [r[0:64, :] for r in rs])
            rope(v, done, rk[0:64, :], s_("cos_r"), s_("sin_r"), [r[0:64, :] for r in rs])
            done.link(v.tensor_scalar(rk[0:64, :], rk[0:64, :], RET_SCALE, None, ALU.mult))
            rope(v, done, nq[0:64, :], s_("cos_n"), s_("sin_n"), [r[0:64, 0:16] for r in rs])
            rope(v, done, kv5[0:64, :], s_("cos_k"), s_("sin_k"), [r[0:64, 0:16] for r in rs])
            rope(v, done, kvw[0:32, :], s_("cos_w", 32), s_("sin_w", 32), [r[0:32, 0:16] for r in rs])
            v.memset(q_kv, 0.0)
            done.link(v.memset(q_own, 0.0))
            v.sem_inc(S["s_rot"], 1)
            v.wait_ge(S["s_tr_in"], 1)
            qs = tr[:, 0, :].rearrange("p (s k g) -> p s k g", s=NS_TOK, k=KV)
            for kv in range(KV):
                v.tensor_copy(q_kv[:, kv].rearrange("p (s k g) -> p s k g", s=NS_TOK, k=KV)[:, :, kv, :], qs[:, :, kv, :])
            for b in range(NS_TOK):
                for kv in range(KV):
                    last = v.tensor_copy(q_own[:, b, kv, 8 * b + 4 * kv:8 * b + 4 * kv + 4], qs[:, b, kv, :])
            last.then_inc(S["s_q"], 1)
            v.wait_ge(S["s_c"], 1)
            own_add, own = s_("own_add").unsqueeze(2), s_("own").unsqueeze(2)
            pc = prob_c[0:64, :].rearrange("p (s b) -> p s b", s=NS_TOK)
            done.link(v.scalar_tensor_tensor(pc, ps[0:64, 5, 0:256].rearrange("p (s b) -> p s b", s=NS_TOK), SCALE,
                                             own_add.broadcast_to([64, 8, NBLK]), ALU.mult, ALU.add))
            done.link(v.tensor_reduce(mx[0:64, 0:1], prob_c[0:64, :], AX_X, ALU.max))
            v.tensor_scalar(nm[0:64, 0:1], mx[0:64, 0:1], -1.0, None, ALU.mult).then_inc(S["s_cmax"], 1)
            v.wait_ge(S["s_cexp"], 1)
            done.link(v.reciprocal(rc[0:64, 0:1], sm[0:64, 0:1]))
            done.link(v.tensor_tensor(pc, pc, own.broadcast_to([64, 8, NBLK]), ALU.mult))
            v.tensor_scalar(prob_c[0:64, :], prob_c[0:64, :], rc[0:64, 0:1], None, ALU.mult).then_inc(S["s_cprob"], 1)
            v.wait_ge(S["s_imp"], 1)
            done.link(v.tensor_copy(imp8[0:16, :], ps[0:16, 6, 0:256]))
            done.link(v.tensor_reduce(score[0:16, 0:NBLK], imp8[0:16, :].rearrange("p (s b) -> p b s", s=NS_TOK), AX_X, ALU.add))
            v.memset(score[0:16, 0:1], -NEG)
            done.link(v.memset(score[0:16, NBLK - 1:NBLK + 1], -NEG))
            other = score[0:16, :].unsqueeze(1).broadcast_to([16, NBLK + 1, NBLK + 1])
            mine = score[0:16, :].unsqueeze(2).broadcast_to([16, NBLK + 1, NBLK + 1])
            v.tensor_tensor(cmpt[0:16], other, mine, ALU.is_gt)
            done.link(v.tensor_tensor(eqt[0:16], other, mine, ALU.is_equal))
            done.link(v.tensor_tensor(eqt[0:16], eqt[0:16], s_("earlier", 16).rearrange("p (a b) -> p a b", a=NBLK + 1), ALU.mult))
            done.link(v.tensor_tensor(cmpt[0:16], cmpt[0:16], eqt[0:16], ALU.add))
            done.link(v.tensor_reduce(selrow[0:16, :], cmpt[0:16], AX_X, ALU.add))
            v.tensor_scalar(selrow[0:16, :], selrow[0:16, :], float(TOPK), None, ALU.is_lt).then_inc(S["s_rank"], 1)
            v.wait_ge(S["s_selb"], 1)
            done.link(v.tensor_scalar(sel[0:64, :], ps[0:64, 6, 256:256 + NBLK + 1], 1.0, -NEG, ALU.subtract, ALU.mult))
            v.sem_inc(S["s_sel"], 1)
            gam = s_("gamma", P).unsqueeze(2).broadcast_to([P, H, DH])
            for b in range(NS_TOK):
                v.wait_ge(S[f"s_st_in{b % 2}"], 32 * (b // 2 + 1))
                if b >= 2:
                    v.wait_ge(S["s_st_o"], b - 1)
                    v.wait_ge(S[f"s_st_out{b % 2}"], 16 * (b // 2))
                v.tensor_tensor(s_old[b % 2], s_old[b % 2], gam, ALU.mult)
                done.link(v.tensor_tensor(v_rep[b % 2], v_rep[b % 2], tr[:, 2, 8 * b:8 * b + 8].unsqueeze(2).broadcast_to([P, H, DH]), ALU.mult))
                v.tensor_tensor(s_new[b % 2], s_old[b % 2], v_rep[b % 2], ALU.add).then_inc(S["s_st_new"], 1)
            v.wait_ge(S["s_scored"], 10 * NS_TOK)
            v.wait_ge(S["s_otr"], 1)
            for j in range(NPAGE):
                by_block = lambda t: t.rearrange("p (b r) -> p b r", r=4)
                v.scalar_tensor_tensor(by_block(probs[:, j * P:(j + 1) * P]), by_block(ps[0:64, j // 4, j % 4 * P:(j % 4 + 1) * P]), SCALE,
                                       sel[0:64, 0:NBLK].unsqueeze(2).broadcast_to([64, NBLK, 4]), ALU.mult, ALU.add)
            v.scalar_tensor_tensor(probs[:, PAST:PAST + 8], ps[0:64, 5, 256:264], SCALE, s_("own_add"), ALU.mult, ALU.add)
            v.scalar_tensor_tensor(probw[:, 0:8], ps[0:64, 5, 264:272], SCALE, s_("own_add"), ALU.mult, ALU.add)
            done.link(v.tensor_scalar(probw[:, 8:8 + WIN], ps[0:64, 4, :], SCALE, None, ALU.mult))
            done.link(v.memset(probw[:, 8:9], NEG))
            v.tensor_reduce(mx[0:64, 1:2], probs, AX_X, ALU.max)
            done.link(v.tensor_reduce(mx[0:64, 2:3], probw, AX_X, ALU.max))
            v.tensor_scalar(nm[0:64, 1:3], mx[0:64, 1:3], -1.0, None, ALU.mult).then_inc(S["s_max"], 1)
            v.wait_ge(S["s_or_in"], 1)
            done.link(v.tensor_reduce(r64(mean), r64(osum), AX_X, ALU.add))
            done.link(v.tensor_scalar(r64(mean), r64(mean), 1.0 / DH, None, ALU.mult))
            done.link(v.tensor_scalar(r64(osum), r64(osum), r64(mean), None, ALU.subtract))
            done.link(v.tensor_tensor(r64(otmp), r64(osum), r64(osum), ALU.mult))
            v.tensor_reduce(r64(var), r64(otmp), AX_X, ALU.add).then_inc(S["s_var"], 1)
            v.wait_ge(S["s_exp"], 1)
            v.wait_ge(S["s_gate"], 1)
            done.link(v.reciprocal(rc[0:64, 1:3], sm[0:64, 1:3]))
            done.link(v.tensor_tensor(rc[0:64, 1:3], rc[0:64, 1:3], gate[0:64, 1:3], ALU.mult))
            v.tensor_scalar(probs, probs, rc[0:64, 1:2], None, ALU.mult)
            v.tensor_scalar(probw, probw, rc[0:64, 2:3], None, ALU.mult)
            done.link(v.tensor_scalar(prob_c[0:64, :], prob_c[0:64, :], gate[0:64, 0:1], None, ALU.mult))
            v.sem_inc(S["s_prob"], 1)
            v.wait_ge(S["s_std"], 1)
            done.link(v.reciprocal(r64(var), r64(var)))
            done.link(v.scalar_tensor_tensor(r64(osum), r64(osum), r64(var), r64(gnr), ALU.mult, ALU.mult))
            v.wait_ge(S["s_silu"], 1)
            v.tensor_tensor(r64(osum), r64(osum), r64(rg), ALU.mult).then_inc(S["s_gated"], 1)
            v.wait_ge(S["s_pt_in"], 4)
            for b in range(NS_TOK):
                if b >= 2:
                    v.wait_ge(S["s_vst"], b - 1)
                v.tensor_tensor(pown[:, b % 2], pt[:, 0:20, :], s_("own_row", P)[:, 64 * b:64 * b + 64].unsqueeze(1).broadcast_to([P, 20, 64]),
                                ALU.mult).then_inc(S["s_pown"], 1)
            v.wait_ge(S["s_vst"], 8)
            half = s_("half")
            done.link(v.tensor_scalar(r64(osum), ps[0:64, 7, 0:DH], half[:, 0:1], None, ALU.mult))
            v.scalar_tensor_tensor(r64(osum), ps[0:64, 7, DH:2 * DH], half[:, 1:2], r64(osum), ALU.mult, ALU.add
                                   ).then_inc(S["s_half"], 1)

        @block.tensor
        def _(pe):
            id64 = ident[0:64, 0:64]
            pe.wait_ge(S["s_rot"], 1)
            for n, t in enumerate((nq, rq, rk, kv5)):
                pe.transpose(ps[:, 0, 64 * n:64 * n + 64], t[0:64, :], id64)
            pe.transpose(ps[:, 0, 256:288], kvw[0:32, :], ident[0:32, 0:32]).then_inc(S["s_tr"], 1)
            pe.wait_ge(S["s_tr_in"], 1)
            for g in (0, 1):
                for kv in range(KV):
                    last = pe.transpose(ps[:, 4, kv * 256 + g * P:kv * 256 + (g + 1) * P], m.pooled[:, 0, g, kv * DH:(kv + 1) * DH], ident)
            last.then_inc(S["s_kct"], 1)
            pe.wait_ge(S["s_kct_in"], 1)
            pe.wait_ge(S["s_q"], 1)
            for dst, keys in ((slice(0, 256), [kct[:, kv, :] for kv in range(KV)]),
                              (slice(256, 264), [tr[:, 3, :].rearrange("p (s x) -> p x s", x=8)[:, 4 + kv, :] for kv in range(KV)]),
                              (slice(264, 272), [tr[:, 4, 0:32].rearrange("p (s x) -> p x s", x=4)[:, kv, :] for kv in range(KV)])):
                for kv in range(KV):
                    last = pe.matmul(ps[0:64, 5, dst], q_kv[:, kv, :], keys[kv], start=(kv == 0), stop=(kv == 1))
            last.then_inc(S["s_c"], 1)
            pe.wait_ge(S["s_cprob"], 1)
            pe.matmul(ps[0:16, 6, 0:256], s_("to_kv")[0:64, :], prob_c[0:64, :], start=True, stop=True).then_inc(S["s_imp"], 1)
            pe.wait_ge(S["s_rank"], 1)
            pe.matmul(ps[0:64, 6, 256:256 + NBLK + 1], s_("from_kv", 16), selrow[0:16, :], start=True, stop=True).then_inc(S["s_selb"], 1)
            pe.wait_ge(S["s_sel"], 1)

            def turn(n):
                b, c, kv = n // 10, n // 2 % 5, n % 2
                if b >= 4 and c == 0 and kv == 0:
                    pe.wait_ge(k_full[b % 4], 16)
                if b >= 4 and c == 4 and kv == 0:
                    pe.wait_ge(kw_full[b % 4], 16)
                if n >= 2:
                    pe.wait_ge(S["s_keys"], n - 1)
                for j in range(4):
                    rows = pages[b % 4][:, 4 * c + j, :] if c < 4 else windows[:, b % 4, j * KV * DH:(j + 1) * KV * DH]
                    last = pe.transpose(ps[:, 6 + kv, j * P:(j + 1) * P], rows[:, kv * DH:(kv + 1) * DH], ident)
                last.then_inc(S["s_turned"], 1)

            turn(0)
            for n in range(10 * NS_TOK):
                b, c, kv = n // 10, n // 2 % 5, n % 2
                if n + 1 < 10 * NS_TOK:
                    turn(n + 1)
                pe.wait_ge(S["s_keys"], n + 1)
                pe.matmul(ps[0:64, c, :], q_own[:, b, kv, :], keys_t[:, 2 * kv + n // 2 % 2], start=(b == 0 and kv == 0),
                                 stop=(b == 7 and kv == 1)).then_inc(S["s_scored"], 1)
                if n % 10 == 9:
                    pe.wait_ge(S["s_st_new"], b + 1)
                    for h in range(H):
                        q = 8 * b + h
                        last = pe.matmul(ps[:, 5, 272 + q:273 + q], s_new[b % 2][:, h, :], tr[:, 1, q:q + 1], start=True, stop=True)
                    last.then_inc(S["s_st_o"], 1)
            pe.wait_ge(S["s_otr"], 1)
            pe.wait_ge(S["s_keys"], 10 * NS_TOK)
            pe.transpose(ps[0:64, 6, 0:DH], ot_r, ident).then_inc(S["s_or"], 1)
            pe.wait_ge(S["s_prob"], 1)
            for n in range(23):
                if n < 16:
                    src = probs[:, n * P:(n + 1) * P]
                elif n < 20:
                    src = probw[:, 8 + (n - 16) * P:8 + (n - 15) * P]
                elif n < 22:
                    src = prob_c[0:64, (n - 20) * P:(n - 19) * P]
                else:
                    src = new_cols
                rows = 16 if n == 22 else P
                last = pe.transpose(ps[0:rows, n // 8, (n % 8) * 64:(n % 8) * 64 + 64], src, id64)
            last.then_inc(S["s_pt"], 1)
            pe.wait_ge(S["s_gated"], 1)
            pe.transpose(ps[:, 6, 256:320], osum[0:64, :], id64).then_inc(S["s_ft"], 1)
            pe.wait_ge(S["s_pt_in"], 4)
            for g in (0, 1):
                pe.matmul(ps[0:64, 7, 0:256], pt[:, 20 + g, :], m.pooled[:, 1, g, :], start=(g == 0), stop=False)
            pe.matmul(ps[0:64, 7, 0:256], pt[0:16, 22, :], v_new[0:16, :], start=False, stop=False)
            for b in range(NS_TOK):
                u, i = b % 4, b // 4
                pe.wait_ge(S["s_pown"], b + 1)
                pe.wait_ge(v_full[u], 16 * (i + 1))
                pe.wait_ge(vw_full[u], 16 * (i + 1))
                for n in range(20):
                    vals = pages[u][:, n, :] if n < 16 else windows[:, u, (n - 16) * 256:(n - 15) * 256]
                    last = pe.matmul(ps[0:64, 7, 0:256], pown[:, b % 2, n, :], vals, start=False, stop=(b == 7 and n == 19))
                last.then_inc(S["s_vst"], 1)
            pe.wait_ge(S["s_half"], 1)
            pe.transpose(ps[:, 3, 0:64], osum[0:64, :], id64).then_inc(S["s_ot"], 1)


def phase_c(nc, a, o, m, sem):
    arena, ps, xt = m.arena, m.ps, m.xt
    _, _, (cr, CR) = constants()
    ring = view(arena, RING, 8, 4, CHUNK)
    hw = Taker(arena, PROJ, XT0)
    h = hw(3, D)
    ln = hw(2, D)
    w_r = hw(KT, NG + NE)
    wk = Taker(arena, WORK, KVC)
    x = wk(3, D)
    ht = xt
    r_ = lambda n, r=P: m.cr[0:r, CR[n][0]:CR[n][0] + CR[n][1]]
    sm = Taker(arena, 16384, RING + 20480)
    stats, agg, rstd = sm(3, 4, 6), sm(3, 2), sm(3)
    bias, lg = sm(NG + NE), sm(3, NG + NE)
    gm, gs, tm, goh, pg = sm(3), sm(3), sm(3), sm(3, NG), sm(3, NG)
    el, sel, c8 = sm(3, NG, EPG), sm(3, EPG), sm(3, EPG)
    em, es, m1, m2 = sm(3), sm(3), sm(3), sm(3)
    oh = [sm(3, EPG), sm(3, EPG)]
    e12 = [sm(3, NG, EPG), sm(3, NG, EPG)]
    both, sums = sm(3, NE), sm(2, NE)
    nb_t, nb_w, base, endb, posb = sm(1), sm(P), sm(NE), sm(NE), sm(3, NE)
    cnt_t, nb_rep, slots, ge = sm(1), sm(NE), sm(2, 3), sm(MAXB, NE)
    btab_f = sm(MAXB + 1)
    zero_i = sm(MAXB).bitcast(I32)
    tok_id = sm(3).bitcast(I32)
    names = (
        "c_in c_x c_free c_acc c_mv c_std c_h c_hst c_ht c_hti c_lg c_gx c_exp c_e c_cum c_nb c_bs "
        "c_pos c_zero c_zst c_scat c_slot c_tmp c_sub ")
    S = {n: sem(n) for n in names.split()}
    w_full = [sem(f"c_wfull{j}") for j in range(8)]
    w_o = a["w_o"].rearrange("(k p) n -> p k n", p=P)

    with nc.Block() as block:
        @block.sync
        def _(sp):
            for i in range(2):
                for j in range(8):
                    if i:
                        sp.wait_ge(S["c_free"], j + 1)
                    cols = i * 1024 + (j // 4) * 512
                    sp.dma_start(ring[:, j], w_o[:, (j % 4) * 4:(j % 4) * 4 + 4, cols:cols + CHUNK]).then_inc(w_full[j], 16)
            sp.wait_ge(S["c_h"], 3)
            for t, (t0, n) in enumerate(TOK):
                sp.dma_start(m.h_d[t0:t0 + n, :], h[0:n, t, :]).then_inc(S["c_hst"], 16)
            sp.wait_ge(S["c_hst"], 48)

        @block.gpsimd
        def _(pool):
            pool.dma_start(tok_id, a["tok_id"]).then_inc(S["c_tmp"], 16)
            pool.memset(zero_i, 0).then_inc(S["c_zero"], 1)
            pool.wait_ge(S["c_zero"], 1)
            pool.dma_start(m.slot_d.rearrange("(s b) o -> s (b o)", s=BS), zero_i[0:BS, :]).then_inc(S["c_zst"], 16)
            pool.wait_ge(S["c_zst"], 16)
            pool.wait_ge(S["c_tmp"], 16)
            pool.wait_ge(S["c_pos"], 1)
            for k in (0, 1):
                for t, (_, n) in enumerate(TOK):
                    pool.indirect_dma_start(out=m.slot_d, out_offset=bass.IndirectOffsetOnAxis(ap=m.pos[0:n, k, t:t + 1], axis=0),
                                            in_=tok_id[0:n, t:t + 1], in_offset=None).then_inc(S["c_scat"], 16)
            pool.wait_ge(S["c_scat"], 96)
            pool.dma_start(m.slot_tok[0:BS, :], m.slot_d.rearrange("(b s) o -> s (b o)", s=BS),
                           allow_slow_non_contiguous=True).then_inc(S["c_slot"], 16)
            pool.wait_ge(S["c_slot"], 16)

        @block.scalar
        def _(act):
            A = nc.scalar
            xr = a["x"]
            for t, (t0, n) in enumerate(TOK):
                act.dma_start(x[0:n, t, :], xr[t0:t0 + n, :]).then_inc(S["c_x"], 16)
            act.dma_start(m.cr, a["const_r"]).then_inc(S["c_in"], 16)
            act.dma_start(w_r, a["w_r"].rearrange("p (k n) -> p k n", k=KT)).then_inc(S["c_in"], 16)
            act.dma_start(bias, a["b_r"].broadcast_to([P, NG + NE])).then_inc(S["c_in"], 16)
            act.dma_start(ln[:, 0, :], a["ln1_g"].broadcast_to([P, D])).then_inc(S["c_in"], 16)
            act.dma_start(ln[:, 1, :], a["ln1_b"].broadcast_to([P, D])).then_inc(S["c_in"], 16)
            act.wait_ge(S["c_in"], 80)
            for t, (_, n) in enumerate(TOK):
                act.wait_ge(S["c_mv"], t + 1)
                A.activation(rstd[0:n, t:t + 1], agg[0:n, t, 1:2], ACT.Sqrt, bias=r_("eps", n)).then_inc(S["c_std"], 1)
            for k in range(KT):
                act.wait_ge(S["c_ht"], k + 1)
                A.copy(ht[:, k, :], ps[:, k % 2, 0:T]).then_inc(S["c_hti"], 1)
            act.wait_ge(S["c_gx"], 1)
            A.activation(pg, pg, ACT.Exp).then_inc(S["c_exp"], 1)
            act.wait_ge(S["c_sub"], 1)
            A.activation(sel, sel, ACT.Exp).then_inc(S["c_exp"], 1)

        @block.vector
        def _(v):
            done = m.dve
            v.wait_ge(S["c_x"], 48)
            for n4 in range(4):
                v.wait_ge(S["c_free"], 4 * (n4 + 1))
                for t, (_, n) in enumerate(TOK):
                    cols = slice(n4 * CHUNK, (n4 + 1) * CHUNK)
                    last = v.scalar_tensor_tensor(h[0:n, t, cols], x[0:n, t, cols], ALPHA, ps[0:n, 3 * (n4 % 2) + t, :], ALU.mult, ALU.add)
                last.then_inc(S["c_acc"], 1)
                v.wait_ge(S["c_acc"], n4 + 1)
                for t, (_, n) in enumerate(TOK):
                    last = v.bn_stats(stats[0:n, t, n4, :], h[0:n, t, cols])
            done.link(last)
            v.wait_ge(S["c_in"], 80)
            for t, (_, n) in enumerate(TOK):
                v.bn_aggr(agg[0:n, t, :], stats[0:n, t].rearrange("p a b -> p (a b)")).then_inc(S["c_mv"], 1)
            for t, (_, n) in enumerate(TOK):
                v.wait_ge(S["c_std"], t + 1)
                done.link(v.reciprocal(rstd[0:n, t:t + 1], rstd[0:n, t:t + 1]))
                done.link(v.tensor_scalar(h[0:n, t], h[0:n, t], agg[0:n, t, 0:1], rstd[0:n, t:t + 1], ALU.subtract, ALU.mult))
                done.link(v.tensor_tensor(h[0:n, t], h[0:n, t], ln[0:n, 0], ALU.mult))
                v.tensor_tensor(h[0:n, t], h[0:n, t], ln[0:n, 1], ALU.add).then_inc(S["c_h"], 1)
            done.link(v.memset(lg, 0.0))
            v.wait_ge(S["c_lg"], 1)
            for t, (_, n) in enumerate(TOK):
                last = v.tensor_tensor(lg[0:n, t], ps[0:n, 2 + t, 0:NG + NE], bias[0:n, :], ALU.add)
            done.link(last)
            gl = lg[:, :, 0:NG]
            b3 = lambda t, n: t.unsqueeze(2).broadcast_to([P, 3, n])

            def first_max(out, vals, top, desc, n):
                done.link(v.tensor_reduce(top, vals, AX_X, ALU.max))
                done.link(v.tensor_tensor(out, vals, b3(top, n), ALU.is_equal))
                done.link(v.tensor_tensor(out, out, desc.unsqueeze(1).broadcast_to([P, 3, n]), ALU.mult))
                done.link(v.tensor_reduce(tm, out, AX_X, ALU.max))
                done.link(v.tensor_tensor(out, out, b3(tm, n), ALU.is_equal))

            first_max(goh, gl, gm, r_("desc4"), NG)
            v.tensor_tensor(pg, gl, b3(gm, NG), ALU.subtract).then_inc(S["c_gx"], 1)
            e4 = lg[:, :, NG:].rearrange("p t (g e) -> p t g e", g=NG)
            for t in range(3):
                last = v.tensor_tensor(el[:, t], e4[:, t], goh[:, t].unsqueeze(2).broadcast_to([P, NG, EPG]), ALU.mult)
            done.link(last)
            for t in range(3):
                last = v.tensor_reduce(sel[:, t], el[:, t].rearrange("p g e -> p e g"), AX_X, ALU.add)
            done.link(last)
            done.link(v.tensor_reduce(em, sel, AX_X, ALU.max))
            v.tensor_tensor(sel, sel, b3(em, EPG), ALU.subtract).then_inc(S["c_sub"], 1)
            v.wait_ge(S["c_exp"], 2)
            v.tensor_reduce(gs, pg, AX_X, ALU.add)
            done.link(v.tensor_reduce(es, sel, AX_X, ALU.add))
            v.reciprocal(gs, gs)
            done.link(v.reciprocal(es, es))
            done.link(v.tensor_tensor(sel, sel, b3(es, EPG), ALU.mult))
            first_max(oh[0], sel, m1, r_("desc8"), EPG)
            done.link(v.scalar_tensor_tensor(sel, oh[0], -2.0, sel, ALU.mult, ALU.add))
            first_max(oh[1], sel, m2, r_("desc8"), EPG)
            done.link(v.tensor_tensor(es, m1, m2, ALU.add))
            done.link(v.reciprocal(es, es))
            done.link(v.tensor_tensor(es, es, gs, ALU.mult))
            v.tensor_tensor(m.gate_w[:, 0], m1, es, ALU.mult)
            v.tensor_tensor(m.gate_w[:, 1], m2, es, ALU.mult)
            done.link(v.tensor_tensor(goh, goh, b3(r_("valid"), NG), ALU.mult))
            for k in (0, 1):
                for t in range(3):
                    last = v.tensor_tensor(e12[k][:, t], goh[:, t].unsqueeze(2).broadcast_to([P, NG, EPG]),
                                           oh[k][:, t].unsqueeze(1).broadcast_to([P, NG, EPG]), ALU.mult)
            done.link(last)
            flat = lambda t: t.rearrange("p t g e -> p t (g e)")
            done.link(v.tensor_tensor(both, flat(e12[0]), flat(e12[1]), ALU.add))
            done.link(v.tensor_tensor(sums[:, 0], both[:, 0], both[:, 1], ALU.add))
            v.tensor_tensor(sums[:, 1], sums[:, 0], both[:, 2], ALU.add).then_inc(S["c_e"], 1)
            v.wait_ge(S["c_cum"], 1)
            for cnt, dst in ((ps[0:NE, 6, 0:1], nb_t[0:NE, :]), (ps[:, 6, 32:64], nb_rep)):
                done.link(v.tensor_scalar(dst, cnt, 0.0, None, ALU.is_gt))
                for n in range(1, (T + BS - 1) // BS):
                    done.link(v.scalar_tensor_tensor(dst, cnt, float(n * BS), dst, ALU.is_gt, ALU.add))
            v.tensor_copy(nb_w[0:NE, :], nb_t[0:NE, :].broadcast_to([NE, P])).then_inc(S["c_nb"], 1)
            v.wait_ge(S["c_bs"], 1)
            done.link(v.tensor_copy(base, ps[:, 6, 64:96]))
            done.link(v.tensor_tensor(endb, base, nb_rep, ALU.add))
            for t in range(3):
                last = v.scalar_tensor_tensor(posb[:, t], base, float(BS), ps[:, 5, 32 * t:32 * t + 32], ALU.mult, ALU.add)
            done.link(last)
            for k in (0, 1):
                done.link(v.tensor_tensor(both, flat(e12[k]), posb, ALU.mult))
                done.link(v.tensor_reduce(slots[:, k], both, AX_X, ALU.add))
            v.tensor_copy(m.pos, slots).then_inc(S["c_pos"], 1)
            done.link(v.tensor_tensor(ge[0:1], endb[0:1].unsqueeze(1).broadcast_to([1, MAXB, NE]),
                                      r_("blocks", 1).unsqueeze(2).broadcast_to([1, MAXB, NE]), ALU.is_le))
            done.link(v.tensor_reduce(btab_f[0:1, 0:MAXB], ge[0:1], AX_X, ALU.add))
            done.link(v.tensor_scalar(btab_f[0:1, 0:MAXB], btab_f[0:1, 0:MAXB], float(NE - 1), None, ALU.min))
            done.link(v.tensor_copy(btab_f[0:1, MAXB:MAXB + 1], endb[0:1, NE - 1:NE]))
            done.link(v.tensor_copy(m.btab[0:1, :], btab_f[0:1, :]))

        @block.tensor
        def _(pe):
            for n4 in range(4):
                if n4 >= 2:
                    pe.wait_ge(S["c_acc"], n4 - 1)
                for q in range(4):
                    j = 4 * (n4 % 2) + q
                    pe.wait_ge(w_full[j], 16 * (n4 // 2 + 1))
                    for kk in range(4):
                        k = 4 * q + kk
                        for t, (t0, n) in enumerate(TOK):
                            last = pe.matmul(ps[0:n, 3 * (n4 % 2) + t, :], xt[:, k, t0:t0 + n], ring[:, j, kk, :],
                                             start=(k == 0), stop=(k == KT - 1))
                    last.then_inc(S["c_free"], 1)
            pe.wait_ge(S["c_in"], 80)
            ident = r_("ident")
            pe.wait_ge(S["c_h"], 3)
            for k in range(KT):
                if k >= 2:
                    pe.wait_ge(S["c_hti"], k - 1)
                for t, (t0, n) in enumerate(TOK):
                    last = pe.transpose(ps[:, k % 2, t0:t0 + n], h[0:n, t, k * P:(k + 1) * P], ident[0:n, 0:n])
                last.then_inc(S["c_ht"], 1)
            pe.wait_ge(S["c_hti"], KT)
            for t, (t0, n) in enumerate(TOK):
                for k in range(KT):
                    last = pe.matmul(ps[0:n, 2 + t, 0:NG + NE], ht[:, k, t0:t0 + n], w_r[:, k, :], start=(k == 0), stop=(k == KT - 1))
            last.then_inc(S["c_lg"], 1)
            pe.wait_ge(S["c_e"], 1)
            for t in range(3):
                pe.matmul(ps[:, 5, 32 * t:32 * t + 32], r_("before"), both[:, t], start=True, stop=(t == 0))
                if t:
                    pe.matmul(ps[:, 5, 32 * t:32 * t + 32], r_("ones"), both[:, 0] if t == 1 else sums[:, 0], start=False, stop=True)
            pe.matmul(ps[0:NE, 6, 0:1], sums[:, 1], r_("ones")[:, 0:1], start=True, stop=True)
            pe.matmul(ps[:, 6, 32:64], r_("ones"), sums[:, 1], start=True, stop=True).then_inc(S["c_cum"], 1)
            pe.wait_ge(S["c_nb"], 1)
            pe.matmul(ps[:, 6, 64:96], nb_w[0:NE, :], r_("lt32", NE), start=True, stop=True).then_inc(S["c_bs"], 1)


def phase_d(nc, a, o, m, sem):
    ps = m.ps
    ident = m.cr[:, 0:P]
    stack = ExitStack()

    def own(name, *dims, dt=F32):
        return stack.enter_context(nc.sbuf_tensor(name, [P, *dims], dt))

    ring = 6
    raw = own("d_raw", ring, 4 * CHUNK)
    wh, wl = (own(n, ring, 4 * CHUNK, dt=F32R) for n in ("d_wh", "d_wl"))
    xs = own("d_xs", KT, P, dt=F32R)
    hs = own("d_hs", DE // P, P, dt=F32R)
    xg = own("d_xg", D)
    gate, up, hb = own("d_gate", DE), own("d_up", DE), own("d_hb", DE)
    y, y_low = own("d_y", D), own("d_ylow", D)
    blank = own("d_blank", 512)
    names = ("d_used d_high d_split d_xg d_xt d_xhigh d_xlow d_gu d_silu d_lows d_sum d_hb d_ht d_hhigh d_hlow "
             "d_ylow d_y d_yst d_blank_st d_blank_set d_seen d_xgfree")
    S = {n: sem(n) for n in names.split()}
    full = [sem(f"d_full{j}") for j in range(ring)]
    wg = a["w_gate"].rearrange("e (k p) f -> e p k f", p=P)
    wu = a["w_up"].rearrange("e (k p) f -> e p k f", p=P)
    wd = a["w_down"].rearrange("e (k p) f -> e p k f", p=P)

    with nc.Block() as block:
        def filled(eng):
            return eng.value_load(m.btab[0:1, MAXB:MAXB + 1], min_val=1, max_val=MAXB)

        @block.sync
        def _(sp):
            n_blocks = filled(sp)
            with sp.Fori(0, MAXB) as b:
                with sp.If(b < n_blocks):
                    e = sp.value_load(m.btab[0:1, bass.ds(b, 1)], min_val=0, max_val=NE - 1)
                    for j in range(12):
                        sp.wait_ge(S["d_split"], b * 12 + (j + 1))
                        to = raw[:, j % ring]
                        if j < 8:
                            src = (wg, wu)[j % 2][e, :, 4 * (j // 2):4 * (j // 2) + 4, :]
                            sp.dma_start(to.rearrange("p (k f) -> p k f", k=4), src).then_inc(full[j % ring], 16)
                        else:
                            sp.dma_start(to, wd[e, :, j - 8, :]).then_inc(full[j % ring], 16)

        @block.gpsimd
        def _(pool):
            n_blocks = filled(pool)

            def fetch():
                pool.indirect_dma_start(out=xg[0:BS, :], out_offset=None, in_=m.h_d,
                                        in_offset=bass.IndirectOffsetOnAxis(ap=m.cur_tok[0:BS, :], axis=0)).then_inc(S["d_xg"], 16)

            pool.tensor_copy(m.cur_tok[0:BS, :], m.slot_tok[0:BS, 0:1]).then_inc(S["d_xgfree"], 1)
            pool.wait_ge(S["d_xgfree"], 1)
            fetch()
            with pool.Fori(0, MAXB - 1) as b:
                with pool.If(b < n_blocks):
                    pool.wait_ge(S["d_xt"], b + 1)
                    pool.tensor_copy(m.cur_tok[0:BS, :], m.slot_tok[0:BS, bass.ds(b + 1, 1)]).then_inc(S["d_xgfree"], 1)
                    pool.wait_ge(S["d_xgfree"], b + 2)
                    pool.sem_inc(S["d_seen"], 1)
                    fetch()

        def xt_parts(part):
            return xs[:, :, part * BS:(part + 1) * BS]

        xt_ps = ps[:, 2:4, :].rearrange("p a (k s) -> p (a k) s", s=BS)
        ht_ps = ps[:, 0, 0:256].rearrange("p (k s) -> p k s", s=BS)

        @block.scalar
        def _(act):
            A = nc.scalar
            n_blocks = filled(act)
            act.wait_ge(S["d_xt"], 1)
            A.copy(xt_parts(0), xt_ps).then_inc(S["d_xhigh"], 1)

            def read_low(b):
                act.wait_ge(S["d_used"], b * 12 + ring)
                A.copy(y_low[0:BS, :].rearrange("p (a b) -> p a b", a=4), ps[BS:P, 4:8, :]).then_inc(S["d_ylow"], 1)

            def store(b):
                act.wait_ge(S["d_y"], b + 1)
                act.dma_start(m.y_d[bass.ds((b - 1) * BS, BS), :], y[0:BS, :]).then_inc(S["d_yst"], 16)

            def expert(b, first=False):
                for j in range(12):
                    act.wait_ge(full[j % ring], b * 32 + (j // ring + 1) * 16)
                    act.wait_ge(S["d_used"], b * 12 + (j + 1))
                    A.copy(wh[:, j % ring], raw[:, j % ring]).then_inc(S["d_high"], 1)
                    if j == ring - 1 and not first:
                        read_low(b)
                    if j == ring + 2 and not first:
                        store(b)
                act.wait_ge(S["d_used"], b * 12 + (8 + ring))
                A.copy(gate[0:BS, :], ps[BS:P, 0, :]).then_inc(S["d_lows"], 1)
                A.copy(up[0:BS, :], ps[BS:P, 1, :]).then_inc(S["d_lows"], 1)
                act.wait_ge(S["d_sum"], b + 1)
                A.activation(gate[0:BS, :], gate[0:BS, :], ACT.Silu).then_inc(S["d_silu"], 1)
                act.wait_ge(S["d_ht"], b + 1)
                A.copy(hs[:, :, 0:BS], ht_ps).then_inc(S["d_hhigh"], 1)
                act.wait_ge(S["d_xt"], b + 2)
                A.copy(xt_parts(0), xt_ps).then_inc(S["d_xhigh"], 1)

            expert(0, first=True)
            act.wait_ge(S["d_blank_set"], 1)
            with act.Fori(1, MAXB) as b:
                with act.If(b < n_blocks):
                    expert(b)
                    act.sem_inc(S["d_blank_st"], 16)
                with act.Else():
                    act.dma_start(m.y_d[bass.ds(b * BS, BS), :].rearrange("p (a b) -> p a b", a=4),
                                  blank[0:BS].unsqueeze(1).broadcast_to([BS, 4, 512])).then_inc(S["d_blank_st"], 16)
            read_low(n_blocks)
            store(n_blocks)
            act.wait_ge(S["d_yst"], n_blocks * 16 + 16)
            act.sem_inc(S["d_seen"], 1)
            act.wait_ge(S["d_blank_st"], 16 * (MAXB - 1))

        @block.vector
        def _(v):
            n_blocks = filled(v)
            v.memset(blank[:, :], 0.0).then_inc(S["d_blank_set"], 1)
            v.sem_inc(S["d_split"], ring)
            v.sem_inc(S["d_yst"], 16)
            v.wait_ge(S["d_xhigh"], 1)
            v.tensor_tensor(xt_parts(1), xt_ps, xt_parts(0).bitcast(F32), ALU.subtract).then_inc(S["d_xlow"], 1)

            def add_low(b):
                v.wait_ge(S["d_ylow"], b)
                v.wait_ge(S["d_yst"], b * 16)
                v.tensor_tensor(y[0:BS, :].rearrange("p (a b) -> p a b", a=4), ps[0:BS, 4:8, :],
                                y_low[0:BS, :].rearrange("p (a b) -> p a b", a=4), ALU.add).then_inc(S["d_y"], 1)

            def expert(b, first=False):
                for j in range(12):
                    v.wait_ge(S["d_high"], b * 12 + (j + 1))
                    v.tensor_tensor(wl[:, j % ring], raw[:, j % ring], wh[:, j % ring].bitcast(F32), ALU.subtract).then_inc(S["d_split"], 1)
                    if j == ring and not first:
                        add_low(b)
                v.wait_ge(S["d_lows"], b * 2 + 1)
                v.tensor_tensor(gate[0:BS, :], ps[0:BS, 0, :], gate[0:BS, :], ALU.add).then_inc(S["d_sum"], 1)
                v.wait_ge(S["d_lows"], b * 2 + 2)
                v.tensor_tensor(up[0:BS, :], ps[0:BS, 1, :], up[0:BS, :], ALU.add).then_inc(S["d_gu"], 1)
                v.wait_ge(S["d_gu"], b + 1)
                v.wait_ge(S["d_silu"], b + 1)
                v.tensor_tensor(hb[0:BS, :], gate[0:BS, :], up[0:BS, :], ALU.mult).then_inc(S["d_hb"], 1)
                v.wait_ge(S["d_hhigh"], b + 1)
                v.tensor_tensor(hs[:, :, BS:P], ht_ps, hs[:, :, 0:BS].bitcast(F32), ALU.subtract).then_inc(S["d_hlow"], 1)
                v.wait_ge(S["d_xhigh"], b + 2)
                v.tensor_tensor(xt_parts(1), xt_ps, xt_parts(0).bitcast(F32), ALU.subtract).then_inc(S["d_xlow"], 1)

            expert(0, first=True)
            with v.Fori(1, MAXB) as b:
                with v.If(b < n_blocks):
                    expert(b)
            add_low(n_blocks)

        @block.tensor
        def _(pe):
            n_blocks = filled(pe)
            pe.sem_inc(S["d_used"], ring)
            pe.sem_inc(S["d_y"], 1)
            id64 = ident[0:BS, 0:BS]

            def turn_tokens():
                for k in range(KT):
                    last = pe.transpose(ps[:, 2 + k // 8, (k % 8) * BS:(k % 8 + 1) * BS], xg[0:BS, k * P:(k + 1) * P], id64)
                last.then_inc(S["d_xt"], 1)

            pe.wait_ge(S["d_xg"], 16)
            turn_tokens()
            with pe.Fori(0, MAXB) as b:
                with pe.If(b < n_blocks):
                    def products(j, lhs, banks, first, final):
                        pe.wait_ge(S["d_split"], b * 12 + (ring + j + 1))
                        for part in (wh, wl):
                            for n in range(4):
                                cols = slice(n * CHUNK, (n + 1) * CHUNK)
                                last = pe.matmul(ps[:, banks[n], :], lhs[n], part[:, j % ring, cols],
                                                 start=(first and part is wh and (n == 0 or banks[n] != banks[0])),
                                                 stop=(final and part is wl and (n == 3 or banks[n] != banks[3])))
                        last.then_inc(S["d_used"], 1)

                    pe.wait_ge(S["d_xlow"], b + 1)
                    for j in range(8):
                        products(j, [xs[:, 4 * (j // 2) + n, :] for n in range(4)], [j % 2] * 4, j < 2, j >= 6)
                    pe.wait_ge(S["d_xg"], b * 16 + 32)
                    pe.sem_inc(S["d_seen"], 1)
                    turn_tokens()
                    pe.wait_ge(S["d_hb"], b + 1)
                    pe.sem_inc(S["d_seen"], 1)
                    for f in range(4):
                        last = pe.transpose(ps[:, 0, f * BS:(f + 1) * BS], hb[0:BS, f * P:(f + 1) * P], id64)
                    last.then_inc(S["d_ht"], 1)
                    pe.wait_ge(S["d_hlow"], b + 1)
                    pe.wait_ge(S["d_y"], b + 1)
                    for f in range(4):
                        products(8 + f, [hs[:, f, :]] * 4, [4, 5, 6, 7], f == 0, f == 3)
    stack.close()

    arena = m.make_arena()
    fin = Taker(arena, 0, 26000)
    h, y1, y2, ln = fin(3, D), fin(3, D), fin(3, D), fin(2, D)
    stats, agg, rstd = fin(3, 4, 6), fin(3, 2), fin(3)
    S.update({n: sem(n) for n in "f_in f_g0 f_g1 f_mv f_std f_o f_st".split()})

    with nc.Block() as block:
        @block.gpsimd
        def _(pool):
            for k, dst in enumerate((y1, y2)):
                for t, (_, n) in enumerate(TOK):
                    pool.indirect_dma_start(out=dst[0:n, t, :], out_offset=None, in_=m.y_d,
                                            in_offset=bass.IndirectOffsetOnAxis(ap=m.pos[0:n, k, t:t + 1], axis=0)).then_inc(S[f"f_g{k}"], 16)

        @block.vector
        def _(v):
            done = m.dve
            v.wait_ge(S["f_in"], 80)
            v.wait_ge(S["f_g0"], 48)
            v.wait_ge(S["f_g1"], 48)
            for t, (_, n) in enumerate(TOK):
                done.link(v.tensor_scalar(h[0:n, t], h[0:n, t], ALPHA, None, ALU.mult))
                for k, yk in enumerate((y1, y2)):
                    done.link(v.scalar_tensor_tensor(h[0:n, t], yk[0:n, t], m.gate_w[0:n, k, t:t + 1], h[0:n, t], ALU.mult, ALU.add))
                for c in range(4):
                    last = v.bn_stats(stats[0:n, t, c, :], h[0:n, t, c * CHUNK:(c + 1) * CHUNK])
                done.link(last)
                v.bn_aggr(agg[0:n, t, :], stats[0:n, t].rearrange("p a b -> p (a b)")).then_inc(S["f_mv"], 1)
            for t, (_, n) in enumerate(TOK):
                v.wait_ge(S["f_std"], t + 1)
                done.link(v.reciprocal(rstd[0:n, t:t + 1], rstd[0:n, t:t + 1]))
                done.link(v.tensor_scalar(h[0:n, t], h[0:n, t], agg[0:n, t, 0:1], rstd[0:n, t:t + 1], ALU.subtract, ALU.mult))
                done.link(v.tensor_tensor(h[0:n, t], h[0:n, t], ln[0:n, 0], ALU.mult))
                v.tensor_tensor(h[0:n, t], h[0:n, t], ln[0:n, 1], ALU.add).then_inc(S["f_o"], 1)

        @block.scalar
        def _(act):
            for n, src in enumerate((a["ln2_g"], a["ln2_b"])):
                act.dma_start(ln[:, n, :], src.broadcast_to([P, D])).then_inc(S["f_in"], 16)
            for t, (t0, n) in enumerate(TOK):
                act.dma_start(h[0:n, t, :], m.h_d[t0:t0 + n, :]).then_inc(S["f_in"], 16)
            for t, (_, n) in enumerate(TOK):
                act.wait_ge(S["f_mv"], t + 1)
                nc.scalar.activation(rstd[0:n, t:t + 1], agg[0:n, t, 1:2], ACT.Sqrt, bias=m.cr[0:n, P:P + 1]).then_inc(S["f_std"], 1)
            for t, (t0, n) in enumerate(TOK):
                act.wait_ge(S["f_o"], t + 1)
                dst = o["y_s"].rearrange("a b d -> (a b) d") if t == 2 else o["y_p"][0, t0:t0 + n, :]
                act.dma_start(dst, h[0:n, t, :]).then_inc(S["f_st"], 16)
            act.wait_ge(S["f_st"], 48)


def trunk(nc, a, o, upto=9):
    with ExitStack() as ctx:
        m = Memory()
        keep_t = ctx.enter_context(nc.sbuf_tensor("keep", [P, KEEP], F32))
        arena_stack = ExitStack()
        m.make_arena = lambda: ctx.enter_context(nc.sbuf_tensor("arena_f", [P, 26000], F32))
        m.arena = arena_stack.enter_context(nc.sbuf_tensor("arena", [P, END], F32))
        m.ps = ctx.enter_context(nc.psum_tensor("ps", [P, 8, 512], F32))

        def sem(name):
            return ctx.enter_context(nc.semaphore(name))

        def dram(name, shape, dt=F32):
            return nc.dram_tensor(name, shape, dt).ap()

        m.proj = view(m.arena, PROJ, 2, IN_W)
        m.xt = view(m.arena, XT0, KT, T)
        m.pooled = view(m.arena, KVC, 2, 2, KV * DH)
        m.cst = view(m.arena, CONST, 2064)
        m.small = Taker(m.arena, MISC, END)
        m.wrep = m.small(2, DH)
        m.ps_a = dram("sample_proj", (6, NS_TOK, 1024))
        m.ps_w = dram("sample_proj_w", (NS_TOK, 512))
        m.ps_g = dram("sample_proj_g", (NS_TOK, NGL))
        m.seq_row = m.small(NS_TOK).bitcast(I32)
        m.pages = [view(m.arena, RING + 4096 * n, NPAGE, KV * DH) for n in range(4)]
        m.windows = view(m.arena, RING + 16384, 4, 2 * WIN)
        m.kv5_d = dram("sample_kv", (NS_TOK, 8, DH))
        m.kvw_d = dram("sample_kvw", (NS_TOK, 4, DH))
        m.h_d, m.y_d = dram("h_rows", (T, D)), dram("y_rows", (MAXB * BS, D))
        m.slot_d = dram("slot_token", (MAXB * BS, 1), I32)
        keep = Taker(keep_t, 0, KEEP)
        m.cr = keep(constants()[2][0].shape[1])
        m.slot_tok, m.btab, m.cur_tok = keep(MAXB).bitcast(I32), keep(MAXB + 1).bitcast(I32), keep(1).bitcast(I32)
        m.pos = keep(6).bitcast(I32).rearrange("p (k t) -> p k t", k=2)
        m.gate_w = keep(2, 3)
        m.dve_done, m.act_done = sem("dve_done"), sem("act_done")
        for n, phase in enumerate((phase_a, phase_b, phase_s, phase_c, phase_d)):
            if n < upto:
                own = []

                def take(name):
                    own.append(nc.alloc_semaphore(name=name))
                    return own[-1]

                if n == 4:
                    arena_stack.close()
                phase(nc, a, o, m, take)
                if n < 4:
                    nc.clear_and_free_semaphores(own)
                    nc.all_engine_barrier()


_OUTS = [(1, 256, 2048), (8, 1, 2048)] + [(1, 1, 256, 2, 128)] * 4 + [(1, 1, 512, 2, 128)] * 2 + [(1, 1, 8, 128, 128)] + \
    [(1, 8, 1, 2, 128)] * 4 + [(1, 8, 512, 2, 128)] * 2 + [(1, 8, 8, 128, 128)]
_NAMES = ["y_p", "y_s", "p_ck", "p_cv", "p_sk", "p_sv", "p_wk", "p_wv", "p_ret",
          "s_ck", "s_cv", "s_sk", "s_sv", "s_wk", "s_wv", "s_ret"]


def host_layout(i):
    f = np.ascontiguousarray
    i = {k: np.asarray(v) for k, v in i.items()}
    (cp, _), (cs, _), (cr, _) = constants()
    x = np.concatenate([i["x_prompt"].reshape(NP_TOK, D), i["x_sample"].reshape(NS_TOK, D)], 0)
    tiles = lambda w: f(w.reshape(KT, P, -1).transpose(1, 0, 2).reshape(P, -1))
    p = np.arange(P)[:, None]
    q = np.arange(4)[None]
    half = np.tile(4 * (p % 2) + q, (1, 2)).astype(np.int32)
    return {
        "x": x, "tok_id": (np.arange(P)[:, None] + P * np.arange(3)[None]).astype(np.int32), "x_t": tiles(f(x.T)), "const_p": cp, "const_s": cs, "const_r": cr, "half_of": half,
        "eighth_of": np.tile(p % 8, (1, NS_TOK)).astype(np.int32),
        "page_table": i["page_table"],
        "w_in": i["w_in"][0], "w_gl": tiles(i["w_in"][0][:, GL:]),
        "w_cmp_k": i["w_cmp_k"][0], "w_cmp_v": i["w_cmp_v"][0],
        "cmp_k": i["cache_cmp_k"].reshape(-1, 16 * KV * DH), "cmp_v": i["cache_cmp_v"].reshape(-1, 16 * KV * DH),
        "sel_k": i["cache_sel_k"].reshape(-1, 16 * KV * DH), "sel_v": i["cache_sel_v"].reshape(-1, 16 * KV * DH),
        "win_k": i["cache_win_k"][0].reshape(NS_TOK, WIN, KV * DH), "win_v": i["cache_win_v"][0].reshape(NS_TOK, WIN, KV * DH),
        "state": i["state_ret"][0], "gn_g": i["ret_gn_g"], "gn_rows": f(np.broadcast_to(i["ret_gn_g"].reshape(1, H, DH), (8, H, DH)).reshape(64, DH)),
        "w_o": i["w_o"][0], "ln1_g": i["ln1_g"], "ln1_b": i["ln1_b"], "ln2_g": i["ln2_g"], "ln2_b": i["ln2_b"],
        "w_r": tiles(np.concatenate([i["w_group"][0], i["w_expert"][0]], 1)),
        "b_r": np.concatenate([i["b_group"], i["b_expert"]], 1),
        "w_gate": i["w_gate"][0], "w_up": i["w_up"][0], "w_down": i["w_down"][0],
    }


def kernel(**inputs):
    import concourse.bacc as bacc
    from concourse.bass_utils import run_bass_kernel_spmd as run

    nc = bacc.Bacc("TRN2", target_bir_lowering=False, num_devices=1)
    arrays = host_layout(inputs)
    a = {k: nc.dram_tensor(f"in_{k}", v.shape, mybir.dt.from_np(v.dtype), kind="ExternalInput").ap()
         for k, v in arrays.items()}
    o = {n: nc.dram_tensor(f"out_{n}", s, F32, kind="ExternalOutput").ap() for n, s in zip(_NAMES, _OUTS)}
    trunk(nc, a, o)
    r = run(nc, [{f"in_{k}": v for k, v in arrays.items()}], core_ids=[0])
    return tuple(r.results[0][f"out_{n}"] for n in _NAMES)
```
